# Optimizing a Trainium2 kernel written in Bass

```python
import math
import jax
import jax.numpy as jnp
from jax import lax
import numpy as np
import jax, jax.numpy as jnp

D_MODEL = 1024
BATCH = 1
SEQ = 512
DEPTH = 1

N_META = 16
EPS = 1e-6
DA_HEADS = 4
DA_HEAD_DIM = 64
DA_V_DIM = 2 * DA_HEAD_DIM
DA_WIDTH = DA_HEADS * DA_V_DIM
ROPE_THETA = 500000.0
ROPE_DIM = DA_HEAD_DIM // 4
Q_BLOCK = 128
GLA_HEADS = 4
GLA_DK = 64
GLA_DV = 128
GLA_WIDTH = GLA_HEADS * GLA_DV
GLA_GATE_RANK = 16
GLA_TAU = 16.0
GLA_CHUNK = 64
MIX_WIDTH = DA_WIDTH + GLA_WIDTH
IN_SIZES = (DA_HEADS * 2 * DA_HEAD_DIM, DA_HEADS * 2 * DA_HEAD_DIM, DA_WIDTH, GLA_HEADS * GLA_DK, GLA_HEADS * GLA_DK, GLA_WIDTH, GLA_WIDTH, GLA_GATE_RANK, GLA_GATE_RANK)
IN_WIDTH = sum(IN_SIZES)
PEER_HEADS = 8
PEER_NKEYS = 128
PEER_EXPERTS = PEER_NKEYS * PEER_NKEYS
PEER_KEY_DIM = 128
PEER_TOPK = 16
PEER_BLOCK = 256


def rmsnorm(x, w):
    xf = x.astype(jnp.float32)
    y = xf * lax.rsqrt(jnp.mean(xf * xf, axis=-1, keepdims=True) + EPS)
    return (y * w.astype(jnp.float32)).astype(x.dtype)

def partial_rope(x, pos):
    inv = jnp.power(ROPE_THETA, -jnp.arange(0, ROPE_DIM, 2, dtype=jnp.float32) / ROPE_DIM)
    ang = pos.astype(jnp.float32)[:, None] * inv[None, :]
    cos = jnp.cos(ang)[None, :, None, None, :]
    sin = jnp.sin(ang)[None, :, None, None, :]
    xr = x[..., :ROPE_DIM].astype(jnp.float32)
    x1, x2 = xr[..., :ROPE_DIM // 2], xr[..., ROPE_DIM // 2:]
    rot = jnp.concatenate([x1 * cos - x2 * sin, x2 * cos + x1 * sin], axis=-1)
    return jnp.concatenate([rot.astype(x.dtype), x[..., ROPE_DIM:]], axis=-1)

def diff_attention(q, k, v, lam, pos):
    B, T = q.shape[0], q.shape[1]
    q = partial_rope(q, pos) * (DA_HEAD_DIM ** -0.5)
    k = partial_rope(k, pos)
    nb = -(-T // Q_BLOCK)
    qp = jnp.pad(q, ((0, 0), (0, nb * Q_BLOCK - T), (0, 0), (0, 0), (0, 0)))
    qb = qp.reshape(B, nb, Q_BLOCK, DA_HEADS, 2, DA_HEAD_DIM).transpose(1, 0, 2, 3, 4, 5)

    def block(qi):
        s = jnp.einsum('bqhcd,bkhcd->bhcqk', qi, k).astype(jnp.float32)
        p = jax.nn.softmax(s, axis=-1)
        a = p[:, :, 0] - lam * p[:, :, 1]
        return jnp.einsum('bhqk,bkhv->bqhv', a.astype(v.dtype), v)

    o = lax.map(block, qb)
    return o.transpose(1, 0, 2, 3, 4).reshape(B, nb * Q_BLOCK, DA_HEADS, DA_V_DIM)[:, :T]

def gla_chunk_scan(q, k, v, g):
    B, L = q.shape[0], q.shape[1]
    n = L // GLA_CHUNK

    def to_chunks(a):
        return a.reshape(B, n, GLA_CHUNK, a.shape[2], a.shape[3]).transpose(1, 0, 3, 2, 4)

    mask = jnp.tril(jnp.ones((GLA_CHUNK, GLA_CHUNK), dtype=bool))[:, :, None]

    def step(state, inp):
        qc, kc, vc, gc = inp
        b = jnp.cumsum(gc, axis=2)
        rel = b[:, :, :, None, :] - b[:, :, None, :, :]
        decay = jnp.exp(jnp.where(mask, rel, -jnp.inf))
        attn = jnp.einsum('bhid,bhjd,bhijd->bhij', qc, kc, decay)
        o = jnp.einsum('bhij,bhjv->bhiv', attn, vc) + jnp.einsum('bhid,bhdv->bhiv', qc * jnp.exp(b), state)
        b_last = b[:, :, -1]
        state = state * jnp.exp(b_last)[..., None] + jnp.einsum('bhjd,bhjv->bhdv', kc * jnp.exp(b_last[:, :, None] - b), vc)
        return state, o

    state0 = jnp.zeros((B, q.shape[2], q.shape[3], v.shape[3]), jnp.float32)
    _, o = lax.scan(step, state0, (to_chunks(q), to_chunks(k), to_chunks(v), to_chunks(g)))
    return o.transpose(1, 0, 3, 2, 4).reshape(B, L, q.shape[2], v.shape[3])

def gla_bidirectional(q, k, v, g_f, g_b):
    pad = (-N_META) % GLA_CHUNK
    padf = lambda a: jnp.pad(a, ((0, 0), (pad, 0), (0, 0), (0, 0)))
    flip = lambda a: a[:, ::-1]
    qp, kp, vp = padf(q), padf(k), padf(v)
    o_f = gla_chunk_scan(qp, kp, vp, padf(g_f))
    o_b = flip(gla_chunk_scan(flip(qp), flip(kp), flip(vp), flip(padf(g_b))))
    return (o_f + o_b)[:, pad:]

def peer_ffn(x, w_q, sub_keys, u, v):
    N, D = x.shape
    nb = -(-N // PEER_BLOCK)
    xb = jnp.pad(x, ((0, nb * PEER_BLOCK - N), (0, 0))).reshape(nb, PEER_BLOCK, D)

    def block(xi):
        n = xi.shape[0]
        q = (xi @ w_q).reshape(n, PEER_HEADS, 2, PEER_KEY_DIM)
        s = jnp.einsum('nhpc,hpkc->nhpk', q, sub_keys).astype(jnp.float32)
        ts, ti = lax.top_k(s, PEER_TOPK)
        cand_s = (ts[:, :, 0, :, None] + ts[:, :, 1, None, :]).reshape(n, PEER_HEADS, PEER_TOPK * PEER_TOPK)
        cand_i = (ti[:, :, 0, :, None] * PEER_NKEYS + ti[:, :, 1, None, :]).reshape(n, PEER_HEADS, PEER_TOPK * PEER_TOPK)
        best_s, best_p = lax.top_k(cand_s, PEER_TOPK)
        idx = jnp.take_along_axis(cand_i, best_p, axis=-1)
        gate = jax.nn.softmax(best_s, axis=-1)
        act = jax.nn.gelu(jnp.einsum('nd,nhkd->nhk', xi, u[idx]).astype(jnp.float32), approximate=False)
        return jnp.einsum('nhk,nhkd->nd', (gate * act).astype(xi.dtype), v[idx])

    return lax.map(block, xb).reshape(nb * PEER_BLOCK, D)[:N]

def first_inputs(seed: int = 0) -> dict:
    key = jax.random.key(seed)
    ks = jax.random.split(key, 24)
    nrm = lambda k, shape, s: jax.random.normal(k, shape, jnp.float32) * s
    gain = lambda k, shape: 1.0 + 0.02 * jax.random.normal(k, shape, jnp.float32)
    return {
        'x': nrm(ks[0], (BATCH, SEQ, D_MODEL), 1.0),
        'meta_tokens': nrm(ks[1], (N_META, D_MODEL), 1.0),
        'ln1_w': gain(ks[2], (DEPTH, D_MODEL)),
        'w_in': nrm(ks[3], (DEPTH, D_MODEL, IN_WIDTH), D_MODEL ** -0.5),
        'da_lambda_q1': nrm(ks[4], (DEPTH, DA_HEAD_DIM), 0.1),
        'da_lambda_k1': nrm(ks[5], (DEPTH, DA_HEAD_DIM), 0.1),
        'da_lambda_q2': nrm(ks[6], (DEPTH, DA_HEAD_DIM), 0.1),
        'da_lambda_k2': nrm(ks[7], (DEPTH, DA_HEAD_DIM), 0.1),
        'da_subln_w': gain(ks[8], (DEPTH, DA_V_DIM)),
        'gla_gate_w2_f': nrm(ks[9], (DEPTH, GLA_GATE_RANK, GLA_HEADS * GLA_DK), GLA_GATE_RANK ** -0.5),
        'gla_gate_b_f': nrm(ks[10], (DEPTH, GLA_HEADS * GLA_DK), 0.1),
        'gla_gate_w2_b': nrm(ks[11], (DEPTH, GLA_GATE_RANK, GLA_HEADS * GLA_DK), GLA_GATE_RANK ** -0.5),
        'gla_gate_b_b': nrm(ks[12], (DEPTH, GLA_HEADS * GLA_DK), 0.1),
        'gla_norm_w': gain(ks[13], (DEPTH, GLA_DV)),
        'w_out': nrm(ks[14], (DEPTH, MIX_WIDTH, D_MODEL), MIX_WIDTH ** -0.5),
        'ln2_w': gain(ks[15], (DEPTH, D_MODEL)),
        'peer_w_q': nrm(ks[16], (DEPTH, D_MODEL, PEER_HEADS * 2 * PEER_KEY_DIM), D_MODEL ** -0.5),
        'peer_sub_keys': nrm(ks[17], (DEPTH, PEER_HEADS, 2, PEER_NKEYS, PEER_KEY_DIM), PEER_KEY_DIM ** -0.5),
        'peer_u': nrm(ks[18], (DEPTH, PEER_EXPERTS, D_MODEL), D_MODEL ** -0.5),
        'peer_v': nrm(ks[19], (DEPTH, PEER_EXPERTS, D_MODEL), PEER_HEADS ** -0.5),
        'final_norm_w': gain(ks[20], (D_MODEL,)),
    }

def first_block(x, meta_tokens, ln1_w, w_in, da_lambda_q1, da_lambda_k1, da_lambda_q2, da_lambda_k2, da_subln_w, gla_gate_w2_f, gla_gate_b_f, gla_gate_w2_b, gla_gate_b_b, gla_norm_w, w_out, ln2_w, peer_w_q, peer_sub_keys, peer_u, peer_v, final_norm_w):
    B = x.shape[0]
    meta = jnp.broadcast_to(meta_tokens.astype(x.dtype)[None], (B, N_META, D_MODEL))
    h = jnp.concatenate([meta, x], axis=1)
    T = h.shape[1]
    pos = jnp.arange(T)
    splits = np.cumsum(IN_SIZES)[:-1].tolist()
    for l in range(DEPTH):
        xn = rmsnorm(h, ln1_w[l])
        proj = xn @ w_in[l]
        dq, dk, dv, gq, gk, gv, gr, zf, zb = jnp.split(proj, splits, axis=-1)

        lam_init = 0.8 - 0.6 * math.exp(-0.3 * l)
        lam = (jnp.exp(jnp.sum(da_lambda_q1[l].astype(jnp.float32) * da_lambda_k1[l].astype(jnp.float32)))
               - jnp.exp(jnp.sum(da_lambda_q2[l].astype(jnp.float32) * da_lambda_k2[l].astype(jnp.float32))) + lam_init)
        da = diff_attention(dq.reshape(B, T, DA_HEADS, 2, DA_HEAD_DIM), dk.reshape(B, T, DA_HEADS, 2, DA_HEAD_DIM),
                            dv.reshape(B, T, DA_HEADS, DA_V_DIM), lam, pos)
        da = (rmsnorm(da, da_subln_w[l]) * (1.0 - lam_init)).reshape(B, T, DA_WIDTH)

        f32 = jnp.float32
        log_g_f = jax.nn.log_sigmoid((zf @ gla_gate_w2_f[l] + gla_gate_b_f[l]).astype(f32)) / GLA_TAU
        log_g_b = jax.nn.log_sigmoid((zb @ gla_gate_w2_b[l] + gla_gate_b_b[l]).astype(f32)) / GLA_TAU
        go = gla_bidirectional((gq.astype(f32) * (GLA_DK ** -0.5)).reshape(B, T, GLA_HEADS, GLA_DK),
                               gk.astype(f32).reshape(B, T, GLA_HEADS, GLA_DK),
                               gv.astype(f32).reshape(B, T, GLA_HEADS, GLA_DV),
                               log_g_f.reshape(B, T, GLA_HEADS, GLA_DK),
                               log_g_b.reshape(B, T, GLA_HEADS, GLA_DK))
        go = rmsnorm(go, gla_norm_w[l]).reshape(B, T, GLA_WIDTH).astype(h.dtype) * jax.nn.silu(gr)

        h = h + jnp.concatenate([da, go], axis=-1) @ w_out[l]
        if l == DEPTH - 1:
            h = h[:, N_META:]

        hn = rmsnorm(h, ln2_w[l])
        h = h + peer_ffn(hn.reshape(-1, D_MODEL), peer_w_q[l], peer_sub_keys[l], peer_u[l], peer_v[l]).reshape(h.shape)
    return rmsnorm(h, final_norm_w)


POOL_WINDOWS = (2, 4, 8, 16)
N_POOL_GROUPS = 4
D_POOL = D_MODEL // 2
POOL_GROUP = D_POOL // N_POOL_GROUPS
N_HEADS = 8
D_LAT = D_MODEL // 8
N_IDX_HEADS = 8
D_IDX = 32
INDEX_SCALE = (N_IDX_HEADS ** -0.5) * (D_IDX ** -0.5)
ATTN_SCALE = D_LAT ** -0.5
TOP_K_MAX = 256
D_CONV = D_MODEL // 2
CONV_WIDTH = 3
N_BRANCH = 3
D_FF = -(-8 * D_MODEL // (3 * 256)) * 256
SPLITS = (D_POOL, N_HEADS * D_LAT, D_LAT, N_IDX_HEADS * D_IDX, D_IDX,
          N_IDX_HEADS, D_CONV, D_CONV, D_CONV, N_BRANCH * D_MODEL)
N_IN = sum(SPLITS)


def rms_norm(x, g):
    xf = x.astype(jnp.float32)
    y = xf * lax.rsqrt(jnp.mean(xf * xf, axis=-1, keepdims=True) + EPS)
    return (y * g.astype(jnp.float32)).astype(x.dtype)

def split_columns(p):
    offs, acc = [], 0
    for s in SPLITS[:-1]:
        acc += s
        offs.append(acc)
    return jnp.split(p, offs, axis=-1)

def pool_mixer(u, pool_w, pool_scale):
    B, L, _ = u.shape
    uf = u.astype(jnp.float32)
    cs = lax.cumsum(uf, axis=1)
    pos1 = jnp.arange(1, L + 1)
    outs = []
    for g, w in enumerate(POOL_WINDOWS):
        csg = cs[..., g * POOL_GROUP:(g + 1) * POOL_GROUP]
        shifted = jnp.pad(csg, ((0, 0), (w, 0), (0, 0)))[:, :L]
        count = jnp.minimum(pos1, w).astype(jnp.float32)[None, :, None]
        mean = (csg - shifted) / count
        outs.append(mean - uf[..., g * POOL_GROUP:(g + 1) * POOL_GROUP])
    pooled = jnp.stack(outs, axis=2).astype(u.dtype)
    mixed = jnp.einsum('blgc,gcd->blgd', pooled, pool_w).reshape(B, L, D_POOL)
    return mixed * pool_scale

def dsa_attention(q, qi, wi, c, ki):
    B, L = q.shape[0], q.shape[1]
    k_top = min(TOP_K_MAX, SEQ // 4)
    nb = -(-L // Q_BLOCK)
    Lp = nb * Q_BLOCK
    pad = Lp - L

    def to_blocks(a):
        a = jnp.pad(a, [(0, 0), (0, pad)] + [(0, 0)] * (a.ndim - 2))
        return jnp.moveaxis(a.reshape(B, nb, Q_BLOCK, *a.shape[2:]), 1, 0)

    kpos = jnp.arange(L, dtype=jnp.int32)
    qpos = jnp.arange(Lp, dtype=jnp.int32).reshape(nb, Q_BLOCK)
    wi = wi * INDEX_SCALE

    def block(args):
        qb, qib, wb, pb = args
        s = jnp.einsum('bqhd,bkd->bqhk', qib, ki).astype(jnp.float32)
        score = jnp.einsum('bqhk,bqh->bqk', jax.nn.relu(s), wb.astype(jnp.float32))
        causal = kpos[None, None, :] <= pb[None, :, None]
        score = jnp.where(causal, score, -jnp.inf)
        _, sel = lax.top_k(score, k_top)
        c_sel = jax.vmap(lambda cb, ib: cb[ib])(c, sel)
        logits = jnp.einsum('bqhd,bqkd->bqhk', qb, c_sel).astype(jnp.float32) * ATTN_SCALE
        valid = (sel <= pb[None, :, None])[:, :, None, :]
        p = jax.nn.softmax(jnp.where(valid, logits, -jnp.inf), axis=-1).astype(c.dtype)
        return jnp.einsum('bqhk,bqkd->bqhd', p, c_sel)

    out = lax.map(block, (to_blocks(q), to_blocks(qi), to_blocks(wi), qpos))
    out = jnp.moveaxis(out, 0, 1).reshape(B, Lp, N_HEADS * D_LAT)
    return out[:, :L]

def short_conv_mixer(b_gate, c_gate, u, conv_w):
    v = c_gate * u
    rhs = conv_w.reshape(CONV_WIDTH, 1, D_CONV)
    y = lax.conv_general_dilated(v, rhs, window_strides=(1,),
                                 padding=[(CONV_WIDTH - 1, 0)],
                                 dimension_numbers=('NWC', 'WIO', 'NWC'),
                                 feature_group_count=D_CONV)
    return b_gate * y

def hybrid_layer(h, norm1_g, w_in, b_gate, pool_w, pool_scale, w_a, kv_norm_g,
                 w_b, conv_w, w_c, w_o, norm2_g, w_gate_up, w_down):
    B, L, _ = h.shape
    xn = rms_norm(h, norm1_g)
    p = xn @ w_in
    (u_pool, q, c_lat, q_idx, k_idx, w_idx, cb, cc, cu, g_raw) = split_columns(p)
    y_a = pool_mixer(u_pool, pool_w, pool_scale) @ w_a
    c_lat = rms_norm(c_lat, kv_norm_g)
    attn = dsa_attention(q.reshape(B, L, N_HEADS, D_LAT),
                         q_idx.reshape(B, L, N_IDX_HEADS, D_IDX),
                         w_idx, c_lat, k_idx)
    y_b = attn @ w_b
    y_c = short_conv_mixer(cb, cc, cu, conv_w) @ w_c
    g = jax.nn.sigmoid(g_raw + b_gate).reshape(B, L, N_BRANCH, D_MODEL)
    m = g[:, :, 0] * y_a + g[:, :, 1] * y_b + g[:, :, 2] * y_c
    h = h + m @ w_o
    hn = rms_norm(h, norm2_g)
    gate, up = jnp.split(hn @ w_gate_up, 2, axis=-1)
    return h + (jax.nn.silu(gate) * up) @ w_down

def second_inputs(seed: int = 0) -> dict:
    key = jax.random.key(seed)
    ks = jax.random.split(key, 20)
    f32 = jnp.float32

    def nrm(k, shape, fan):
        return jax.random.normal(k, shape, f32) * (fan ** -0.5)

    def gain(k, shape):
        return 1.0 + 0.1 * jax.random.normal(k, shape, f32)

    return {
        "x": jax.random.normal(ks[0], (BATCH, SEQ, D_MODEL), f32),
        "meta": jax.random.normal(ks[1], (N_META, D_MODEL), f32),
        "norm1_g": gain(ks[2], (DEPTH, D_MODEL)),
        "w_in": nrm(ks[3], (DEPTH, D_MODEL, N_IN), D_MODEL),
        "b_gate": 0.01 * jax.random.normal(ks[4], (DEPTH, N_BRANCH * D_MODEL), f32),
        "pool_w": nrm(ks[5], (DEPTH, N_POOL_GROUPS, POOL_GROUP, POOL_GROUP), POOL_GROUP),
        "pool_scale": gain(ks[6], (DEPTH, D_POOL)),
        "w_a": nrm(ks[7], (DEPTH, D_POOL, D_MODEL), D_POOL),
        "kv_norm_g": gain(ks[8], (DEPTH, D_LAT)),
        "w_b": nrm(ks[9], (DEPTH, N_HEADS * D_LAT, D_MODEL), N_HEADS * D_LAT),
        "conv_w": nrm(ks[10], (DEPTH, CONV_WIDTH, D_CONV), CONV_WIDTH),
        "w_c": nrm(ks[11], (DEPTH, D_CONV, D_MODEL), D_CONV),
        "w_o": nrm(ks[12], (DEPTH, D_MODEL, D_MODEL), D_MODEL),
        "norm2_g": gain(ks[13], (DEPTH, D_MODEL)),
        "w_gate_up": nrm(ks[14], (DEPTH, D_MODEL, 2 * D_FF), D_MODEL),
        "w_down": nrm(ks[15], (DEPTH, D_FF, D_MODEL), D_FF),
        "final_g": gain(ks[16], (D_MODEL,)),
    }

def second_block(x, meta, norm1_g, w_in, b_gate, pool_w, pool_scale, w_a, kv_norm_g,
              w_b, conv_w, w_c, w_o, norm2_g, w_gate_up, w_down, final_g):
    B = x.shape[0]
    meta_b = jnp.broadcast_to(meta[None], (B, N_META, D_MODEL)).astype(x.dtype)
    h = jnp.concatenate([meta_b, x], axis=1)
    for l in range(DEPTH):
        h = hybrid_layer(h, norm1_g[l], w_in[l], b_gate[l], pool_w[l], pool_scale[l],
                         w_a[l], kv_norm_g[l], w_b[l], conv_w[l], w_c[l], w_o[l],
                         norm2_g[l], w_gate_up[l], w_down[l])
    return rms_norm(h, final_g)[:, N_META:]


def setup_inputs(seed=0):
    out = dict(first_inputs(seed))
    for name, value in second_inputs(seed + 1).items():
        if name != "x":
            out[name + "_2"] = value
    return out


def reference(
    x, meta_tokens, ln1_w, w_in, da_lambda_q1, da_lambda_k1, da_lambda_q2, da_lambda_k2,
    da_subln_w, gla_gate_w2_f, gla_gate_b_f, gla_gate_w2_b, gla_gate_b_b, gla_norm_w, w_out,
    ln2_w, peer_w_q, peer_sub_keys, peer_u, peer_v, final_norm_w, meta_2, norm1_g_2, w_in_2,
    b_gate_2, pool_w_2, pool_scale_2, w_a_2, kv_norm_g_2, w_b_2, conv_w_2, w_c_2, w_o_2,
    norm2_g_2, w_gate_up_2, w_down_2, final_g_2,
):
    x = first_block(
        x, meta_tokens, ln1_w, w_in, da_lambda_q1, da_lambda_k1, da_lambda_q2, da_lambda_k2,
        da_subln_w, gla_gate_w2_f, gla_gate_b_f, gla_gate_w2_b, gla_gate_b_b, gla_norm_w, w_out,
        ln2_w, peer_w_q, peer_sub_keys, peer_u, peer_v, final_norm_w,
    )
    return second_block(
        x, meta_2, norm1_g_2, w_in_2, b_gate_2, pool_w_2, pool_scale_2, w_a_2, kv_norm_g_2,
        w_b_2, conv_w_2, w_c_2, w_o_2, norm2_g_2, w_gate_up_2, w_down_2, final_g_2,
    )


_drawn_inputs = setup_inputs


def setup_inputs(seed=0):
    import zlib

    import numpy as np

    out = dict(_drawn_inputs(seed))
    spreads = {}
    factors = {'gla_norm_w': 2.697, 'b_gate_2': 8.0, 'kv_norm_g_2': 3.579}
    for name, (base, spread) in spreads.items():
        noise = np.random.default_rng([zlib.crc32(name.encode()), seed]).standard_normal(out[name].shape)
        drawn = base * np.exp(spread * noise) if base else spread * noise
        out[name] = jnp.asarray(drawn.astype(out[name].dtype))
    for name, factor in factors.items():
        out[name] = (out[name] * factor).astype(out[name].dtype)
    return out
```

```python
import math
from contextlib import ExitStack

import numpy as np

import concourse.bass as bass
from concourse import mybir

F32 = mybir.dt.float32
F32R = mybir.dt.float32r
BF16 = mybir.dt.bfloat16
U32 = mybir.dt.uint32
ALU = mybir.AluOpType
ACT = mybir.ActivationFunctionType
AX = mybir.AxisListType

P = 128
D = 1024
KD = D // P
T = 512
NT = T // P
META = 16
TM = META + T
BANK = 512
NBANK = 8
SLAB = 2
SLOTS = 4
EPS = 1e-6
NEG = -3.0e38
FILL = -1.0e30

DA_HEADS, DA_DIM, DA_V = 4, 64, 128
ROPE = DA_DIM // 4
HALF = ROPE // 2
THETA = 500000.0
LAM_INIT = 0.8 - 0.6 * math.exp(-0.3 * 0)
GLA_HEADS, GLA_DK, GLA_DV, GLA_TAU, CHUNK, RANK = 4, 64, 128, 16.0, 64, 16
NCHUNK = T // CHUNK

CONSTS = {}


def _const_layout():
    at = 0
    for name, width in (("ident", P), ("causal", P), ("causal_fill", P), ("iota", P), ("sum_f", P + 2),
                        ("sum_b", P + 2), ("sum_m", META), ("keep_f", GLA_HEADS * P), ("keep_b", GLA_HEADS * P),
                        ("cos", (NT + 1) * 8 * HALF), ("sin", (NT + 1) * 8 * HALF)):
        CONSTS[name] = (at, at + width)
        at += width
    return at


CONST_W = _const_layout()
CONST_2_W = CONSTS["causal_fill"][1]


def const_table():
    table = np.zeros((P, CONST_W), np.float32)

    def put(name, value):
        a, b = CONSTS[name]
        table[:value.shape[0], a:b] = value.reshape(value.shape[0], b - a)

    j, i = np.arange(P)[:, None], np.arange(P)[None, :]
    same = (j // CHUNK) == (i // CHUNK)
    mid = CHUNK // 2
    upto = same & (j % CHUNK <= mid)
    frm = same & (j % CHUNK >= mid)
    put("ident", np.eye(P, dtype=np.float32))
    put("iota", np.tile(np.arange(P, dtype=np.float32), (P, 1)))
    half = np.arange(2)[None, :] * CHUNK
    for name, along, to_mid in (("sum_f", same & (j <= i), upto), ("sum_b", same & (j >= i), frm)):
        shifted = (along.astype(np.float32) - to_mid) / GLA_TAU
        mids = to_mid[:, [0, CHUNK]].astype(np.float32) / GLA_TAU
        put(name, np.concatenate([shifted, mids], 1))
    jm, im = np.arange(META)[:, None], np.arange(META)[None, :]
    put("sum_m", ((jm <= im).astype(np.float32) - 1.0) / GLA_TAU)
    put("keep_f", np.tile((same & (j <= i)).astype(np.float32), (1, GLA_HEADS)))
    put("keep_b", np.tile((same & (j >= i)).astype(np.float32), (1, GLA_HEADS)))
    put("causal", (i <= j).astype(np.float32))
    put("causal_fill", np.where(i <= j, 0.0, FILL).astype(np.float32))
    inv = np.power(np.float32(THETA), -np.arange(0, ROPE, 2, dtype=np.float32) / np.float32(ROPE)).astype(np.float32)
    for name, f in (("cos", np.cos), ("sin", np.sin)):
        v = np.zeros((P, NT + 1, 8, HALF), np.float32)
        for t in range(NT + 1):
            n = P if t < NT else META
            pos = (np.arange(n) + (META + t * P if t < NT else 0)).astype(np.float32)
            v[:n, t] = f((pos[:, None] * inv[None, :]).astype(np.float32)).astype(np.float32)[:, None, :]
        put(name, v)
    return table


class Chain:

    def __init__(self, eng, sem):
        self.eng, self.sem, self.n = eng, sem, 0
        self.turn, self.per_turn = None, 0

    def __call__(self, ins):
        ins.then_inc(self.sem, 1)
        self.n += 1
        now = self.n if self.turn is None else self.n + self.turn * self.per_turn
        self.eng.wait_ge(self.sem, now)

    def loop(self, turn, per_turn):
        self.turn, self.per_turn, self.start = turn, per_turn, self.n

    def end_loop(self, turns):
        assert self.n - self.start == self.per_turn, (self.n - self.start, self.per_turn)
        self.n = self.start + self.per_turn * turns
        self.turn = None


SEMAPHORES = []


def clear_semaphores(nc):
    with nc.Block() as block:

        @block.gpsimd
        def _(pool):
            nc.clear_and_free_semaphores(SEMAPHORES)
    SEMAPHORES.clear()


class Scope:

    def __init__(self, nc, ctx, name):
        self.nc, self.ctx, self.name = nc, ctx, name

    def sb(self, name, shape, dt=F32, side="left"):
        return self.ctx.enter_context(self.nc.sbuf_tensor(f"{self.name}_{name}", shape, dt, side=side))

    def sem(self, name):
        sem = self.nc.alloc_semaphore(f"{self.name}_{name}")
        SEMAPHORES.append(sem)
        return sem

    def block(self):
        return self.ctx.enter_context(self.nc.Block())


class WeightRing:

    def __init__(self, s):
        self.raw = s.sb("w_raw", [P, SLOTS, SLAB, BANK])
        self.hi = s.sb("w_hi", [P, SLOTS, SLAB, BANK], F32R)
        self.lo = s.sb("w_lo", [P, SLOTS, SLAB, BANK], F32R)
        self.landed = [s.sem(f"w_landed{k}") for k in range(SLOTS)]
        self.raw_free = s.sem("w_raw_free")
        self.hi_ready = s.sem("w_hi_ready")
        self.lo_ready = s.sem("w_lo_ready")
        self.slot_free = s.sem("w_slot_free")

    def open_raw(self, pool):
        pool.sem_inc(self.raw_free, SLOTS)

    def open_slots(self, pe):
        pe.sem_inc(self.slot_free, SLOTS - 1)

    def load(self, sp, n, slot, src, parts=None):
        sp.wait_ge(self.raw_free, n + 1)
        width = src.shape[2]
        sp.dma_start(self.raw[:, slot, :src.shape[1], :width], src).then_inc(self.landed[slot], 16)

    def round_hi(self, act, n, slot, turn, width=BANK, rows=SLAB):
        act.wait_ge(self.landed[slot], (turn + 1) * 16)
        act.wait_ge(self.slot_free, n + 1)
        act.activation(self.hi[:, slot, :rows, :width], self.raw[:, slot, :rows, :width], ACT.Copy)\
            .then_inc(self.hi_ready, 1)

    def take_lo(self, pool, n, slot, width=BANK, rows=SLAB):
        pool.wait_ge(self.hi_ready, n + 1)
        pool.tensor_tensor(self.lo[:, slot, :rows, :width], self.raw[:, slot, :rows, :width],
                           self.hi[:, slot, :rows, :width].bitcast(F32), ALU.subtract)\
            .then_inc(self.lo_ready, 1)
        pool.wait_ge(self.lo_ready, n + 1)
        pool.sem_inc(self.raw_free, 1)


def split_products(pe, out, lhs, rhs, start, stop, skip=False, frees=None):
    first = pe.matmul(out, lhs[0], rhs[0], start=start, stop=False, skip_group_check=skip)
    if frees is not None:
        first.then_inc(frees, 1)
    pe.matmul(out, lhs[0], rhs[1], start=False, stop=False, skip_group_check=skip)
    return pe.matmul(out, lhs[1], rhs[0], start=False, stop=stop, skip_group_check=skip)


def weight_slab(w, s, c0, width=BANK, rows=SLAB):
    return w.rearrange("(k p) n -> p k n", p=P)[:, SLAB * s:SLAB * s + rows, bass.ds(c0, width)]


AHEAD, REST = slice(0, SLOTS - 1), slice(SLOTS - 1, None)


class Gemm:

    def __init__(self, s, ring, bank, name=""):
        self.ring, self.bank = ring, bank
        self.tile_done, self.bank_free = s.sem(name + "tile_done"), s.sem(name + "bank_free")
        self.slab0 = self.tile0 = 0

    def plan(self, blocks, turns=1):
        slab, tile = self.slab0, self.tile0
        for b in blocks:
            b["slab0"], b["slabs"] = slab, -(-b["ktiles"] // SLAB)
            slab += b["slabs"]
            b["ms"] = list(range(NT if b["kind"] == "rows" else b["width"] // P)) + [-1] * b["meta"]
            b["tile0"] = tile
            tile += len(b["ms"])
        if turns > 1:
            assert (slab - self.slab0) % SLOTS == 0 and (tile - self.tile0) % NBANK == 0
        per = (slab - self.slab0, tile - self.tile0)
        for b in blocks:
            b["per"] = per
        self.slab0 += turns * per[0]
        self.tile0 += turns * per[1]
        return blocks

    def open_banks(self, taker):
        taker.sem_inc(self.bank_free, NBANK)

    def on_sync(self, sp, b, turn=0):
        for i in range(b["slabs"]):
            n = b["slab0"] + i
            self.ring.load(sp, n + turn * b["per"][0], n % SLOTS, b["slab"](i, turn))

    def on_scalar(self, act, b, turn=0, part=slice(None)):
        for i in range(b["slabs"])[part]:
            n = b["slab0"] + i
            self.ring.round_hi(act, n + turn * b["per"][0], n % SLOTS,
                               n // SLOTS + turn * (b["per"][0] // SLOTS), b["width"])

    def on_gpsimd(self, pool, b, turn=0):
        for i in range(b["slabs"]):
            n = b["slab0"] + i
            self.ring.take_lo(pool, n + turn * b["per"][0], n % SLOTS, b["width"])

    def on_tensor(self, pe, b, turn=0):
        ring = self.ring
        pe.wait_ge(self.bank_free, b["tile0"] + len(b["ms"]) + turn * b["per"][1])
        for i in range(b["slabs"]):
            n = b["slab0"] + i
            pe.wait_ge(ring.lo_ready, n + 1 + turn * b["per"][0])
            for kk in range(SLAB):
                kt = i * SLAB + kk
                first, final = kt == 0, kt == b["ktiles"] - 1
                for j, m in enumerate(b["ms"]):
                    frees = ring.slot_free if kk == 0 and j == 0 else None
                    out = self.bank[:, (b["tile0"] + j) % NBANK, :]
                    wh, wl = ring.hi[:, n % SLOTS, kk, :], ring.lo[:, n % SLOTS, kk, :]
                    x = b["x"](kt, m)
                    if b["kind"] == "rows":
                        last = split_products(pe, out[:, 0:b["width"]], x, (wh[:, 0:b["width"]], wl[:, 0:b["width"]]),
                                              first, final, frees=frees)
                    elif m >= 0:
                        c = slice(m * P, (m + 1) * P)
                        last = split_products(pe, out, (wh[:, c], wl[:, c]), x, first, final, frees=frees)
                    else:
                        for mm in range(b["width"] // P):
                            c = slice(mm * P, (mm + 1) * P)
                            last = split_products(pe, out[:, mm * META:(mm + 1) * META], (wh[:, c], wl[:, c]), x,
                                                  first and mm == 0, final, True)
                    if final:
                        last.then_inc(self.tile_done, 1)

    def take(self, eng, b, use, turn=0):
        for j, m in enumerate(b["ms"]):
            n = b["tile0"] + j
            eng.wait_ge(self.tile_done, n + 1 + turn * b["per"][1])
            use(j, m, self.bank[:, n % NBANK, :]).then_inc(self.bank_free, 1)



class RowStats:

    def __init__(self, s, rows, meta, name="n_", junk=None):
        self.rows, self.meta, self.width = rows, meta, rows.shape[2]
        self.tiles = NT + (meta is not None)
        self.junk = s.sb(name + "junk", [P, self.width]) if junk is None else junk
        self.ss, self.root = s.sb(name + "ss", [P, NT + 1]), s.sb(name + "root", [P, NT + 1])
        self.rstd = s.sb(name + "rstd", [P, NT + 1])
        self.squared, self.meaned, self.rooted = s.sem(name + "squared"), s.sem(name + "mean"), s.sem(name + "root")

    def tile(self, t):
        return (self.rows[:, t, :], P) if t < NT else (self.meta[:, :], META)

    def groups(self):
        return [(P, slice(0, NT))] + ([(META, slice(NT, NT + 1))] if self.meta is not None else [])

    def on_scalar(self, act, ready):
        for t in range(self.tiles):
            ready(act, t)
            src, n = self.tile(t)
            act.activation(self.junk[0:n, :], src, ACT.Square, accum_out=self.ss[0:n, t:t + 1])\
                .then_inc(self.squared, 1)
            act.wait_ge(self.squared, t + 1)
        act.wait_ge(self.meaned, len(self.groups()))
        for n, cols in self.groups():
            act.activation(self.root[0:n, cols], self.ss[0:n, cols], ACT.Sqrt).then_inc(self.rooted, 1)

    def on_vector(self, dve, chain):
        dve.wait_ge(self.squared, self.tiles)
        for n, cols in self.groups():
            dve.tensor_scalar(self.ss[0:n, cols], self.ss[0:n, cols], 1.0 / self.width, EPS, ALU.mult, ALU.add)\
                .then_inc(self.meaned, 1)
        dve.wait_ge(self.rooted, len(self.groups()))
        for n, cols in self.groups():
            last = dve.reciprocal(self.rstd[0:n, cols], self.root[0:n, cols])
        chain(last)


class NormColumns:

    def __init__(self, s, rows, meta, gain_col, hi, lo, ident, bank, xs=None, junk=None):
        self.stats = RowStats(s, rows, meta, junk=junk)
        self.meta, self.gain, self.hi, self.lo, self.ident, self.bank = meta, gain_col, hi, lo, ident, bank
        self.xs = s.sb("n_xs", [P, self.stats.tiles, D]) if xs is None else xs
        self.mtmp = s.sb("n_mtmp", [P, KD, META]) if meta is not None else None
        self.scaled, self.turned = s.sem("n_scaled"), s.sem("n_turned")
        self.hi_done, self.done = s.sem("n_hi"), s.sem("n_done")
        off = META if meta is not None else 0
        self.cols = slice(off, off + T)

    def on_scalar(self, act, ready):
        self.stats.on_scalar(act, ready)
        for k in range(KD):
            act.wait_ge(self.turned, k + 1)
            act.activation(self.hi[:, k, self.cols], self.bank[:, k, :], ACT.Copy,
                           scale=self.gain[:, k:k + 1]).then_inc(self.hi_done, 1)

    def on_vector(self, dve, chain):
        self.stats.on_vector(dve, chain)
        for t in range(self.stats.tiles):
            src, n = self.stats.tile(t)
            dve.tensor_scalar(self.xs[0:n, t, :], src, self.stats.rstd[0:n, t:t + 1], None, ALU.mult)\
                .then_inc(self.scaled, 1)
        for k in range(KD):
            dve.wait_ge(self.hi_done, k + 1)
            dve.scalar_tensor_tensor(self.lo[:, k, self.cols], self.bank[:, k, :], self.gain[:, k:k + 1],
                                     self.hi[:, k, self.cols].bitcast(F32), ALU.mult, ALU.subtract)\
                .then_inc(self.done, 1)
        if self.meta is not None:
            dve.wait_ge(self.turned, KD + 1)
            src = self.bank[:, 0, 0:KD * META].rearrange("p (k m) -> p k m", k=KD)
            gain = self.gain[:, :].unsqueeze(2).to_broadcast([P, KD, META])
            chain(dve.tensor_tensor(self.mtmp[:, :, :], src, gain, ALU.mult))
            hi = self.hi[:, :, 0:META]
            chain(dve.tensor_copy(hi, self.mtmp[:, :, :]))
            dve.tensor_tensor(self.lo[:, :, 0:META], self.mtmp[:, :, :], hi.bitcast(F32), ALU.subtract)\
                .then_inc(self.done, 1)

    def total(self):
        return KD + (self.meta is not None)

    def on_tensor(self, pe):
        pe.wait_ge(self.scaled, NT)
        for k in range(KD):
            for t in range(NT):
                last = pe.transpose(self.bank[:, k, t * P:(t + 1) * P], self.xs[:, t, k * P:(k + 1) * P],
                                    self.ident)
            last.then_inc(self.turned, 1)
        if self.meta is not None:
            pe.wait_ge(self.scaled, NT + 1)
            pe.wait_ge(self.done, 1)
            for k in range(KD):
                last = pe.transpose(self.bank[:, 0, k * META:(k + 1) * META],
                                    self.xs[0:META, NT, k * P:(k + 1) * P], self.ident[0:META, 0:META])
            last.then_inc(self.turned, 1)



def phase_project_1(nc, bank, const, io, life):
    with ExitStack() as ctx:
        s = Scope(nc, ctx, "p1")
        h, hm = s.sb("h", [P, NT, D]), s.sb("h_meta", [META, D])
        xh, xl = s.sb("xh", [P, KD, TM], F32R), s.sb("xl", [P, KD, TM], F32R)
        gain = s.sb("gain", [P, KD])
        ring = WeightRing(s)
        gemm = Gemm(s, ring, bank)
        c_landed, g_landed = s.sem("const_landed"), s.sem("gain_landed")
        x_landed = [s.sem(f"x_landed{t}") for t in range(NT + 1)]
        vec = s.sem("vector_steps")
        ident = const[:, CONSTS["ident"][0]:CONSTS["ident"][1]]
        norm = NormColumns(s, h, hm, gain, xh, xl, ident, bank)

        def rows(kt, m):
            c = slice(META + m * P, META + (m + 1) * P) if m >= 0 else slice(0, P)
            return xh[:, kt, c], xl[:, kt, c]

        def columns(kt, m):
            c = slice(META, TM) if m >= 0 else slice(0, META)
            return xh[:, kt, c], xl[:, kt, c]

        def part(kind, c0, width, meta, dst, dst_meta):
            return dict(kind=kind, slab=lambda i, turn: weight_slab(io["w_in"], i, c0, width), width=width,
                        ktiles=KD, x=rows if kind == "rows" else columns, meta=meta, dst=dst, dst_meta=dst_meta)

        L = life
        blocks = gemm.plan([
            part("rows", 0, BANK, False, L["q"], None), part("rows", 512, BANK, True, L["k"], L["k_m"]),
            part("rows", 1024, BANK, True, L["v"], L["v_m"]), part("columns", 1536, BANK, True, L["gqk"], None),
            part("rows", 2048, BANK, True, L["gv"], L["gv_m"]), part("rows", 2560, BANK, False, L["gr"], None),
            part("columns", 2976, P, True, L["zT"], None)])
        block = s.block()

        @block.sync
        def _(sp):
            sp.dma_start(const[:, :], io["const"]).then_inc(c_landed, 16)
            for t in range(NT):
                sp.dma_start(h[:, t, :], io["x"][t * P:(t + 1) * P, :]).then_inc(x_landed[t], 16)
            sp.dma_start(hm[:, :], io["meta_tokens"]).then_inc(x_landed[NT], 16)
            sp.dma_start(gain[:, :], io["ln1_w"]).then_inc(g_landed, 16)
            for b in blocks:
                gemm.on_sync(sp, b)

        @block.gpsimd
        def _(pool):
            ring.open_raw(pool)
            for b in blocks:
                gemm.on_gpsimd(pool, b)

        @block.scalar
        def _(act):
            act.wait_ge(g_landed, 16)
            norm.on_scalar(act, lambda e, t: e.wait_ge(x_landed[t], 16))
            for b in blocks:
                gemm.on_scalar(act, b)

        @block.tensor
        def _(pe):
            ring.open_slots(pe)
            pe.wait_ge(c_landed, 16)
            norm.on_tensor(pe)
            pe.wait_ge(norm.done, norm.total())
            for b in blocks:
                gemm.on_tensor(pe, b)

        @block.vector
        def _(dve):
            chain = Chain(dve, vec)
            gemm.open_banks(dve)
            dve.wait_ge(g_landed, 16)
            for landed in x_landed:
                dve.wait_ge(landed, 16)
            norm.on_vector(dve, chain)
            for b in blocks:
                def use(j, m, got):
                    if b["kind"] == "rows" and m >= 0:
                        return dve.tensor_copy(b["dst"][:, m, :], got)
                    if b["kind"] == "rows":
                        return dve.tensor_copy(b["dst_meta"][:, :], got[0:META, :])
                    if m >= 0:
                        return dve.tensor_copy(b["dst"][:, m, META:TM], got)
                    n = b["width"] // P
                    return dve.tensor_copy(b["dst"][:, :, 0:META],
                                           got[:, 0:n * META].rearrange("p (m c) -> p m c", m=n))

                gemm.take(dve, b, use)



def phase_diff_attention(nc, bank, const, io, life):
    with ExitStack() as ctx:
        s = Scope(nc, ctx, "da")
        q, k, km, v, vm, mix = (life[n] for n in ("q", "k", "k_m", "v", "v_m", "mix"))
        qT = s.sb("qT", [P, DA_HEADS, T])
        kT = s.sb("kT", [P, DA_HEADS, TM])
        rot = s.sb("rot", [P, 4, NT * 8 * HALF])
        p = s.sb("p", [P, 2, 2, TM])
        a = s.sb("a", [P, 2, TM])
        aT = s.sb("aT", [P, 2, T])
        aTm = s.sb("aTm", [META, 2, P])
        nmax, total, inv = s.sb("nmax", [P, 4]), s.sb("total", [P, 4]), s.sb("inv", [P, 4])
        lam_in = s.sb("lam_in", [P, 4, DA_DIM])
        lam_prod = s.sb("lam_prod", [P, 2, DA_DIM])
        lam_sum, lam = s.sb("lam_sum", [P, 2]), s.sb("lam", [P, 2])
        sub_w = s.sb("sub_w", [P, DA_V])
        sq = s.sb("sq", [P, NT * DA_HEADS, DA_V])
        ss, root = s.sb("ss", [P, NT * DA_HEADS]), s.sb("root", [P, NT * DA_HEADS])
        in_landed = s.sem("in_landed")
        turned_q, turned_k, cols_ready = s.sem("rot_q"), s.sem("rot_k"), s.sem("cols_ready")
        tp, lam_exp, lam_done = s.sem("transposed"), s.sem("lam_exp"), s.sem("lam_done")
        scored, maxed, exped, pair_done = s.sem("scored"), s.sem("maxed"), s.sem("exped"), s.sem("pair_done")
        diffed, a_turned, aT_ready = s.sem("diffed"), s.sem("a_turned"), s.sem("aT_ready")
        o_done, o_taken, squared, rooted, ms = (s.sem("o_done"), s.sem("o_taken"), s.sem("squared"),
                                                s.sem("rooted"), s.sem("mean_square"))
        vec = s.sem("vector_steps")
        ident = const[:, CONSTS["ident"][0]:CONSTS["ident"][1]]

        def angles(name, t0, t1, n):
            c0 = CONSTS[name][0] + t0 * 8 * HALF
            return const[0:n, c0:c0 + (t1 - t0) * 8 * HALF].rearrange("p (t h c) -> p t h c", h=8, c=HALF)

        turns = [(hd, t) for hd in range(DA_HEADS) for t in range(NT)]

        def pair(r, c):
            return 2 * ((2 * r + c) % 3)

        def scores_of(r, c):
            return bank[:, pair(r, c):pair(r, c) + 2, :].rearrange("p b n -> p (b n)")[:, 0:TM]

        block = s.block()

        @block.sync
        def _(sp):
            for n, name in enumerate(("da_lambda_q1", "da_lambda_k1", "da_lambda_q2", "da_lambda_k2")):
                sp.dma_start(lam_in[:, n, :], io[name].to_broadcast([P, DA_DIM])).then_inc(in_landed, 16)
            sp.dma_start(sub_w[:, :], io["da_subln_w"].to_broadcast([P, DA_V])).then_inc(in_landed, 16)

        @block.scalar
        def _(act):
            act.wait_ge(lam_done, 1)
            act.activation(lam[:, :], lam_sum[:, :], ACT.Exp).then_inc(lam_exp, 1)
            for r in range(len(turns) + 1):
                if r < len(turns):
                    for c in range(2):
                        u = 2 * r + c
                        act.wait_ge(maxed, u + 1)
                        if r >= 2:
                            act.wait_ge(diffed, r - 1)
                        act.activation(p[:, r % 2, c, :], scores_of(r, c), ACT.Exp,
                                       bias=nmax[:, u % 4:u % 4 + 1], accum_out=total[:, u % 4:u % 4 + 1])\
                            .then_inc(exped, 1)
                if r >= 1:
                    act.wait_ge(a_turned, r)
                    if r >= 3:
                        act.wait_ge(o_done, r - 2)
                    act.activation(aTm[:, (r - 1) % 2, :], bank[0:META, 7, 0:P], ACT.Copy)
                    act.activation(aT[:, (r - 1) % 2, :], bank[:, 6, :], ACT.Copy).then_inc(aT_ready, 1)
            act.wait_ge(o_taken, len(turns))
            act.activation(sq[:, :, :].rearrange("p (t h) v -> p t h v", t=NT),
                           mix[:, :, 0:DA_HEADS * DA_V].rearrange("p t (h v) -> p t h v", h=DA_HEADS),
                           ACT.Square).then_inc(squared, 1)
            act.wait_ge(ms, 1)
            act.activation(root[:, :], ss[:, :], ACT.Sqrt).then_inc(rooted, 1)

        @block.tensor
        def _(pe):
            def columns(n, src, sem, count):
                pe.wait_ge(sem, count)
                if n >= 4:
                    pe.wait_ge(cols_ready, n - 3)
                for t in range(NT):
                    last = pe.transpose(bank[:, n % 4, t * P:(t + 1) * P], src(t), ident)
                last.then_inc(tp, 1)

            for hd in range(DA_HEADS):
                columns(hd, lambda t: q[:, t, hd * P:(hd + 1) * P], turned_q, 1)
            for hd in range(DA_HEADS):
                columns(DA_HEADS + hd, lambda t: k[:, t, hd * P:(hd + 1) * P], turned_k, 2)
            for hd in range(DA_HEADS):
                last = pe.transpose(bank[:, 4, hd * META:(hd + 1) * META], km[:, hd * P:(hd + 1) * P],
                                    ident[0:META, 0:META])
            last.then_inc(tp, 1)
            pe.wait_ge(cols_ready, 2 * DA_HEADS + 1)
            for r in range(len(turns) + 2):
                if r < len(turns):
                    hd, t = turns[r]
                    for c in range(2):
                        u = 2 * r + c
                        if u >= 3:
                            pe.wait_ge(exped, u - 2)
                        cc = slice(c * DA_DIM, (c + 1) * DA_DIM)
                        b = pair(r, c)
                        pe.matmul(bank[:, b, :], qT[cc, hd, t * P:(t + 1) * P], kT[cc, hd, 0:BANK],
                                  start=True, stop=True)
                        pe.matmul(bank[:, b + 1, 0:TM - BANK], qT[cc, hd, t * P:(t + 1) * P],
                                  kT[cc, hd, BANK:TM], start=True, stop=True).then_inc(scored, 1)
                if r >= 1 and r <= len(turns):
                    e = r - 1
                    pe.wait_ge(diffed, e + 1)
                    if e >= 1:
                        pe.wait_ge(o_taken, e)
                        pe.wait_ge(aT_ready, e)
                    pe.transpose(bank[0:META, 7, 0:P], a[:, e % 2, 0:META], ident)
                    for kt in range(NT):
                        last = pe.transpose(bank[:, 6, kt * P:(kt + 1) * P],
                                            a[:, e % 2, META + kt * P:META + (kt + 1) * P], ident)
                    last.then_inc(a_turned, 1)
                if r >= 1 and r <= len(turns):
                    e = r - 1
                    hd = turns[e][0]
                    pe.wait_ge(aT_ready, e + 1)
                    o = bank[:, 7, P:2 * P]
                    pe.matmul(o, aTm[:, e % 2, :], vm[:, hd * DA_V:(hd + 1) * DA_V], start=True, stop=False)
                    for kt in range(NT):
                        last = pe.matmul(o, aT[:, e % 2, kt * P:(kt + 1) * P],
                                         v[:, kt, hd * DA_V:(hd + 1) * DA_V], start=False, stop=kt == NT - 1)
                    last.then_inc(o_done, 1)

        @block.vector
        def _(dve):
            chain = Chain(dve, vec)

            def rotate(rows, t0, t1, n):
                x1, x2 = rows[:, :, :, 0:HALF], rows[:, :, :, HALF:ROPE]
                cos, sin = angles("cos", t0, t1, n), angles("sin", t0, t1, n)
                w = (t1 - t0) * 8 * HALF
                r = [rot[0:n, i, 0:w].rearrange("p (t h c) -> p t h c", h=8, c=HALF) for i in range(4)]
                dve.tensor_tensor(r[0], x1, cos, ALU.mult)
                dve.tensor_tensor(r[1], x2, sin, ALU.mult)
                dve.tensor_tensor(r[2], x2, cos, ALU.mult)
                chain(dve.tensor_tensor(r[3], x1, sin, ALU.mult))
                dve.tensor_tensor(x1, r[0], r[1], ALU.subtract)
                return dve.tensor_tensor(x2, r[2], r[3], ALU.add)

            def split(ap):
                return ap.rearrange("p t (h c) -> p t h c", h=8)

            ins = rotate(split(q[:, :, :]), 0, NT, P)
            ins.then_inc(turned_q, 1)
            dve.wait_ge(turned_q, 1)
            ins = rotate(split(k[:, :, :]), 0, NT, P)
            ins.then_inc(turned_k, 1)
            dve.wait_ge(turned_k, 1)
            ins = rotate(km[:, :].rearrange("p (t h c) -> p t h c", t=1, h=8), NT, NT + 1, META)
            ins.then_inc(turned_k, 1)
            dve.wait_ge(in_landed, 16 * 5)
            for n in range(2):
                chain(dve.tensor_tensor(lam_prod[:, n, :], lam_in[:, 2 * n, :], lam_in[:, 2 * n + 1, :], ALU.mult))
            dve.tensor_reduce(lam_sum[:, :], lam_prod[:, :, :], AX.X, ALU.add).then_inc(lam_done, 1)
            chain(dve.tensor_scalar(sub_w[:, :], sub_w[:, :], 1.0 - LAM_INIT, None, ALU.mult))
            dve.wait_ge(lam_exp, 1)
            chain(dve.tensor_tensor(lam[:, 0:1], lam[:, 1:2], lam[:, 0:1], ALU.subtract))
            chain(dve.tensor_scalar(lam[:, 0:1], lam[:, 0:1], -LAM_INIT, None, ALU.add))

            for hd in range(DA_HEADS):
                dve.wait_ge(tp, hd + 1)
                dve.tensor_scalar(qT[:, hd, :], bank[:, hd % 4, :], DA_DIM ** -0.5, None, ALU.mult)\
                    .then_inc(cols_ready, 1)
            for hd in range(DA_HEADS):
                dve.wait_ge(tp, DA_HEADS + hd + 1)
                dve.tensor_copy(kT[:, hd, META:TM], bank[:, hd % 4, :]).then_inc(cols_ready, 1)
            dve.wait_ge(tp, 2 * DA_HEADS + 1)
            dve.tensor_copy(kT[:, :, 0:META],
                            bank[:, 4, 0:DA_HEADS * META].rearrange("p (h m) -> p h m", m=META))\
                .then_inc(cols_ready, 1)

            def take_output(e):
                hd, t = turns[e]
                dve.wait_ge(o_done, e + 1)
                dve.tensor_copy(mix[:, t, hd * DA_V:(hd + 1) * DA_V], bank[:, 7, P:2 * P]).then_inc(o_taken, 1)

            for r in range(len(turns) + 1):
                if r < len(turns):
                    for c in range(2):
                        u = 2 * r + c
                        dve.wait_ge(scored, u + 1)
                        if u >= 4:
                            dve.wait_ge(exped, u - 3)
                        dve.tensor_reduce(nmax[:, u % 4:u % 4 + 1], scores_of(r, c), AX.X, ALU.max,
                                          negate=True).then_inc(maxed, 1)
                if r >= 1:
                    e = r - 1
                    o = 2 * (e % 2)
                    if e >= 1:
                        take_output(e - 1)
                    dve.wait_ge(exped, 2 * e + 2)
                    if e >= 2:
                        dve.wait_ge(a_turned, e - 1)
                    chain(dve.reciprocal(inv[:, o:o + 2], total[:, o:o + 2]))
                    dve.tensor_scalar(a[:, e % 2, :], p[:, e % 2, 0, :], inv[:, o:o + 1], None, ALU.mult)
                    chain(dve.tensor_tensor(inv[:, o + 1:o + 2], inv[:, o + 1:o + 2], lam[:, 0:1], ALU.mult))
                    dve.scalar_tensor_tensor(a[:, e % 2, :], p[:, e % 2, 1, :], inv[:, o + 1:o + 2],
                                             a[:, e % 2, :], ALU.mult, ALU.add).then_inc(diffed, 1)
            take_output(len(turns) - 1)
            dve.wait_ge(squared, 1)
            chain(dve.tensor_reduce(ss[:, :], sq[:, :, :], AX.X, ALU.add))
            dve.tensor_scalar(ss[:, :], ss[:, :], 1.0 / DA_V, EPS, ALU.mult, ALU.add).then_inc(ms, 1)
            dve.wait_ge(rooted, 1)
            chain(dve.reciprocal(root[:, :], root[:, :]))
            for t in range(NT):
                for hd in range(DA_HEADS):
                    o = mix[:, t, hd * DA_V:(hd + 1) * DA_V]
                    n = t * DA_HEADS + hd
                    dve.scalar_tensor_tensor(o, o, root[:, n:n + 1], sub_w[:, :], ALU.mult, ALU.mult)



def phase_linear_attention(nc, bank, const, io, life):
    with ExitStack() as ctx:
        s = Scope(nc, ctx, "gla")
        qk, zT, gv, gvm, gr, mix = (life[n] for n in ("gqk", "zT", "gv", "gv_m", "gr", "mix"))
        FW, BW = 0, 1
        GK = GLA_HEADS * GLA_DK
        w2 = s.sb("w2", [P, 2 * GK])
        w2_bias = s.sb("w2_bias", [P, 2 * GK])
        norm_w = s.sb("norm_w", [P, GLA_DV])
        y, e = s.sb("y", [P, NT + 1, 2 * GK]), s.sb("e", [P, NT + 1, 2 * GK])
        grow, shrink = life["q"], life["k"]
        qs, ks = s.sb("qs", [P, 4, T]), s.sb("ks", [P, 4, T])
        mid, decay = s.sb("mid", [P, 4, NCHUNK]), s.sb("decay", [P, 4, NCHUNK])
        decay_m = s.sb("decay_m", [P, 2])
        km, kmT = s.sb("km", [P, 2, META]), s.sb("kmT", [META, GK])
        ksT = s.sb("ksT", [P, 4, NT, P])
        at = s.sb("at", [P, 2, NT, GLA_HEADS * P])
        kv = s.sb("kv", [P, 4, NCHUNK, GLA_DV])
        st = s.sb("st", [P, 4, NCHUNK, GLA_DV])
        sq = kv[:, 0:2, :, :].rearrange("p g c v -> p (g c) v")
        gate = gr
        ss = s.sb("ss", [P, NT * GLA_HEADS])
        names = ("w2_landed", "zeroed", "z_done", "y_done", "e_done", "ln_done", "lg_done", "b_done", "grown",
                 "qk_done", "mid_taken", "decay_sum", "decayed", "km_done", "k_turned", "k_taken", "a_done",
                 "a_taken", "kv_done", "kv_taken", "states", "o_done", "o_taken", "squared", "mean", "rooted",
                 "gated", "vector_steps")
        S = {n: s.sem(n) for n in names}
        ident = const[:, CONSTS["ident"][0]:CONSTS["ident"][1]]

        def c(name, n=P):
            return const[0:n, CONSTS[name][0]:CONSTS[name][1]]

        sums = [c("sum_f"), c("sum_b")]
        rows96 = slice(96, 96 + 2 * RANK)
        tiles = [(t, P) for t in range(NT)] + [(NT, META)]
        block = s.block()

        @block.sync
        def _(sp):
            sp.wait_ge(S["zeroed"], 1)
            sp.dma_start(w2[96:96 + RANK, 0:GK], io["gla_gate_w2_f"]).then_inc(S["w2_landed"], 16)
            sp.dma_start(w2[96 + RANK:P, GK:2 * GK], io["gla_gate_w2_b"]).then_inc(S["w2_landed"], 16)
            sp.dma_start(w2_bias[:, 0:GK], io["gla_gate_b_f"].to_broadcast([P, GK])).then_inc(S["w2_landed"], 16)
            sp.dma_start(w2_bias[:, GK:2 * GK], io["gla_gate_b_b"].to_broadcast([P, GK]))\
                .then_inc(S["w2_landed"], 16)
            sp.dma_start(norm_w[:, :], io["gla_norm_w"].to_broadcast([P, GLA_DV])).then_inc(S["w2_landed"], 16)

        @block.tensor
        def _(pe):
            pe.wait_ge(S["w2_landed"], 16 * 5)
            for t, n in tiles:
                cols = slice(META + t * P, META + (t + 1) * P) if t < NT else slice(0, META)
                pe.matmul(bank[0:n, t, :], zT[rows96, 0, cols], w2[rows96, :], start=True, stop=True)\
                    .then_inc(S["z_done"], 1)
            pe.wait_ge(S["lg_done"], 2)
            for g in range(4):
                for t in range(NT):
                    lg = y[:, t, g * P:(g + 1) * P]
                    last = pe.matmul(bank[:, g, t * P:(t + 1) * P], lg, sums[g // 2][:, 0:P], start=True, stop=True)
                last.then_inc(S["b_done"], 1)
            for g in range(4):
                for t in range(NT):
                    lg = y[:, t, g * P:(g + 1) * P]
                    pe.matmul(bank[:, 5, 2 * (g * NT + t):2 * (g * NT + t) + 2], lg, sums[g // 2][:, P:P + 2],
                              start=True, stop=True)
            for m in range(2):
                last = pe.matmul(bank[:, 5, 64 + m * META:64 + (m + 1) * META], y[0:META, NT, m * P:(m + 1) * P],
                                 c("sum_m", META), start=True, stop=True)
            last.then_inc(S["b_done"], 1)
            for g in range(4):
                pe.wait_ge(S["qk_done"], g + 1)
                if g >= 2:
                    pe.wait_ge(S["k_taken"], g - 1)
                for t in range(NT):
                    last = pe.transpose(bank[:, 6 + g % 2, t * P:(t + 1) * P], ks[:, g, t * P:(t + 1) * P], ident)
                last.then_inc(S["k_turned"], 1)
            pe.wait_ge(S["km_done"], 1)
            pe.wait_ge(S["k_taken"], 4)
            for m in range(2):
                last = pe.transpose(bank[0:META, 6, m * P:(m + 1) * P], km[:, m, :], ident)
            last.then_inc(S["k_turned"], 1)
            for t in range(NT):
                if t == 0:
                    pe.wait_ge(S["grown"], 5)
                    pe.wait_ge(S["mid_taken"], 2)
                else:
                    pe.wait_ge(S["a_taken"], t)
                for d in range(2):
                    for hd in range(GLA_HEADS):
                        g, hp = 2 * d + hd // 2, hd % 2
                        r = slice(hp * GLA_DK, (hp + 1) * GLA_DK)
                        last = pe.matmul(bank[:, 2 * d + hp, (hd // 2) * P:(hd // 2 + 1) * P],
                                         ks[r, g, t * P:(t + 1) * P], qs[r, g, t * P:(t + 1) * P],
                                         start=True, stop=True)
                last.then_inc(S["a_done"], 1)
            pe.wait_ge(S["k_taken"], 5)
            for hd in range(GLA_HEADS):
                out = bank[(hd % 2) * GLA_DK:(hd % 2 + 1) * GLA_DK, 7, (hd // 2) * GLA_DV:(hd // 2 + 1) * GLA_DV]
                last = pe.matmul(out, kmT[:, hd * GLA_DK:(hd + 1) * GLA_DK],
                                 gvm[:, hd * GLA_DV:(hd + 1) * GLA_DV], start=True, stop=True)
            last.then_inc(S["kv_done"], 1)
            pe.wait_ge(S["a_taken"], NT)
            for d in range(2):
                for cp in range(2):
                    for half in range(2):
                        n = (d * 2 + cp) * 2 + half
                        b = n % 4
                        if n >= 4:
                            pe.wait_ge(S["kv_taken"], 1 + n - 3)
                        for i in range(2):
                            t = 2 * half + i
                            r = slice(cp * CHUNK, (cp + 1) * CHUNK)
                            for hd in range(GLA_HEADS):
                                m, hp = hd // 2, hd % 2
                                out = bank[hp * GLA_DK:(hp + 1) * GLA_DK, b,
                                           (i * 2 + m) * GLA_DV:(i * 2 + m + 1) * GLA_DV]
                                last = pe.matmul(out, ksT[r, 2 * d + m, t, hp * GLA_DK:(hp + 1) * GLA_DK],
                                                 gv[r, t, hd * GLA_DV:(hd + 1) * GLA_DV], start=True, stop=True)
                        last.then_inc(S["kv_done"], 1)
            pe.wait_ge(S["kv_taken"], 9)
            pe.wait_ge(S["states"], 2)
            for t in range(NT):
                for hp in range(2):
                    b = (2 * t + hp) % NBANK
                    for m in range(2):
                        hd = 2 * m + hp
                        r = slice(hp * GLA_DK, (hp + 1) * GLA_DK)
                        cols = slice(m * GLA_DV, (m + 1) * GLA_DV)
                        pe.matmul(bank[:, b, cols], at[:, 0, t, (hp * 2 + m) * P:(hp * 2 + m + 1) * P],
                                  gv[:, t, hd * GLA_DV:(hd + 1) * GLA_DV], start=True, stop=False,
                                  skip_group_check=True)
                        for cp in range(2):
                            ch = 2 * t + cp
                            out = bank[cp * CHUNK:(cp + 1) * CHUNK, b, cols]
                            toks = slice(ch * CHUNK, (ch + 1) * CHUNK)
                            for d in range(2):
                                if d == BW and ch == NCHUNK - 1:
                                    continue
                                last = pe.matmul(out, qs[r, 2 * d + m, toks], st[r, 2 * d + m, ch, :],
                                                 start=False, stop=True, skip_group_check=True)
                    last.then_inc(S["o_done"], 1)

        @block.scalar
        def _(act):
            act.activation(gate[:, :, :], gr[:, :, :], ACT.Silu).then_inc(S["gated"], 1)
            for i, (n, ts) in enumerate(((P, slice(0, NT)), (META, slice(NT, NT + 1)))):
                act.wait_ge(S["y_done"], i + 1)
                act.activation(e[0:n, ts, :], e[0:n, ts, :], ACT.Exp, scale=-1.0).then_inc(S["e_done"], 1)
            for i, (n, ts) in enumerate(((P, slice(0, NT)), (META, slice(NT, NT + 1)))):
                act.wait_ge(S["e_done"], i + 1)
                act.activation(e[0:n, ts, :], e[0:n, ts, :], ACT.Ln, bias=1.0).then_inc(S["ln_done"], 1)
            for g in range(4):
                act.wait_ge(S["b_done"], g + 1)
                act.activation(grow[:, g, :], bank[:, g, :], ACT.Exp)
                act.activation(shrink[:, g, :], bank[:, g, :], ACT.Exp, scale=-1.0).then_inc(S["grown"], 1)
            act.wait_ge(S["b_done"], 5)
            act.activation(km[:, :, :], bank[:, 5, 64:64 + 2 * META].rearrange("p (m c) -> p m c", m=2), ACT.Exp,
                           scale=-1.0).then_inc(S["grown"], 1)
            act.wait_ge(S["decay_sum"], 1)
            act.activation(decay[:, :, :], decay[:, :, :], ACT.Exp)
            act.activation(decay_m[:, :], decay_m[:, :], ACT.Exp).then_inc(S["decayed"], 1)
            for g in range(4):
                act.wait_ge(S["k_turned"], g + 1)
                act.activation(ksT[:, g, :, :].rearrange("p t c -> p (t c)"), bank[:, 6 + g % 2, :], ACT.Copy)\
                    .then_inc(S["k_taken"], 1)
            act.wait_ge(S["k_turned"], 5)
            act.activation(kmT[:, :], bank[0:META, 6, 0:GK], ACT.Copy).then_inc(S["k_taken"], 1)
            act.wait_ge(S["decayed"], 1)
            act.wait_ge(S["kv_done"], 1)
            for m in range(2):
                last = act.activation(st[:, m, 0, :], bank[:, 7, m * GLA_DV:(m + 1) * GLA_DV], ACT.Copy,
                                      scale=decay_m[:, m:m + 1])
            last.then_inc(S["kv_taken"], 1)
            for d in range(2):
                for cp in range(2):
                    for half in range(2):
                        n = (d * 2 + cp) * 2 + half
                        act.wait_ge(S["kv_done"], n + 2)
                        for i in range(2):
                            for m in range(2):
                                g, ch = 2 * d + m, 2 * (2 * half + i) + cp
                                last = act.activation(kv[:, g, ch, :],
                                                      bank[:, n % 4, (i * 2 + m) * GLA_DV:(i * 2 + m + 1) * GLA_DV],
                                                      ACT.Copy, scale=decay[:, g, ch:ch + 1])
                        last.then_inc(S["kv_taken"], 1)
            act.wait_ge(S["o_taken"], 2 * NT)
            act.activation(sq.rearrange("p (t h) v -> p t h v", t=NT),
                           mix[:, :, 512:1024].rearrange("p t (h v) -> p t h v", h=GLA_HEADS),
                           ACT.Square).then_inc(S["squared"], 1)
            act.wait_ge(S["mean"], 1)
            act.activation(ss[:, :], ss[:, :], ACT.Sqrt).then_inc(S["rooted"], 1)

        @block.vector
        def _(dve):
            chain = Chain(dve, S["vector_steps"])
            dve.memset(w2[96:P, :], 0.0).then_inc(S["zeroed"], 1)
            dve.wait_ge(S["w2_landed"], 16 * 5)
            for t, n in tiles:
                dve.wait_ge(S["z_done"], t + 1)
                last = dve.tensor_tensor(y[0:n, t, :], bank[0:n, t, :], w2_bias[0:n, :], ALU.add)
            chain(last)
            groups = ((P, slice(0, NT)), (META, slice(NT, NT + 1)))
            for n, ts in groups:
                dve.scalar_tensor_tensor(e[0:n, ts, :], y[0:n, ts, :], -1.0, y[0:n, ts, :], ALU.mult, ALU.max)\
                    .then_inc(S["y_done"], 1)
            for i, (n, ts) in enumerate(groups):
                dve.wait_ge(S["ln_done"], i + 1)
                dve.scalar_tensor_tensor(y[0:n, ts, :], y[0:n, ts, :], 0.0, e[0:n, ts, :], ALU.min, ALU.subtract)\
                    .then_inc(S["lg_done"], 1)
            for g in range(4):
                m = g % 2
                dve.wait_ge(S["grown"], g + 1)
                dve.scalar_tensor_tensor(qs[:, g, :], qk[:, m, META:TM], GLA_DK ** -0.5, grow[:, g, :],
                                         ALU.mult, ALU.mult)
                dve.tensor_tensor(ks[:, g, :], qk[:, 2 + m, META:TM], shrink[:, g, :], ALU.mult)\
                    .then_inc(S["qk_done"], 1)
            dve.wait_ge(S["grown"], 5)
            dve.tensor_tensor(km[:, :, :], km[:, :, :], qk[:, 2:4, 0:META], ALU.mult).then_inc(S["km_done"], 1)
            dve.wait_ge(S["b_done"], 5)
            dve.tensor_copy(mid[:, :, :], bank[:, 5, 0:4 * NCHUNK].rearrange("p (g c) -> p g c", g=4))\
                .then_inc(S["mid_taken"], 1)
            dve.wait_ge(S["mid_taken"], 1)
            dve.tensor_copy(decay_m[:, :], mid[:, 0:2, 0])
            ends = [bank[:, g, :].rearrange("p (c i) -> p c i", i=CHUNK)[:, :, CHUNK - 1 if g < 2 else 0]
                    for g in range(4)]
            for g in range(4):
                if g < 2:
                    dve.tensor_tensor(decay[:, g, 0:NCHUNK - 1], ends[g][:, 0:NCHUNK - 1], mid[:, g, 1:NCHUNK], ALU.add)
                    last = dve.tensor_copy(decay[:, g, NCHUNK - 1:NCHUNK], ends[g][:, NCHUNK - 1:NCHUNK])
                else:
                    dve.tensor_tensor(decay[:, g, 1:NCHUNK], ends[g][:, 1:NCHUNK], mid[:, g, 0:NCHUNK - 1], ALU.add)
                    last = dve.tensor_copy(decay[:, g, 0:1], ends[g][:, 0:1])
            last.then_inc(S["mid_taken"], 1)
            dve.wait_ge(S["mid_taken"], 2)
            dve.sem_inc(S["decay_sum"], 1)
            for t in range(NT):
                dve.wait_ge(S["a_done"], t + 1)
                for d, keep in ((FW, c("keep_f")), (BW, c("keep_b"))):
                    last = dve.tensor_tensor(
                        at[:, d, t, :].rearrange("p (b n) -> p b n", b=2), bank[:, 2 * d:2 * d + 2, 0:2 * P],
                        keep.rearrange("p (b n) -> p b n", b=2), ALU.mult)
                last.then_inc(S["a_taken"], 1)
                dve.wait_ge(S["a_taken"], t + 1)
                last = dve.tensor_tensor(at[:, 0, t, :], at[:, 0, t, :], at[:, 1, t, :], ALU.add)
            chain(last)
            dve.wait_ge(S["kv_taken"], 1)
            dve.wait_ge(S["decayed"], 1)
            for i in range(NCHUNK - 1):
                f, b = i, NCHUNK - 1 - i
                if i == 0:
                    dve.wait_ge(S["kv_taken"], 9)
                for m in range(2):
                    last = dve.scalar_tensor_tensor(st[:, m, f + 1, :], st[:, m, f, :], decay[:, m, f:f + 1],
                                                    kv[:, m, f, :], ALU.mult, ALU.add)
                for m in range(2, 4):
                    if i == 0:
                        last = dve.tensor_copy(st[:, m, b - 1, :], kv[:, m, b, :])
                    else:
                        last = dve.scalar_tensor_tensor(st[:, m, b - 1, :], st[:, m, b, :], decay[:, m, b:b + 1],
                                                        kv[:, m, b, :], ALU.mult, ALU.add)
                chain(last)
            dve.sem_inc(S["states"], 2)
            for t in range(NT):
                for hp in range(2):
                    dve.wait_ge(S["o_done"], 2 * t + hp + 1)
                    out = mix[:, t, 512:1024].rearrange("p (m hp v) -> p m hp v", m=2, hp=2)[:, :, hp, :]
                    dve.tensor_copy(out, bank[:, 2 * t + hp, 0:2 * GLA_DV].rearrange("p (m v) -> p m v", m=2))\
                        .then_inc(S["o_taken"], 1)
            dve.wait_ge(S["squared"], 1)
            chain(dve.tensor_reduce(ss[:, :], sq, AX.X, ALU.add))
            dve.tensor_scalar(ss[:, :], ss[:, :], 1.0 / GLA_DV, EPS, ALU.mult, ALU.add).then_inc(S["mean"], 1)
            dve.wait_ge(S["rooted"], 1)
            chain(dve.reciprocal(ss[:, :], ss[:, :]))
            for t in range(NT):
                for hd in range(GLA_HEADS):
                    o = mix[:, t, 512 + hd * GLA_DV:512 + (hd + 1) * GLA_DV]
                    n = t * GLA_HEADS + hd
                    last = dve.scalar_tensor_tensor(o, o, ss[:, n:n + 1], norm_w[:, :], ALU.mult, ALU.mult)
            chain(last)
            dve.wait_ge(S["gated"], 1)
            dve.tensor_tensor(mix[:, :, 512:1024], mix[:, :, 512:1024], gate[:, :, :], ALU.mult)


class TurnColumns:

    def __init__(self, s, rows, hi, lo, ident, bank, name="t_"):
        self.rows, self.hi, self.lo, self.ident, self.bank = rows, hi, lo, ident, bank
        self.tiles = rows.shape[2] // P
        self.turned, self.hi_done, self.done = s.sem(name + "turned"), s.sem(name + "hi"), s.sem(name + "done")

    def on_tensor(self, pe):
        for k in range(self.tiles):
            for t in range(NT):
                last = pe.transpose(self.bank[:, k, t * P:(t + 1) * P], self.rows[:, t, k * P:(k + 1) * P],
                                    self.ident)
            last.then_inc(self.turned, 1)

    def on_scalar(self, act):
        for k in range(self.tiles):
            act.wait_ge(self.turned, k + 1)
            act.activation(self.hi[:, k, :], self.bank[:, k, :], ACT.Copy).then_inc(self.hi_done, 1)

    def on_vector(self, dve):
        for k in range(self.tiles):
            dve.wait_ge(self.hi_done, k + 1)
            dve.tensor_tensor(self.lo[:, k, :], self.bank[:, k, :], self.hi[:, k, :].bitcast(F32), ALU.subtract)\
                .then_inc(self.done, 1)


PEER_H, PEER_KEYS, PEER_K = 8, 128, 16
HP = 2 * PEER_H



def phase_mix_out(nc, bank, const, io, life):
    with ExitStack() as ctx:
        s = Scope(nc, ctx, "mo")
        mix, h = life["mix"], life["h"]
        xh, xl = s.sb("xh", [P, KD, T], F32R), s.sb("xl", [P, KD, T], F32R)
        x_in = s.sb("x_in", [P, NT, D])
        ring = WeightRing(s)
        gemm = Gemm(s, ring, bank)
        x_landed, stored, done = s.sem("x_landed"), s.sem("stored"), s.sem("h_done")
        ident = const[:, CONSTS["ident"][0]:CONSTS["ident"][1]]
        turn = TurnColumns(s, mix, xh, xl, ident, bank)

        def part(c0):
            return dict(kind="rows", slab=lambda i, _: weight_slab(io["w_out"], i, c0), width=BANK, ktiles=KD,
                        x=lambda kt, m: (xh[:, kt, m * P:(m + 1) * P], xl[:, kt, m * P:(m + 1) * P]),
                        meta=False, c0=c0)

        blocks = gemm.plan([part(0), part(BANK)])
        block = s.block()

        @block.sync
        def _(sp):
            sp.dma_start(x_in[:, :, :], io["x"].rearrange("(t p) d -> p t d", p=P)).then_inc(x_landed, 16)
            for b in blocks:
                gemm.on_sync(sp, b)
            sp.wait_ge(done, 1)
            sp.dma_start(io["h1"].rearrange("(t p) d -> p t d", p=P), h[:, :, :]).then_inc(stored, 16)
            sp.wait_ge(stored, 16)

        @block.gpsimd
        def _(pool):
            ring.open_raw(pool)
            for b in blocks:
                gemm.on_gpsimd(pool, b)

        @block.scalar
        def _(act):
            turn.on_scalar(act)
            for b in blocks:
                gemm.on_scalar(act, b)

        @block.tensor
        def _(pe):
            ring.open_slots(pe)
            turn.on_tensor(pe)
            pe.wait_ge(turn.done, KD)
            for b in blocks:
                gemm.on_tensor(pe, b)

        @block.vector
        def _(dve):
            gemm.open_banks(dve)
            turn.on_vector(dve)
            dve.wait_ge(x_landed, 16)
            for b in blocks:
                gemm.take(dve, b, lambda j, m, got: dve.tensor_tensor(
                    h[:, m, b["c0"]:b["c0"] + BANK], got, x_in[:, m, b["c0"]:b["c0"] + BANK], ALU.add))
            dve.wait_ge(gemm.bank_free, NBANK + gemm.tile0)
            dve.sem_inc(done, 1)



def phase_peer_query(nc, bank, const, io, life):
    with ExitStack() as ctx:
        s = Scope(nc, ctx, "pq")
        h, sc = life["h"], life["scores"]
        xh, xl = s.sb("xh", [P, KD, T], F32R), s.sb("xl", [P, KD, T], F32R)
        gain = s.sb("gain", [P, KD])
        keys = s.sb("keys", [P, HP, PEER_KEYS])
        qT = s.sb("qT", [P, HP, T])
        ring = WeightRing(s)
        gemm = Gemm(s, ring, bank)
        landed, stored, vec = s.sem("landed"), s.sem("stored"), s.sem("vector_steps")
        scored, score_taken = s.sem("scored"), s.sem("score_taken")
        ident = const[:, CONSTS["ident"][0]:CONSTS["ident"][1]]
        norm = NormColumns(s, h, None, gain, xh, xl, ident, bank)

        def part(b):
            return dict(kind="columns", width=BANK, ktiles=KD, meta=False, b=b,
                        slab=lambda i, turn: weight_slab(io["peer_w_q"], i, turn * 2 * BANK + b * BANK),
                        x=lambda kt, m: (xh[:, kt, :], xl[:, kt, :]))

        TURNS = HP * P // (2 * BANK)
        blocks = gemm.plan([part(0), part(1)], TURNS)
        block = s.block()

        @block.sync
        def _(sp):
            sp.dma_start(gain[:, :], io["ln2_w"]).then_inc(landed, 16)
            sp.dma_start(keys[:, :, :], io["peer_keys"]).then_inc(landed, 16)
            with sp.Fori(0, TURNS) as turn:
                for b in blocks:
                    gemm.on_sync(sp, b, turn)
            sp.wait_ge(norm.done, norm.total())
            sp.dma_start(io["hn_hi"], xh[:, :, :].bitcast(F32)).then_inc(stored, 16)
            sp.dma_start(io["hn_lo"], xl[:, :, :].bitcast(F32)).then_inc(stored, 16)
            sp.wait_ge(stored, 32)

        @block.gpsimd
        def _(pool):
            ring.open_raw(pool)
            with pool.Fori(0, TURNS) as turn:
                for b in blocks:
                    gemm.on_gpsimd(pool, b, turn)

        @block.scalar
        def _(act):
            act.wait_ge(landed, 32)
            norm.on_scalar(act, lambda e, t: None)
            with act.Fori(0, TURNS) as turn:
                for b in blocks:
                    gemm.on_scalar(act, b, turn)

        @block.tensor
        def _(pe):
            ring.open_slots(pe)
            norm.on_tensor(pe)
            pe.wait_ge(norm.done, norm.total())
            with pe.Fori(0, TURNS) as turn:
                for b in blocks:
                    gemm.on_tensor(pe, b, turn)
            pe.wait_ge(gemm.bank_free, NBANK + gemm.tile0)
            for t in range(NT):
                for g in range(4):
                    n = 4 * t + g
                    if n >= NBANK:
                        pe.wait_ge(score_taken, n + 1 - NBANK)
                    for i in range(4):
                        hp = 4 * g + i
                        last = pe.matmul(bank[:, n % NBANK, i * P:(i + 1) * P], qT[:, hp, t * P:(t + 1) * P],
                                         keys[:, hp, :], start=True, stop=True)
                    last.then_inc(scored, 1)

        @block.vector
        def _(dve):
            chain = Chain(dve, vec)
            gemm.open_banks(dve)
            dve.wait_ge(landed, 32)
            norm.on_vector(dve, chain)
            with dve.Fori(0, TURNS) as turn:
                for b in blocks:
                    gemm.take(dve, b, lambda j, m, got: dve.tensor_copy(
                        qT[:, bass.ds(turn * 8 + b["b"] * 4 + m, 1), :].rearrange("p a t -> p (a t)"), got), turn)
            for n in range(4 * NT):
                dve.wait_ge(scored, n + 1)
                dve.tensor_copy(sc[:, n // 4, 4 * (n % 4):4 * (n % 4) + 4, :].rearrange("p a k -> p (a k)"),
                                bank[:, n % NBANK, :]).then_inc(score_taken, 1)



def phase_peer_select(nc, bank, const, io, life):
    with ExitStack() as ctx:
        s = Scope(nc, ctx, "ps")
        sc = life["scores"]
        K, H = PEER_K, PEER_H
        ts, ti = s.sb("ts", [P, HP, K]), s.sb("ti", [P, HP, K], U32)
        tif = s.sb("tif", [P, HP, K])
        cand = s.sb("cand", [P, H, K, K])
        bs, bp = s.sb("bs", [P, H, K]), s.sb("bp", [P, H, K], U32)
        place = s.sb("place", [P, 2, H, K], U32)
        placef = s.sb("placef", [P, 2, H, K])
        hot = s.sb("hot", [P, 2, H, K, K])
        tsum = s.sb("tsum", [P, H])
        pick = s.sb("pick", [P, NT, 3, P])
        V = s.sem("vector_steps")
        shifted, exped, picked, turned = s.sem("shifted"), s.sem("exped"), s.sem("picked"), s.sem("turned")
        ident = const[:, CONSTS["ident"][0]:CONSTS["ident"][1]]
        iota = const[:, CONSTS["iota"][0]:CONSTS["iota"][0] + K]
        block = s.block()

        @block.scalar
        def _(act):
            for t in range(NT):
                act.wait_ge(shifted, t + 1)
                act.activation(bs[:, :, :], bs[:, :, :], ACT.Exp).then_inc(exped, 1)

        @block.tensor
        def _(pe):
            for t in range(NT):
                pe.wait_ge(picked, t + 1)
                for j in range(3):
                    last = pe.transpose(bank[:, j, t * P:(t + 1) * P], pick[:, t, j, :], ident)
            last.then_inc(turned, 1)

        @block.vector
        def _(dve):
            chain = Chain(dve, V)

            def best_16(groups, values, scores, index):
                for half in (slice(0, 8), slice(8, K)):
                    for g in range(groups):
                        last = dve.max(scores(g)[:, half], values(g))
                    chain(last)
                    for g in range(groups):
                        last = dve.max_index(index(g)[:, half], scores(g)[:, half], values(g))
                    chain(last)
                    if half.start == 0:
                        for g in range(groups):
                            last = dve.match_replace(values(g), scores(g)[:, half], values(g), NEG)
                        chain(last)

            for t in range(NT):
                best_16(HP, lambda g: sc[:, t, g, :], lambda g: ts[:, g, :], lambda g: ti[:, g, :])
                dve.tensor_copy(tif[:, :, :], ti[:, :, :])
                pair = ts[:, :, :].rearrange("p (h two) k -> p h two k", two=2)
                chain(dve.tensor_tensor(cand[:, :, :, :], pair[:, :, 0, :].unsqueeze(3).to_broadcast([P, H, K, K]),
                                        pair[:, :, 1, :].unsqueeze(2).to_broadcast([P, H, K, K]), ALU.add))
                best_16(H, lambda g: cand[:, g, :, :].rearrange("p a b -> p (a b)"), lambda g: bs[:, g, :],
                        lambda g: bp[:, g, :])
                chain(dve.tensor_copy(tsum[:, :], bs[:, :, 0]))
                dve.tensor_tensor(bs[:, :, :], bs[:, :, :], tsum[:, :].unsqueeze(2).to_broadcast([P, H, K]),
                                  ALU.subtract).then_inc(shifted, 1)
                dve.tensor_single_scalar(place[:, 0, :, :], bp[:, :, :], 4, ALU.logical_shift_right)
                chain(dve.tensor_single_scalar(place[:, 1, :, :], bp[:, :, :], K - 1, ALU.bitwise_and))
                chain(dve.tensor_copy(placef[:, :, :, :], place[:, :, :, :]))
                keys = tif[:, :, :].rearrange("p (h two) k -> p h two k", two=2)
                for j in range(2):
                    last = dve.tensor_tensor(
                        hot[:, j, :, :, :].rearrange("p h r k -> p (h r) k"),
                        iota.unsqueeze(1).to_broadcast([P, H * K, K]),
                        placef[:, j, :, :].rearrange("p h r -> p (h r)").unsqueeze(2).to_broadcast([P, H * K, K]),
                        ALU.is_equal)
                chain(last)
                for j in range(2):
                    last = dve.tensor_tensor(hot[:, j, :, :, :], hot[:, j, :, :, :],
                                             keys[:, :, j, :].unsqueeze(2).to_broadcast([P, H, K, K]), ALU.mult)
                chain(last)
                for j in range(2):
                    dve.tensor_reduce(pick[:, t, j, :].rearrange("p (h r) -> p h r", h=H), hot[:, j, :, :, :],
                                      AX.X, ALU.add)
                dve.wait_ge(exped, t + 1)
                chain(dve.tensor_reduce(tsum[:, :], bs[:, :, :], AX.X, ALU.add))
                chain(dve.reciprocal(tsum[:, :], tsum[:, :]))
                dve.tensor_tensor(pick[:, t, 2, :].rearrange("p (h r) -> p h r", h=H), bs[:, :, :],
                                  tsum[:, :].unsqueeze(2).to_broadcast([P, H, K]), ALU.mult).then_inc(picked, 1)
                dve.wait_ge(picked, t + 1)
            dve.wait_ge(turned, 1)
            dve.tensor_copy(life["pick_keys"][:, :, :], bank[:, 0:2, :])
            left, parts = hot[:, 0, :, :, :].rearrange("p h r k -> p (h r k)")[:, 0:T], life["pick_gates"]
            chain(dve.tensor_copy(left, bank[:, 2, :]))
            for n in range(3):
                chain(dve.tensor_copy(parts[:, :, n], left))
                if n < 2:
                    chain(dve.tensor_tensor(left, left, parts[:, :, n], ALU.subtract))



SWEEPS = 2
ST = T // SWEEPS
ROUND = 32
ROUNDS = PEER_KEYS // ROUND
GROUP = ST // ROUND
RAW = 4
PARTS = 3


def phase_peer_experts(nc, bank, io, life):
    with ExitStack() as ctx:
        s = Scope(nc, ctx, "pe")
        keys, parts = life["pick_keys"], life["pick_gates"]
        iota = s.sb("iota", [P, P])
        counting = s.sb("counting", [P, P], BF16)
        zero = s.sb("zero", [P, P], F32R)
        gates = [s.sb(f"gates{k}", [P, ROUND, ST]) for k in range(2)]
        xh, xl = s.sb("xh", [P, KD, T], F32R), s.sb("xl", [P, KD, T], F32R)
        u_raw, v_raw = s.sb("u_raw", [P, RAW, KD, P]), s.sb("v_raw", [P, RAW, D])
        uh, ul = s.sb("uh", [P, 2, KD, P], F32R), s.sb("ul", [P, 2, KD, P], F32R)
        vh, vl = s.sb("vh", [P, 2, D], F32R), s.sb("vl", [P, 2, D], F32R)
        hid = s.sb("hid", [P, 2, ST])
        hh, hl = s.sb("hh", [P, 2, ST], F32R), s.sb("hl", [P, 2, ST], F32R)
        eq1 = s.sb("eq1", [P, GROUP, ROUND], BF16)
        hot1 = s.sb("hot1", [P, 2, GROUP, PARTS, ROUND], BF16)
        hot2 = s.sb("hot2", [P, 2, GROUP, P], BF16)
        out = s.sb("out", [P, 4, BANK])
        names = ("iota_landed", "x_landed", "u_hi", "u_lo", "v_hi", "v_lo", "a_done", "a_taken", "hid_ready",
                 "h_hi", "h_lo", "v_done", "hot_ready", "hot_read", "gates_taken", "zeroed", "out_done",
                 "out_taken", "out_stored", "vector_steps")
        S = {n: s.sem(n) for n in names}
        u_landed = [s.sem(f"u_landed{k}") for k in range(RAW)]
        v_landed = [s.sem(f"v_landed{k}") for k in range(RAW)]
        A_BANK, G_BANK = 4, 6
        N = SWEEPS * PEER_KEYS
        block = s.block()


        def rounds(eng, body, at_round=None, at_sweep=None):
            for r in range(SWEEPS * ROUNDS):
                if at_round:
                    at_round(r)
                peel = r % ROUNDS == ROUNDS - 1
                turns = ROUND // RAW - peel
                with eng.Fori(0, turns) as i:
                    for c in range(RAW):
                        body(r, r * ROUND + c, i, c)
                if peel:
                    for c in range(RAW):
                        body(r, r * ROUND + turns * RAW + c, None, c)
                    if at_sweep:
                        at_sweep(r // ROUNDS)

        def at(n, i):
            return n if i is None else i * RAW + n

        def spread_here(r):
            return r < SWEEPS * ROUNDS - 1

        @block.sync
        def _(sp):
            sp.dma_start(iota[:, :], io["const"][:, CONSTS["iota"][0]:CONSTS["iota"][1]])\
                .then_inc(S["iota_landed"], 16)
            sp.dma_start(xh[:, :, :].bitcast(F32), io["hn_hi"]).then_inc(S["x_landed"], 16)
            sp.dma_start(xl[:, :, :].bitcast(F32), io["hn_lo"]).then_inc(S["x_landed"], 16)
            for sweep in range(SWEEPS):
                with sp.Fori(0, PEER_KEYS // RAW) as i:
                    for c in range(RAW):
                        q = at(sweep * PEER_KEYS + c, i)
                        sp.wait_ge(S["u_lo"], q + 1)
                        sp.dma_start(u_raw[:, c, :, :].rearrange("p k j -> p (k j)"),
                                     io["peer_u"][bass.ds(RAW * i + c, 1), :, :].rearrange("a p n -> p (a n)"))\
                            .then_inc(u_landed[c], 16)
                        sp.wait_ge(S["v_lo"], q + 1)
                        sp.dma_start(v_raw[:, c, :],
                                     io["peer_v"][bass.ds(RAW * i + c, 1), :, :].rearrange("a p n -> p (a n)"))\
                            .then_inc(v_landed[c], 16)

        @block.scalar
        def _(act):
            def split_u(n, i):
                turn = n // RAW if i is None else i + n // RAW
                act.wait_ge(u_landed[n % RAW], 16 * turn + 16)
                act.wait_ge(S["a_done"], at(n, i) + 1)
                act.activation(uh[:, n % 2, :, :], u_raw[:, n % RAW, :, :], ACT.Copy).then_inc(S["u_hi"], 1)

            def split_v(n, i):
                turn = n // RAW if i is None else i + n // RAW
                act.wait_ge(v_landed[n % RAW], 16 * turn + 16)
                act.wait_ge(S["v_done"], at(n, i) + 1)
                act.activation(vh[:, n % 2, :], v_raw[:, n % RAW, :], ACT.Copy).then_inc(S["v_hi"], 1)

            def take_gates(r, g, n0, k):
                act.wait_ge(S["hot_read"], g + 3)
                act.activation(gates[r % 2][:, :, bass.ds(n0, GROUP)].rearrange("p i n -> p n i"),
                               bank[:, G_BANK + k, 0:GROUP * ROUND].rearrange("p (n i) -> p n i", n=GROUP),
                               ACT.Copy).then_inc(S["gates_taken"], 1)

            act.sem_inc(S["a_taken"], 2)
            act.sem_inc(S["gates_taken"], 2)
            split_u(0, None)
            split_u(1, None)
            split_v(0, None)
            with act.Fori(0, ROUND // 2) as i:
                for k in range(2):
                    take_gates(0, 2 * i + k, (2 * i + k) * GROUP, k)

            def at_round(r):
                if r:
                    act.wait_ge(S["hid_ready"], r * ROUND)

            def body(r, n, i, c):
                q, k = at(n, i), c % 2
                act.wait_ge(S["a_done"], q + 3)
                act.wait_ge(S["h_lo"], q + 1)
                act.activation(hid[:, k, :], bank[:, A_BANK + k, 0:ST], ACT.Gelu).then_inc(S["a_taken"], 1)
                if i is not None or n + 2 < N:
                    split_u(n + 2, i)
                act.wait_ge(S["hid_ready"], q + 1)
                act.wait_ge(S["v_done"], q + 1)
                act.activation(hh[:, k, :], hid[:, k, :], ACT.Copy).then_inc(S["h_hi"], 1)
                if spread_here(r):
                    take_gates(r + 1, q + ROUND, (q - r * ROUND) * GROUP, k)
                if i is not None or n + 1 < N:
                    split_v(n + 1, i)

            rounds(act, body, at_round)

        @block.gpsimd
        def _(pool):
            pool.sem_inc(S["v_lo"], RAW)
            for sweep in range(SWEEPS):
                with pool.Fori(0, PEER_KEYS // RAW) as i:
                    for c in range(RAW):
                        pool.wait_ge(S["v_hi"], at(sweep * PEER_KEYS + c, i) + 1)
                        pool.tensor_tensor(vl[:, c % 2, :], v_raw[:, c, :], vh[:, c % 2, :].bitcast(F32),
                                           ALU.subtract).then_inc(S["v_lo"], 1)
                for m in range(2):
                    pool.wait_ge(S["out_taken"], 2 * sweep + m + 1)
                    pool.dma_start(io["experts"][(2 * sweep + m) * P:(2 * sweep + m + 1) * P, :]
                                   .rearrange("p (c n) -> p c n", c=2), out[:, 2 * m:2 * m + 2, :])\
                        .then_inc(S["out_stored"], 16)
            pool.wait_ge(S["out_stored"], 16 * 2 * SWEEPS)

        @block.vector
        def _(dve):
            dve.sem_inc(S["u_lo"], RAW)
            dve.sem_inc(S["h_lo"], 2)
            dve.memset(zero[:, :].bitcast(F32), 0.0).then_inc(S["zeroed"], 1)
            dve.wait_ge(S["iota_landed"], 16)
            dve.tensor_copy(counting[:, :], iota[:, :]).then_inc(S["vector_steps"], 1)
            dve.wait_ge(S["vector_steps"], 1)

            def one_hots(r, g, n0, k):
                n = bass.ds(n0, GROUP)
                first = (r % ROUNDS) * ROUND
                dve.wait_ge(S["hot_read"], g + 1)
                dve.tensor_tensor(eq1[:, :, :], counting[:, first:first + ROUND].unsqueeze(1)
                                  .to_broadcast([P, GROUP, ROUND]),
                                  keys[:, 0, n].unsqueeze(2).to_broadcast([P, GROUP, ROUND]), ALU.is_equal)\
                    .then_inc(S["vector_steps"], 1)
                dve.tensor_tensor(hot2[:, k, :, :], counting[:, :].unsqueeze(1).to_broadcast([P, GROUP, P]),
                                  keys[:, 1, n].unsqueeze(2).to_broadcast([P, GROUP, P]), ALU.is_equal)
                dve.wait_ge(S["vector_steps"], g + 2)
                dve.tensor_tensor(hot1[:, k, :, :, :],
                                  eq1[:, :, :].unsqueeze(2).to_broadcast([P, GROUP, PARTS, ROUND]),
                                  parts[:, n, :].unsqueeze(3).to_broadcast([P, GROUP, PARTS, ROUND]), ALU.mult)\
                    .then_inc(S["hot_ready"], 1)
                dve.wait_ge(S["hot_ready"], g + 1)

            def split_u(n, i):
                dve.wait_ge(S["u_hi"], at(n, i) + 1)
                dve.tensor_tensor(ul[:, n % 2, :, :], u_raw[:, n % RAW, :, :], uh[:, n % 2, :, :].bitcast(F32),
                                  ALU.subtract).then_inc(S["u_lo"], 1)

            split_u(0, None)
            split_u(1, None)
            with dve.Fori(0, ROUND // 2) as i:
                for k in range(2):
                    one_hots(0, 2 * i + k, (2 * i + k) * GROUP, k)

            def at_round(r):
                dve.wait_ge(S["gates_taken"], (r + 1) * ROUND + 2)

            def body(r, n, i, c):
                q, k = at(n, i), c % 2
                dve.wait_ge(S["a_taken"], q + 3)
                g = gates[r % 2][:, bass.ds(q - r * ROUND, 1), :].rearrange("p a n -> p (a n)")
                dve.tensor_tensor(hid[:, k, :], hid[:, k, :], g, ALU.mult).then_inc(S["hid_ready"], 1)
                if spread_here(r):
                    one_hots(r + 1, q + ROUND, (q - r * ROUND) * GROUP + (r + 1) // ROUNDS * ST, k)
                dve.wait_ge(S["h_hi"], q + 1)
                dve.tensor_tensor(hl[:, k, :], hid[:, k, :], hh[:, k, :].bitcast(F32), ALU.subtract)\
                    .then_inc(S["h_lo"], 1)
                if i is not None or n + 2 < N:
                    split_u(n + 2, i)

            def at_sweep(sweep):
                dve.wait_ge(S["out_done"], sweep + 1)
                for m in range(2):
                    if sweep:
                        dve.wait_ge(S["out_stored"], 16 * 2 * sweep)
                    dve.tensor_copy(out[:, 2 * m:2 * m + 2, :], bank[:, 2 * m:2 * m + 2, :])\
                        .then_inc(S["out_taken"], 1)

            rounds(dve, body, at_round, at_sweep)

        @block.tensor
        def _(pe):
            pe.sem_inc(S["a_done"], 2)
            pe.sem_inc(S["v_done"], 2)
            pe.sem_inc(S["hot_read"], 2)

            def spread_gates(g, k):
                pe.wait_ge(S["hot_ready"], g + 1)
                pe.wait_ge(S["gates_taken"], g + 1)
                for j in range(GROUP):
                    for p in range(PARTS):
                        last = pe.matmul(bank[:, G_BANK + k, j * ROUND:(j + 1) * ROUND], hot2[:, k, j, :],
                                         hot1[:, k, j, p, :], start=p == 0, stop=p == PARTS - 1)
                last.then_inc(S["hot_read"], 1)

            def scores(q, k, sweep):
                pe.wait_ge(S["u_lo"], q + RAW + 1)
                pe.wait_ge(S["a_taken"], q + 1)
                t = slice(sweep * ST, (sweep + 1) * ST)
                for kt in range(KD):
                    last = split_products(pe, bank[:, A_BANK + k, 0:ST], (uh[:, k, kt, :], ul[:, k, kt, :]),
                                          (xh[:, kt, t], xl[:, kt, t]), kt == 0, kt == KD - 1)
                last.then_inc(S["a_done"], 1)

            def values(q, k):
                pe.wait_ge(S["h_lo"], q + 3)
                pe.wait_ge(S["v_lo"], q + RAW + 1)
                for m in range(2):
                    for c in range(2):
                        t, d = slice(m * P, (m + 1) * P), slice(c * BANK, (c + 1) * BANK)
                        last = split_products(pe, bank[:, 2 * m + c, :], (hh[:, k, t], hl[:, k, t]),
                                              (vh[:, k, d], vl[:, k, d]), False, False, True)
                last.then_inc(S["v_done"], 1)

            def zero_products(start):
                for b in range(4):
                    for c in range(BANK // P):
                        last = pe.matmul(bank[:, b, c * P:(c + 1) * P], zero[:, :], zero[:, :],
                                         start=start and c == 0, stop=not start, skip_group_check=True)
                return last

            pe.wait_ge(S["zeroed"], 1)
            pe.wait_ge(S["x_landed"], 32)
            zero_products(True)
            scores(0, 0, 0)
            with pe.Fori(0, ROUND // 2) as i:
                for k in range(2):
                    spread_gates(2 * i + k, k)

            def body(r, n, i, c):
                q, k = at(n, i), c % 2
                if i is not None or n + 1 < N:
                    last_of_sweep = i is None and (n + 1) % PEER_KEYS == 0
                    scores(q + 1, 1 - k, r // ROUNDS + last_of_sweep)
                if spread_here(r):
                    spread_gates(q + ROUND, k)
                values(q, k)

            def at_sweep(sweep):
                zero_products(False).then_inc(S["out_done"], 1)
                if sweep + 1 < SWEEPS:
                    pe.wait_ge(S["out_taken"], 2 * (sweep + 1))
                    zero_products(True)

            rounds(pe, body, None, at_sweep)



POOL_GROUPS, POOL_D = 4, 512
AH, LAT = 8, 128
IDX_H, IDX_D = 8, 32
INDEX_SCALE = (IDX_H ** -0.5) * (IDX_D ** -0.5)
ATTN_SCALE = LAT ** -0.5
TOP = min(256, T // 4)
FF = 2816
KF = FF // P


def seen(t):
    return META + (t + 1) * P


def phase_project_2(nc, bank, const, io, life):
    with ExitStack() as ctx:
        s = Scope(nc, ctx, "p2")
        xh, xl = life["xh"], life["xl"]
        bias = life["bias"]
        h = life["h_rows"]
        hm = s.sb("h_meta", [META, D])
        gain, gain_row = s.sb("gain", [P, KD]), s.sb("gain_row", [P, D])
        add = s.sb("add", [P, D])
        kv_g = s.sb("kv_g", [P, LAT])
        qi = s.sb("qi", [P, 2, T])
        ki = s.sb("ki", [P, TM])
        wi = s.sb("wi", [P, NT, IDX_H])
        rel = s.sb("rel", [P, 2, TM])
        score = s.sb("score", [P, NT, TM])
        best = s.sb("best", [P, 8])
        c, cm, cT = life["c"], life["c_m"], life["cT"]
        ring = WeightRing(s)
        early = Gemm(s, ring, bank, "early_")
        late = Gemm(s, ring, bank, "late_")
        g_landed, stored = s.sem("gains_landed"), s.sem("stored")
        h_landed, e_landed = s.sem("h_landed"), [s.sem(f"e_landed{k}") for k in range(1)]
        added, y_done, vec = s.sem("added"), s.sem("y_done"), s.sem("vector_steps")
        scored, relued, summed = s.sem("scored"), s.sem("relued"), s.sem("summed")
        c_done, c_turned, c_taken = s.sem("c_done"), s.sem("c_turned"), s.sem("c_taken")
        ident = const[:, CONSTS["ident"][0]:CONSTS["ident"][1]]
        causal = const[:, CONSTS["causal"][0]:CONSTS["causal"][1]]
        causal_fill = const[:, CONSTS["causal_fill"][0]:CONSTS["causal_fill"][1]]
        out_stats = RowStats(s, h, None, "o_")
        norm = NormColumns(s, h, hm, gain, xh, xl, ident, bank, life["xs"], out_stats.junk)
        c_stats = RowStats(s, c, cm, "c_")

        def rows(kt, m):
            cc = slice(META + m * P, META + (m + 1) * P) if m >= 0 else slice(0, P)
            return xh[:, kt, cc], xl[:, kt, cc]

        def columns(kt, m):
            cc = slice(META, TM) if m >= 0 else slice(0, META)
            return xh[:, kt, cc], xl[:, kt, cc]

        def part(kind, w, c0, width, meta, dst=None, first=0):
            return dict(kind=kind, slab=lambda i, turn: weight_slab(w, i, c0, width), width=width, ktiles=KD,
                        x=rows if kind == "rows" else columns, meta=meta, dst=dst, first=first)

        b_index, b_lat = early.plan([part("columns", io["w_index"], 0, 3 * P, True),
                                     part("rows", io["w_latent"], 0, LAT + IDX_H, True)])
        late.slab0 = early.slab0
        w = io["w_in_2"]
        c_conv = 1960
        blocks = late.plan([
            part("columns", w, 0, BANK, True, life["u"]), part("columns", w, 512, BANK, False, life["q2"], 0),
            part("columns", w, 1024, BANK, False, life["q2"], 4), part("columns", w, c_conv, BANK, False, life["cb"]),
            part("columns", w, c_conv + 512, BANK, True, life["cc"]),
            part("columns", w, c_conv + 1024, BANK, True, life["cu"])])
        units = [(t, hd) for t in range(NT) for hd in range(IDX_H)]
        block = s.block()

        @block.sync
        def _(sp):
            sp.dma_start(const[:, :], io["const"][:, 0:CONST_2_W]).then_inc(g_landed, 16)
            sp.dma_start(gain[:, :], io["norm1_g"]).then_inc(g_landed, 16)
            sp.dma_start(gain_row[:, :], io["final_norm_w"].to_broadcast([P, D])).then_inc(g_landed, 16)
            sp.dma_start(kv_g[:, :], io["kv_norm_g"].to_broadcast([P, LAT])).then_inc(g_landed, 16)
            sp.dma_start(hm[:, :], io["meta_2"]).then_inc(g_landed, 16)
            sp.dma_start(h[:, :, :], io["h1"].rearrange("(t p) d -> p t d", p=P)).then_inc(h_landed, 16)
            for t in range(NT):
                if t:
                    sp.wait_ge(added, t)
                sp.dma_start(add[:, :], io["experts"][t * P:(t + 1) * P, :]).then_inc(e_landed[0], 16)
            for b in (b_index, b_lat):
                early.on_sync(sp, b)
            sp.wait_ge(y_done, 1)
            sp.dma_start(io["x2"].rearrange("(t p) d -> p t d", p=P), h[:, :, :]).then_inc(stored, 16)
            for b in blocks:
                late.on_sync(sp, b)
            sp.wait_ge(stored, 16)

        @block.gpsimd
        def _(pool):
            ring.open_raw(pool)
            for b in (b_index, b_lat):
                early.on_gpsimd(pool, b)
            for b in blocks:
                late.on_gpsimd(pool, b)

        @block.scalar
        def _(act):
            late.open_banks(act)
            act.wait_ge(g_landed, 16 * 5)
            act.wait_ge(h_landed, 16)
            out_stats.on_scalar(act, lambda e, t: e.wait_ge(added, t + 1))
            norm.on_scalar(act, lambda e, t: e.wait_ge(y_done, 1))
            for b in (b_index, b_lat):
                early.on_scalar(act, b)
            c_stats.on_scalar(act, lambda e, t: e.wait_ge(early.bank_free, NBANK + early.tile0))
            for n, (t, hd) in enumerate(units):
                act.wait_ge(scored, n + 1)
                if n >= 2:
                    act.wait_ge(summed, n - 1)
                pair = bank[:, 2 * (n % 4):2 * (n % 4) + 2, :].rearrange("p b n -> p (b n)")
                act.activation(rel[:, n % 2, 0:seen(t)], pair[:, 0:seen(t)], ACT.Relu).then_inc(relued, 1)
            act.wait_ge(c_turned, 1)
            act.activation(cT[:, META:TM], bank[:, 0, :], ACT.Copy)
            act.activation(cT[:, 0:META], bank[:, 1, 0:META], ACT.Copy).then_inc(c_taken, 1)

            def use(b):
                def one(j, m, got):
                    if m >= 0:
                        off = META if b["meta"] else 0
                        return act.activation(b["dst"][:, b["first"] + m, off:off + T], got, ACT.Copy)
                    return act.activation(b["dst"][:, :, 0:META],
                                          got[:, 0:4 * META].rearrange("p (m c) -> p m c", m=4), ACT.Copy)
                return one

            late.on_scalar(act, blocks[0])
            for n, b in enumerate(blocks):
                if n + 1 < len(blocks):
                    late.on_scalar(act, blocks[n + 1], 0, AHEAD)
                if b["dst"] is life["cb"]:
                    act.wait_ge(stored, 16)
                late.take(act, b, use(b))
                if n + 1 < len(blocks):
                    late.on_scalar(act, blocks[n + 1], 0, REST)

        @block.tensor
        def _(pe):
            ring.open_slots(pe)
            pe.wait_ge(g_landed, 16 * 5)
            norm.on_tensor(pe)
            pe.wait_ge(norm.done, norm.total())
            for b in (b_index, b_lat):
                early.on_tensor(pe, b)
            pe.wait_ge(early.bank_free, NBANK + early.tile0)
            for n, (t, hd) in enumerate(units):
                if n >= 4:
                    pe.wait_ge(relued, n - 3)
                r = slice((hd % 4) * IDX_D, (hd % 4 + 1) * IDX_D)
                lhs = qi[r, hd // 4, t * P:(t + 1) * P]
                b0, w0 = 2 * (n % 4), min(seen(t), BANK)
                last = pe.matmul(bank[:, b0, 0:w0], lhs, ki[r, 0:w0], start=True, stop=True)
                if seen(t) > BANK:
                    last = pe.matmul(bank[:, b0 + 1, 0:seen(t) - BANK], lhs, ki[r, BANK:seen(t)],
                                     start=True, stop=True)
                last.then_inc(scored, 1)
            pe.wait_ge(relued, len(units))
            pe.wait_ge(c_done, 1)
            for t in range(NT):
                pe.transpose(bank[:, 0, t * P:(t + 1) * P], c[:, t, :], ident)
            pe.transpose(bank[:, 1, 0:META], cm[:, :], ident[0:META, 0:META]).then_inc(c_turned, 1)
            pe.wait_ge(c_taken, 1)
            for b in blocks:
                late.on_tensor(pe, b)

        @block.vector
        def _(dve):
            chain = Chain(dve, vec)
            early.open_banks(dve)
            dve.wait_ge(g_landed, 16 * 5)
            dve.wait_ge(h_landed, 16)
            for t in range(NT):
                dve.wait_ge(e_landed[0], 16 * (t + 1))
                dve.tensor_tensor(h[:, t, :], h[:, t, :], add[:, :], ALU.add).then_inc(added, 1)
            out_stats.on_vector(dve, chain)
            for t in range(NT):
                last = dve.scalar_tensor_tensor(h[:, t, :], h[:, t, :], out_stats.rstd[:, t:t + 1],
                                                gain_row[:, :], ALU.mult, ALU.mult)
            last.then_inc(y_done, 1)
            dve.wait_ge(y_done, 1)
            norm.on_vector(dve, chain)

            def use_index(j, m, got):
                if m < 0:
                    return dve.tensor_copy(ki[:, 0:META], got[:, 2 * META:3 * META])
                return dve.tensor_copy(qi[:, m, :] if m < 2 else ki[:, META:TM], got)

            def use_latent(j, m, got):
                if m < 0:
                    return dve.tensor_copy(cm[:, :], got[0:META, 0:LAT])
                dve.tensor_scalar(wi[:, m, :], got[:, LAT:LAT + IDX_H], INDEX_SCALE, None, ALU.mult)
                return dve.tensor_copy(c[:, m, :], got[:, 0:LAT])

            early.take(dve, b_index, use_index)
            early.take(dve, b_lat, use_latent)
            dve.wait_ge(early.bank_free, NBANK + early.tile0)
            c_stats.on_vector(dve, chain)
            for t in range(NT):
                dve.scalar_tensor_tensor(c[:, t, :], c[:, t, :], c_stats.rstd[:, t:t + 1], kv_g[:, :],
                                         ALU.mult, ALU.mult)
            dve.scalar_tensor_tensor(cm[:, :], cm[:, :], c_stats.rstd[0:META, NT:NT + 1], kv_g[0:META, :],
                                     ALU.mult, ALU.mult).then_inc(c_done, 1)
            for n, (t, hd) in enumerate(units):
                dve.wait_ge(relued, n + 1)
                got, acc = rel[:, n % 2, 0:seen(t)], score[:, t, 0:seen(t)]
                if hd == 0:
                    last = dve.tensor_scalar(acc, got, wi[:, t, 0:1], None, ALU.mult)
                else:
                    dve.wait_ge(summed, n)
                    last = dve.scalar_tensor_tensor(acc, got, wi[:, t, hd:hd + 1], acc, ALU.mult, ALU.add)
                last.then_inc(summed, 1)
            dve.wait_ge(summed, len(units))
            for t in range(NT):
                own = score[:, t, META + t * P:seen(t)]
                chain(dve.tensor_tensor(own, own, causal, ALU.mult))
                last = dve.tensor_tensor(own, own, causal_fill, ALU.add)
            chain(last)
            for t in range(NT):
                work = score[:, t, 0:seen(t)]
                for _ in range(TOP // 8):
                    chain(dve.max(best[:, :], work))
                    chain(dve.match_replace(work, best[:, :], work, NEG))
                b = bias[:, t, 0:seen(t)]
                chain(dve.tensor_scalar(b, work, 2 * NEG / 3, 1.0, ALU.is_lt, ALU.subtract))
                chain(dve.tensor_scalar(b, b, -FILL, None, ALU.mult))
                own = bias[:, t, META + t * P:seen(t)]
                last = dve.tensor_tensor(own, own, causal_fill, ALU.add)
            chain(last)


def phase_sparse_attention(nc, bank, const, io, life):
    with ExitStack() as ctx:
        s = Scope(nc, ctx, "sa")
        q, c, cm, cT, bias = (life[n] for n in ("q2", "c", "c_m", "cT", "bias"))
        oh, ol = life["attn_hi"], life["attn_lo"]
        masked = s.sb("masked", [P, 2, TM])
        p = s.sb("p", [P, 2, TM])
        pT, pTm = s.sb("pT", [P, 2, T]), s.sb("pTm", [META, 2, P])
        mx, total = s.sb("mx", [P, 2]), s.sb("total", [P, 2])
        names = ("scored", "masked_done", "maxed", "exped", "scaled", "turned", "taken", "o_done", "o_hi", "o_lo",
                 "vector_steps")
        S = {n: s.sem(n) for n in names}
        ident = const[:, CONSTS["ident"][0]:CONSTS["ident"][1]]
        units = [(t, hd) for t in range(NT) for hd in range(AH)]
        N = len(units)
        block = s.block()

        @block.tensor
        def _(pe):
            for n in range(N + 2):
                if n < N:
                    t, hd = units[n]
                    if n >= 2:
                        pe.wait_ge(S["masked_done"], n - 1)
                    b0, w0 = 2 * (n % 2), min(seen(t), BANK)
                    lhs = q[:, hd, t * P:(t + 1) * P]
                    last = pe.matmul(bank[:, b0, 0:w0], lhs, cT[:, 0:w0], start=True, stop=True)
                    if seen(t) > BANK:
                        last = pe.matmul(bank[:, b0 + 1, 0:seen(t) - BANK], lhs, cT[:, BANK:seen(t)],
                                         start=True, stop=True)
                    last.then_inc(S["scored"], 1)
                if 1 <= n <= N:
                    e = n - 1
                    t = units[e][0]
                    pe.wait_ge(S["scaled"], e + 1)
                    if e >= 1:
                        pe.wait_ge(S["taken"], e)
                    pe.transpose(bank[0:META, 6, 0:P], p[:, e % 2, 0:META], ident)
                    for kt in range(t + 1):
                        last = pe.transpose(bank[:, 4 + e % 2, kt * P:(kt + 1) * P],
                                            p[:, e % 2, META + kt * P:META + (kt + 1) * P], ident)
                    last.then_inc(S["turned"], 1)
                if n >= 2:
                    e = n - 2
                    t = units[e][0]
                    pe.wait_ge(S["taken"], e + 1)
                    if e >= 1:
                        pe.wait_ge(S["o_lo"], e)
                    o = bank[:, 7, 0:P]
                    pe.matmul(o, cm[:, :], pTm[:, e % 2, :], start=True, stop=False)
                    for kt in range(t + 1):
                        last = pe.matmul(o, c[:, kt, :], pT[:, e % 2, kt * P:(kt + 1) * P], start=False,
                                         stop=kt == t)
                    last.then_inc(S["o_done"], 1)

        @block.scalar
        def _(act):
            for n in range(N + 2):
                if n < N:
                    t = units[n][0]
                    act.wait_ge(S["maxed"], n + 1)
                    if n >= 2:
                        act.wait_ge(S["turned"], n - 1)
                    act.activation(p[:, n % 2, 0:seen(t)], masked[:, n % 2, 0:seen(t)], ACT.Exp,
                                   bias=mx[:, n % 2:n % 2 + 1], scale=ATTN_SCALE,
                                   accum_out=total[:, n % 2:n % 2 + 1]).then_inc(S["exped"], 1)
                if 1 <= n <= N:
                    e = n - 1
                    t = units[e][0]
                    act.wait_ge(S["turned"], e + 1)
                    if e >= 2:
                        act.wait_ge(S["o_done"], e - 1)
                    act.activation(pTm[:, e % 2, :], bank[0:META, 6, 0:P], ACT.Copy)
                    act.activation(pT[:, e % 2, 0:(t + 1) * P], bank[:, 4 + e % 2, 0:(t + 1) * P], ACT.Copy)\
                        .then_inc(S["taken"], 1)
                if n >= 2:
                    e = n - 2
                    t, hd = units[e]
                    act.wait_ge(S["o_done"], e + 1)
                    act.activation(oh[:, hd, t * P:(t + 1) * P], bank[:, 7, 0:P], ACT.Copy).then_inc(S["o_hi"], 1)

        @block.vector
        def _(dve):
            chain = Chain(dve, S["vector_steps"])
            for n in range(N + 3):
                if n < N:
                    t = units[n][0]
                    dve.wait_ge(S["scored"], n + 1)
                    if n >= 2:
                        dve.wait_ge(S["exped"], n - 1)
                    pair = bank[:, 2 * (n % 2):2 * (n % 2) + 2, :].rearrange("p b n -> p (b n)")
                    dve.tensor_tensor_reduce(masked[:, n % 2, 0:seen(t)], pair[:, 0:seen(t)], bias[:, t, 0:seen(t)],
                                             1.0, NEG, ALU.add, ALU.max, mx[:, n % 2:n % 2 + 1])\
                        .then_inc(S["masked_done"], 1)
                    dve.wait_ge(S["masked_done"], n + 1)
                    dve.tensor_scalar(mx[:, n % 2:n % 2 + 1], mx[:, n % 2:n % 2 + 1], -ATTN_SCALE, None,
                                      ALU.mult).then_inc(S["maxed"], 1)
                if n >= 1 and n - 1 < N:
                    e = n - 1
                    t = units[e][0]
                    dve.wait_ge(S["exped"], e + 1)
                    chain(dve.reciprocal(total[:, e % 2:e % 2 + 1], total[:, e % 2:e % 2 + 1]))
                    dve.tensor_scalar(p[:, e % 2, 0:seen(t)], p[:, e % 2, 0:seen(t)], total[:, e % 2:e % 2 + 1],
                                      None, ALU.mult).then_inc(S["scaled"], 1)
                if n >= 3:
                    e = n - 3
                    t, hd = units[e]
                    cols = slice(t * P, (t + 1) * P)
                    dve.wait_ge(S["o_hi"], e + 1)
                    dve.tensor_tensor(ol[:, hd, cols], bank[:, 7, 0:P], oh[:, hd, cols].bitcast(F32), ALU.subtract)\
                        .then_inc(S["o_lo"], 1)


def phase_pool_and_conv(nc, bank, io, life):
    with ExitStack() as ctx:
        s = Scope(nc, ctx, "pc")
        u, cb, cc, cu = (life[n] for n in ("u", "cb", "cc", "cu"))
        ph, pl, vh, vl = (life[n] for n in ("pool_hi", "pool_lo", "conv_hi", "conv_lo"))
        sums = s.sb("sums", [P, 2, TM])
        pooled = s.sb("pooled", [P, POOL_GROUPS, T])
        y = cu[:, :, 0:T]
        pool_w = s.sb("pool_w", [P, POOL_GROUPS, P])
        scale, conv_w = s.sb("scale", [P, POOL_GROUPS]), s.sb("conv_w", [P, 3, POOL_GROUPS])
        landed, pooled_done, mixed_done, vec = (s.sem("landed"), s.sem("pooled"), s.sem("mixed"),
                                                s.sem("vector_steps"))
        v_done = s.sem("v_done")
        block = s.block()

        @block.sync
        def _(sp):
            sp.dma_start(pool_w[:, :, :], io["pool_w"]).then_inc(landed, 16)
            sp.dma_start(scale[:, :], io["pool_scale"]).then_inc(landed, 16)
            sp.dma_start(conv_w[:, :, :], io["conv_w"]).then_inc(landed, 16)

        @block.tensor
        def _(pe):
            pe.wait_ge(landed, 48)
            for g in range(POOL_GROUPS):
                pe.wait_ge(pooled_done, g + 1)
                pe.matmul(bank[:, g, :], pool_w[:, g, :], pooled[:, g, :], start=True, stop=True)\
                    .then_inc(mixed_done, 1)

        @block.gpsimd
        def _(pool):
            pool.tensor_tensor(cc[:, :, :], cc[:, :, :], cu[:, :, :], ALU.mult).then_inc(v_done, 1)

        @block.vector
        def _(dve):
            chain = Chain(dve, vec)
            dve.wait_ge(landed, 48)
            for g in range(POOL_GROUPS):
                src, lo = u[:, g, :], 0
                for j in range(g + 1):
                    dst, step = sums[:, j % 2, :], 1 << j
                    lo += step
                    chain(dve.tensor_tensor(dst[:, lo:TM], src[:, lo:TM], src[:, lo - step:TM - step], ALU.add))
                    src = dst
                last = dve.scalar_tensor_tensor(pooled[:, g, :], src[:, META:TM], 1.0 / (2 << g), u[:, g, META:TM],
                                                ALU.mult, ALU.subtract)
                last.then_inc(pooled_done, 1)
                dve.wait_ge(pooled_done, g + 1)
            for g in range(POOL_GROUPS):
                dve.wait_ge(mixed_done, g + 1)
                last = dve.tensor_scalar(pooled[:, g, :], bank[:, g, :], scale[:, g:g + 1], None, ALU.mult)
            chain(last)
            chain(dve.tensor_copy(ph[:, :, :], pooled[:, :, :]))
            dve.tensor_tensor(pl[:, :, :], pooled[:, :, :], ph[:, :, :].bitcast(F32), ALU.subtract)
            dve.wait_ge(v_done, 1)
            for g in range(POOL_GROUPS):
                last = dve.tensor_scalar(y[:, g, :], cc[:, g, META - 2:TM - 2], conv_w[:, 0, g:g + 1], None,
                                         ALU.mult)
            for k in (1, 2):
                chain(last)
                for g in range(POOL_GROUPS):
                    last = dve.scalar_tensor_tensor(y[:, g, :], cc[:, g, META - 2 + k:TM - 2 + k],
                                                    conv_w[:, k, g:g + 1], y[:, g, :], ALU.mult, ALU.add)
            chain(last)
            chain(dve.tensor_tensor(y[:, :, :], y[:, :, :], cb[:, :, :], ALU.mult))
            chain(dve.tensor_copy(vh[:, :, :], y[:, :, :]))
            dve.tensor_tensor(vl[:, :, :], y[:, :, :], vh[:, :, :].bitcast(F32), ALU.subtract)


def phase_branches(nc, bank, io, life):
    with ExitStack() as ctx:
        s = Scope(nc, ctx, "br")
        xh, xl, mh, ml = (life[n] for n in ("xh", "xl", "m_hi", "m_lo"))
        sg, y = s.sb("sg", [P, 4, T]), s.sb("y", [P, 4, T])
        m_sum = s.sb("m_sum", [P, 4, T])
        b_gate = s.sb("b_gate", [P, 3 * KD])
        ring = WeightRing(s)
        gemm = Gemm(s, ring, bank)
        landed, y_ready, y_used, vec = s.sem("landed"), s.sem("y_ready"), s.sem("y_used"), s.sem("vector_steps")
        G0 = 3496

        def part(w, c0, kt, x, gate):
            return dict(kind="columns", slab=lambda i, turn: weight_slab(w, i, c0 + turn * BANK), width=BANK,
                        ktiles=kt, x=x, meta=False, gate=gate)

        def split(hi, lo):
            return lambda kt, m: (hi[:, kt, :], lo[:, kt, :])

        cols = lambda kt, m: (xh[:, kt, META:TM], xl[:, kt, META:TM])
        plan = []
        for n, (w, kt, hi, lo) in enumerate((("w_a", 4, "pool_hi", "pool_lo"), ("w_b", 8, "attn_hi", "attn_lo"),
                                             ("w_c", 4, "conv_hi", "conv_lo"))):
            gate = part(io["w_in_2"], 0, KD, cols, n)
            gate["slab"] = lambda i, turn, n=n: weight_slab(io["w_in_2"][:, G0 + n * D - BANK:], i,
                                                            (turn + 1) * BANK)
            plan.append(gate)
            plan.append(part(io[w], 0, kt, split(life[hi], life[lo]), None))
        TURNS = D // BANK
        blocks = gemm.plan(plan, TURNS)
        block = s.block()

        @block.sync
        def _(sp):
            sp.dma_start(b_gate[:, :], io["b_gate"]).then_inc(landed, 16)
            with sp.Fori(0, TURNS) as turn:
                for b in blocks:
                    gemm.on_sync(sp, b, turn)

        @block.gpsimd
        def _(pool):
            ring.open_raw(pool)
            with pool.Fori(0, TURNS) as turn:
                for b in blocks:
                    gemm.on_gpsimd(pool, b, turn)

        @block.tensor
        def _(pe):
            ring.open_slots(pe)
            with pe.Fori(0, TURNS) as turn:
                for b in blocks:
                    gemm.on_tensor(pe, b, turn)

        @block.scalar
        def _(act):
            gemm.open_banks(act)
            act.wait_ge(landed, 16)

            def take(n, turn):
                b = blocks[n]
                if b["gate"] is not None:
                    act.wait_ge(y_used, turn * 12 + 4 * b["gate"] + 4)

                def use(j, m, got):
                    if b["gate"] is not None:
                        at = bass.ds(turn * 4 + b["gate"] * KD + m, 1)
                        return act.activation(sg[:, m, :], got, ACT.Sigmoid, bias=b_gate[:, at])
                    return act.activation(y[:, m, :], got, ACT.Copy)

                gemm.take(act, b, use, turn)
                if b["gate"] is None:
                    act.wait_ge(gemm.bank_free, NBANK + b["tile0"] + 4 + turn * b["per"][1])
                    act.sem_inc(y_ready, 4)

            with act.Fori(0, TURNS) as turn:
                gemm.on_scalar(act, blocks[0], turn)
                for n in range(len(blocks)):
                    if n + 1 < len(blocks):
                        gemm.on_scalar(act, blocks[n + 1], turn)
                    take(n, turn)

        @block.vector
        def _(dve):
            chain = Chain(dve, vec)
            dve.sem_inc(y_used, 4)
            with dve.Fori(0, TURNS) as turn:
                chain.loop(turn, 4)
                for n in range(3):
                    dve.wait_ge(y_ready, turn * 12 + 4 * n + 4)
                    if n == 0:
                        dve.tensor_tensor(m_sum[:, :, :], sg[:, :, :], y[:, :, :], ALU.mult).then_inc(y_used, 4)
                    else:
                        chain(dve.tensor_tensor(y[:, :, :], sg[:, :, :], y[:, :, :], ALU.mult))
                        dve.tensor_tensor(m_sum[:, :, :], m_sum[:, :, :], y[:, :, :], ALU.add).then_inc(y_used, 4)
                dve.wait_ge(y_used, turn * 12 + 16)
                at = bass.ds(turn * 4, 4)
                chain(dve.tensor_copy(mh[:, at, :], m_sum[:, :, :]))
                chain(dve.tensor_tensor(ml[:, at, :], m_sum[:, :, :], mh[:, at, :].bitcast(F32), ALU.subtract))
            chain.end_loop(TURNS)


def phase_out_2(nc, bank, io, life):
    with ExitStack() as ctx:
        s = Scope(nc, ctx, "o2")
        mh, ml, h, xh, xl = (life[n] for n in ("m_hi", "m_lo", "h", "fh", "fl"))
        gain = s.sb("gain", [P, KD])
        const = s.sb("const", [P, CONST_2_W])
        ring = WeightRing(s)
        gemm = Gemm(s, ring, bank)
        landed, h_done, vec = s.sem("landed"), s.sem("h_done"), s.sem("vector_steps")
        norm = NormColumns(s, h, None, gain, xh, xl, const[:, CONSTS["ident"][0]:CONSTS["ident"][1]], bank)

        def part(c0):
            return dict(kind="rows", slab=lambda i, _: weight_slab(io["w_o"], i, c0), width=BANK, ktiles=KD,
                        x=lambda kt, m: (mh[:, kt, m * P:(m + 1) * P], ml[:, kt, m * P:(m + 1) * P]),
                        meta=False, c0=c0)

        blocks = gemm.plan([part(0), part(BANK)])
        block = s.block()

        @block.sync
        def _(sp):
            sp.dma_start(const[:, :], io["const"][:, 0:CONST_2_W]).then_inc(landed, 16)
            sp.dma_start(gain[:, :], io["norm2_g"]).then_inc(landed, 16)
            sp.dma_start(h[:, :, :], io["x2"].rearrange("(t p) d -> p t d", p=P)).then_inc(landed, 16)
            for b in blocks:
                gemm.on_sync(sp, b)

        @block.gpsimd
        def _(pool):
            ring.open_raw(pool)
            for b in blocks:
                gemm.on_gpsimd(pool, b)

        @block.scalar
        def _(act):
            for b in blocks:
                gemm.on_scalar(act, b)
            act.wait_ge(landed, 48)
            norm.on_scalar(act, lambda e, t: e.wait_ge(h_done, 1))

        @block.tensor
        def _(pe):
            ring.open_slots(pe)
            for b in blocks:
                gemm.on_tensor(pe, b)
            pe.wait_ge(landed, 48)
            pe.wait_ge(gemm.bank_free, NBANK + gemm.tile0)
            norm.on_tensor(pe)

        @block.vector
        def _(dve):
            chain = Chain(dve, vec)
            gemm.open_banks(dve)
            dve.wait_ge(landed, 48)
            for b in blocks:
                gemm.take(dve, b, lambda j, m, got: dve.tensor_tensor(
                    h[:, m, b["c0"]:b["c0"] + BANK], got, h[:, m, b["c0"]:b["c0"] + BANK], ALU.add))
            dve.wait_ge(gemm.bank_free, NBANK + gemm.tile0)
            dve.sem_inc(h_done, 1)
            norm.on_vector(dve, chain)


def phase_feed_forward(nc, bank, io, life):
    with ExitStack() as ctx:
        s = Scope(nc, ctx, "ff")
        h, xh, xl = life["h"], life["fh"], life["fl"]
        ah, al = s.sb("ah", [P, KF, T], F32R), s.sb("al", [P, KF, T], F32R)
        sg, up = s.sb("sg", [P, 2, T]), s.sb("up", [P, 2, T])
        stats_row = s.sb("gain_row", [P, D])
        ring = WeightRing(s)
        gemm = Gemm(s, ring, bank)
        down = Gemm(s, ring, bank, "down_")
        landed, ready, used, vec = s.sem("landed"), s.sem("pair_ready"), s.sem("pair_used"), s.sem("vector_steps")
        h_done, out_done, stored = s.sem("h_done"), s.sem("out_done"), s.sem("stored")
        stats = RowStats(s, h, None, "s_")

        def part(b):
            return dict(kind="columns", width=BANK, ktiles=KD, meta=False, b=b,
                        slab=lambda i, turn: weight_slab(io["w_gate_up"], i, turn * 2 * BANK + b * BANK),
                        x=lambda kt, m: (xh[:, kt, :], xl[:, kt, :]))

        NB = KF // 2
        TURNS = NB // 2
        pair_blocks = gemm.plan([part(0), part(1)], TURNS)
        tail = gemm.plan([part(2 * TURNS)])[0]
        down.slab0 = gemm.slab0

        def down_part(c0):
            return dict(kind="rows", slab=lambda i, _: weight_slab(io["w_down"], i, c0), width=BANK, ktiles=KF,
                        x=lambda kt, m: (ah[:, kt, m * P:(m + 1) * P], al[:, kt, m * P:(m + 1) * P]),
                        meta=False, c0=c0)

        downs = down.plan([down_part(0), down_part(BANK)])
        block = s.block()

        @block.sync
        def _(sp):
            sp.dma_start(stats_row[:, :], io["final_g"].to_broadcast([P, D])).then_inc(landed, 16)
            with sp.Fori(0, TURNS) as turn:
                for b in pair_blocks:
                    gemm.on_sync(sp, b, turn)
            gemm.on_sync(sp, tail)
            for b in downs:
                down.on_sync(sp, b)
            for t in range(NT):
                sp.wait_ge(out_done, t + 1)
                sp.dma_start(io["out"][t * P:(t + 1) * P, :], h[:, t, :]).then_inc(stored, 16)
            sp.wait_ge(stored, 16 * NT)

        @block.gpsimd
        def _(pool):
            ring.open_raw(pool)
            with pool.Fori(0, TURNS) as turn:
                for b in pair_blocks:
                    gemm.on_gpsimd(pool, b, turn)
            gemm.on_gpsimd(pool, tail)
            for b in downs:
                down.on_gpsimd(pool, b)

        @block.tensor
        def _(pe):
            ring.open_slots(pe)
            with pe.Fori(0, TURNS) as turn:
                for b in pair_blocks:
                    gemm.on_tensor(pe, b, turn)
            gemm.on_tensor(pe, tail)
            pe.wait_ge(gemm.bank_free, NBANK + gemm.tile0)
            pe.wait_ge(used, 2 * NB + 2)
            for b in downs:
                down.on_tensor(pe, b)

        @block.scalar
        def _(act):
            gemm.open_banks(act)

            def take(b, turn=0):
                first = 2 * b["b"] if b is not tail else 4 * TURNS

                def use(j, m, got):
                    if m < 2:
                        act.wait_ge(used, first + m + 1 + turn * 4)
                        return act.activation(sg[:, m, :], got, ACT.Silu)
                    return act.activation(up[:, m - 2, :], got, ACT.Copy)

                gemm.take(act, b, use, turn)
                act.wait_ge(gemm.bank_free, NBANK + b["tile0"] + 4 + turn * b["per"][1])
                act.sem_inc(ready, 2)

            with act.Fori(0, TURNS) as turn:
                for b in pair_blocks:
                    gemm.on_scalar(act, b, turn)
                    take(b, turn)
            gemm.on_scalar(act, tail)
            take(tail)
            for b in downs:
                down.on_scalar(act, b)
            stats.on_scalar(act, lambda e, t: e.wait_ge(h_done, 1))

        @block.vector
        def _(dve):
            chain = Chain(dve, vec)
            dve.sem_inc(used, 2)
            down.open_banks(dve)

            def hidden(b, turn=0):
                first = 2 * b["b"] if b is not tail else 4 * TURNS
                dve.wait_ge(ready, first + 2 + turn * 4)
                at = bass.ds(turn * 4 + first, 2)
                chain(dve.tensor_tensor(up[:, :, :], up[:, :, :], sg[:, :, :], ALU.mult))
                chain(dve.tensor_copy(ah[:, at, :], up[:, :, :]))
                dve.tensor_tensor(al[:, at, :], up[:, :, :], ah[:, at, :].bitcast(F32), ALU.subtract)\
                    .then_inc(used, 2)

            with dve.Fori(0, TURNS) as turn:
                chain.loop(turn, 4)
                for b in pair_blocks:
                    hidden(b, turn)
            chain.end_loop(TURNS)
            hidden(tail)
            dve.wait_ge(landed, 16)
            for b in downs:
                down.take(dve, b, lambda j, m, got: dve.tensor_tensor(
                    h[:, m, b["c0"]:b["c0"] + BANK], got, h[:, m, b["c0"]:b["c0"] + BANK], ALU.add))
            dve.wait_ge(down.bank_free, NBANK + down.tile0)
            dve.sem_inc(h_done, 1)
            stats.on_vector(dve, chain)
            for t in range(NT):
                dve.scalar_tensor_tensor(h[:, t, :], h[:, t, :], stats.rstd[:, t:t + 1], stats_row[:, :],
                                         ALU.mult, ALU.mult).then_inc(out_done, 1)



def program(nc, io):
    SEMAPHORES.clear()
    with ExitStack() as whole:
        bank = whole.enter_context(nc.psum_tensor("bank", [P, NBANK, BANK], F32))
        block_1(nc, bank, io)
        clear_semaphores(nc)
        block_2(nc, bank, io)


def block_1(nc, bank, io):
    picks_end, mix_end, const_end, parts_end, rows_end = (ExitStack() for _ in range(5))
    s = Scope(nc, picks_end, "b1")
    life = {"pick_keys": s.sb("pick_keys", [P, 2, T], BF16, side="right"),
            "pick_gates": s.sb("pick_gates", [P, T, 3], BF16, side="right")}
    const = Scope(nc, const_end, "b1c").sb("const", [P, CONST_W])
    s = Scope(nc, parts_end, "b1p")
    for n in ("q", "k", "v", "gv", "gr"):
        life[n] = s.sb(n, [P, NT, BANK])
    for n in ("k_m", "v_m", "gv_m"):
        life[n] = s.sb(n, [META, BANK])
    life["gqk"], life["zT"] = s.sb("gqk", [P, 4, TM]), s.sb("zT", [P, 1, TM])
    phase_project_1(nc, bank, const, io, life)
    life["mix"] = Scope(nc, mix_end, "b1m").sb("mix", [P, NT, D], side="right")
    phase_diff_attention(nc, bank, const, io, life)
    phase_linear_attention(nc, bank, const, io, life)
    parts_end.close()
    s = Scope(nc, rows_end, "b1r")
    life["h"] = s.sb("h", [P, NT, D])
    phase_mix_out(nc, bank, const, io, life)
    mix_end.close()
    life["scores"] = s.sb("scores", [P, NT, HP, PEER_KEYS])
    phase_peer_query(nc, bank, const, io, life)
    phase_peer_select(nc, bank, const, io, life)
    rows_end.close()
    const_end.close()
    phase_peer_experts(nc, bank, io, life)
    picks_end.close()


def block_2(nc, bank, io):
    life = {}
    left, right = ExitStack(), ExitStack()
    s = Scope(nc, left, "b2")
    for n in ("xh", "xl"):
        life[n] = s.sb(n, [P, KD, TM], F32R)
    r = Scope(nc, right, "b2r")
    const = r.sb("const", [P, CONST_2_W], side="right")
    for n, shape in (("bias", [P, NT, TM]), ("c", [P, NT, LAT]), ("c_m", [META, LAT]), ("cT", [P, TM]),
                     ("u", [P, 4, TM]), ("cc", [P, 4, TM]), ("cu", [P, 4, TM]), ("xs", [P, NT + 1, D]),
                     ("h_rows", [P, NT, D])):
        life[n] = r.sb(n, shape, side="right")
    life["q2"] = life["xs"][:, 0:NT, :].rearrange("p t (two n) -> p (t two) n", two=2)
    life["cb"] = life["h_rows"][:, 0:NT // 2, :].rearrange("p t (two n) -> p (t two) n", two=2)
    phase_project_2(nc, bank, const, io, life)
    for n in ("attn_hi", "attn_lo"):
        life[n] = s.sb(n, [P, AH, T], F32R)
    phase_sparse_attention(nc, bank, const, io, life)
    for n in ("pool_hi", "pool_lo", "conv_hi", "conv_lo"):
        life[n] = s.sb(n, [P, POOL_GROUPS, T], F32R)
    phase_pool_and_conv(nc, bank, io, life)
    right.close()
    right = ExitStack()
    r = Scope(nc, right, "b2m")
    for n in ("m_hi", "m_lo"):
        life[n] = r.sb(n, [P, KD, T], F32R, side="right")
    phase_branches(nc, bank, io, life)
    left.close()
    left = ExitStack()
    s = Scope(nc, left, "b2f")
    life["h"] = s.sb("h", [P, NT, D])
    for n in ("fh", "fl"):
        life[n] = s.sb(n, [P, KD, T], F32R)
    phase_out_2(nc, bank, io, life)
    right.close()
    phase_feed_forward(nc, bank, io, life)
    left.close()



def layouts(i):
    def rows(a):
        return a[0]

    def per_partition(a):
        return a[0].reshape(-1, P).T

    w2 = i["w_in_2"][0]
    at = np.cumsum([0, POOL_D, AH * LAT, LAT, IDX_H * IDX_D, IDX_D, IDX_H])
    q_idx, k_idx, w_idx = (w2[:, at[n]:at[n + 1]] for n in (3, 4, 5))
    gate_up = i["w_gate_up_2"][0].reshape(D, 2, FF // (BANK // 2), BANK // 2)
    return {
        "const": const_table(),
        "x": i["x"][0], "meta_tokens": i["meta_tokens"], "ln1_w": per_partition(i["ln1_w"]),
        "w_in": rows(i["w_in"]),
        "da_lambda_q1": i["da_lambda_q1"], "da_lambda_k1": i["da_lambda_k1"],
        "da_lambda_q2": i["da_lambda_q2"], "da_lambda_k2": i["da_lambda_k2"], "da_subln_w": i["da_subln_w"],
        "gla_gate_w2_f": rows(i["gla_gate_w2_f"]), "gla_gate_b_f": i["gla_gate_b_f"],
        "gla_gate_w2_b": rows(i["gla_gate_w2_b"]), "gla_gate_b_b": i["gla_gate_b_b"],
        "gla_norm_w": i["gla_norm_w"], "w_out": rows(i["w_out"]), "ln2_w": per_partition(i["ln2_w"]),
        "peer_w_q": rows(i["peer_w_q"]),
        "peer_keys": i["peer_sub_keys"].reshape(HP, PEER_KEYS, -1).transpose(2, 0, 1),
        "peer_u": i["peer_u"].reshape(PEER_KEYS, PEER_KEYS, KD, P).transpose(0, 3, 2, 1).reshape(PEER_KEYS, P, D),
        "peer_v": i["peer_v"].reshape(PEER_KEYS, PEER_KEYS, D),
        "final_norm_w": i["final_norm_w"][None],
        "meta_2": i["meta_2"], "norm1_g": per_partition(i["norm1_g_2"]), "w_in_2": w2,
        "w_index": np.concatenate([q_idx] + [k_idx] * 4, 1),
        "w_latent": np.concatenate([w2[:, at[2]:at[3]], w_idx], 1),
        "b_gate": per_partition(i["b_gate_2"]),
        "pool_w": i["pool_w_2"][0].transpose(1, 0, 2), "pool_scale": per_partition(i["pool_scale_2"]),
        "w_a": rows(i["w_a_2"]), "kv_norm_g": i["kv_norm_g_2"], "w_b": rows(i["w_b_2"]),
        "conv_w": i["conv_w_2"][0].reshape(3, POOL_GROUPS, P).transpose(2, 0, 1),
        "w_c": rows(i["w_c_2"]), "w_o": rows(i["w_o_2"]), "norm2_g": per_partition(i["norm2_g_2"]),
        "w_gate_up": gate_up.transpose(0, 2, 1, 3).reshape(D, 2 * FF),
        "w_down": rows(i["w_down_2"]), "final_g": i["final_g_2"][None],
    }


SCRATCH = {"h1": (T, D), "experts": (T, D), "x2": (T, D), "hn_hi": (P, KD, T), "hn_lo": (P, KD, T)}


def kernel(**inputs):
    import concourse.bacc as bacc
    from concourse.bass_utils import run_bass_kernel_spmd

    nc = bacc.Bacc("TRN2", target_bir_lowering=False, num_devices=1)
    arrays, io = {}, {}
    for name, a in layouts({n: np.asarray(a) for n, a in inputs.items()}).items():
        a = np.ascontiguousarray(a)
        arrays[f"in_{name}"] = a
        io[name] = nc.dram_tensor(f"in_{name}", a.shape, mybir.dt.from_np(a.dtype), kind="ExternalInput").ap()
    for name, shape in SCRATCH.items():
        io[name] = nc.dram_tensor(f"scratch_{name}", shape, F32, kind="Internal").ap()
    io["out"] = nc.dram_tensor("out", (T, D), F32, kind="ExternalOutput").ap()
    program(nc, io)
    got = run_bass_kernel_spmd(nc, [arrays], core_ids=[0])
    return got.results[0]["out"].reshape(1, T, D)
```

```python
import math
from contextlib import ExitStack

import numpy as np

import concourse.bass as bass
from concourse import mybir

F32 = mybir.dt.float32
F32R = mybir.dt.float32r
BF16 = mybir.dt.bfloat16
U32 = mybir.dt.uint32
ALU = mybir.AluOpType
ACT = mybir.ActivationFunctionType
AX = mybir.AxisListType

P = 128
D = 1024
KD = D // P
T = 512
NT = T // P
META = 16
TM = META + T
BANK = 512
NBANK = 8
SLAB = 2
SLOTS = 4
EPS = 1e-6
NEG = -3.0e38
FILL = -1.0e30

DA_HEADS, DA_DIM, DA_V = 4, 64, 128
ROPE = DA_DIM // 4
HALF = ROPE // 2
THETA = 500000.0
LAM_INIT = 0.8 - 0.6 * math.exp(-0.3 * 0)
GLA_HEADS, GLA_DK, GLA_DV, GLA_TAU, CHUNK, RANK = 4, 64, 128, 16.0, 64, 16
NCHUNK = T // CHUNK

CONSTS = {}


def _const_layout():
    at = 0
    for name, width in (("ident", P), ("causal", P), ("causal_fill", P), ("iota", P), ("sum_f", P + 2),
                        ("sum_b", P + 2), ("sum_m", META), ("keep_f", GLA_HEADS * P), ("keep_b", GLA_HEADS * P),
                        ("cos", (NT + 1) * 8 * HALF), ("sin", (NT + 1) * 8 * HALF)):
        CONSTS[name] = (at, at + width)
        at += width
    return at


CONST_W = _const_layout()
CONST_2_W = CONSTS["causal_fill"][1]


def const_table():
    table = np.zeros((P, CONST_W), np.float32)

    def put(name, value):
        a, b = CONSTS[name]
        table[:value.shape[0], a:b] = value.reshape(value.shape[0], b - a)

    j, i = np.arange(P)[:, None], np.arange(P)[None, :]
    same = (j // CHUNK) == (i // CHUNK)
    mid = CHUNK // 2
    upto = same & (j % CHUNK <= mid)
    frm = same & (j % CHUNK >= mid)
    put("ident", np.eye(P, dtype=np.float32))
    put("iota", np.tile(np.arange(P, dtype=np.float32), (P, 1)))
    half = np.arange(2)[None, :] * CHUNK
    for name, along, to_mid in (("sum_f", same & (j <= i), upto), ("sum_b", same & (j >= i), frm)):
        shifted = (along.astype(np.float32) - to_mid) / GLA_TAU
        mids = to_mid[:, [0, CHUNK]].astype(np.float32) / GLA_TAU
        put(name, np.concatenate([shifted, mids], 1))
    jm, im = np.arange(META)[:, None], np.arange(META)[None, :]
    put("sum_m", ((jm <= im).astype(np.float32) - 1.0) / GLA_TAU)
    put("keep_f", np.tile((same & (j <= i)).astype(np.float32), (1, GLA_HEADS)))
    put("keep_b", np.tile((same & (j >= i)).astype(np.float32), (1, GLA_HEADS)))
    put("causal", (i <= j).astype(np.float32))
    put("causal_fill", np.where(i <= j, 0.0, FILL).astype(np.float32))
    inv = np.power(np.float32(THETA), -np.arange(0, ROPE, 2, dtype=np.float32) / np.float32(ROPE)).astype(np.float32)
    for name, f in (("cos", np.cos), ("sin", np.sin)):
        v = np.zeros((P, NT + 1, 8, HALF), np.float32)
        for t in range(NT + 1):
            n = P if t < NT else META
            pos = (np.arange(n) + (META + t * P if t < NT else 0)).astype(np.float32)
            v[:n, t] = f((pos[:, None] * inv[None, :]).astype(np.float32)).astype(np.float32)[:, None, :]
        put(name, v)
    return table


class Chain:

    def __init__(self, eng, sem):
        self.eng, self.sem, self.n = eng, sem, 0
        self.turn, self.per_turn = None, 0

    def __call__(self, ins):
        ins.then_inc(self.sem, 1)
        self.n += 1
        now = self.n if self.turn is None else self.n + self.turn * self.per_turn
        self.eng.wait_ge(self.sem, now)

    def loop(self, turn, per_turn):
        self.turn, self.per_turn, self.start = turn, per_turn, self.n

    def end_loop(self, turns):
        assert self.n - self.start == self.per_turn, (self.n - self.start, self.per_turn)
        self.n = self.start + self.per_turn * turns
        self.turn = None


SEMAPHORES = []


def clear_semaphores(nc):
    with nc.Block() as block:

        @block.gpsimd
        def _(pool):
            nc.clear_and_free_semaphores(SEMAPHORES)
    SEMAPHORES.clear()


class Scope:

    def __init__(self, nc, ctx, name):
        self.nc, self.ctx, self.name = nc, ctx, name

    def sb(self, name, shape, dt=F32, side="left"):
        return self.ctx.enter_context(self.nc.sbuf_tensor(f"{self.name}_{name}", shape, dt, side=side))

    def sem(self, name):
        sem = self.nc.alloc_semaphore(f"{self.name}_{name}")
        SEMAPHORES.append(sem)
        return sem

    def block(self):
        return self.ctx.enter_context(self.nc.Block())


class WeightRing:

    def __init__(self, s):
        self.raw = s.sb("w_raw", [P, SLOTS, SLAB, BANK])
        self.hi = s.sb("w_hi", [P, SLOTS, SLAB, BANK], F32R)
        self.lo = s.sb("w_lo", [P, SLOTS, SLAB, BANK], F32R)
        self.landed = [s.sem(f"w_landed{k}") for k in range(SLOTS)]
        self.raw_free = s.sem("w_raw_free")
        self.hi_ready = s.sem("w_hi_ready")
        self.lo_ready = s.sem("w_lo_ready")
        self.slot_free = s.sem("w_slot_free")

    def open_raw(self, pool):
        pool.sem_inc(self.raw_free, SLOTS)

    def open_slots(self, pe):
        pe.sem_inc(self.slot_free, SLOTS - 1)

    def load(self, sp, n, slot, src, parts=None):
        sp.wait_ge(self.raw_free, n + 1)
        width = src.shape[2]
        sp.dma_start(self.raw[:, slot, :src.shape[1], :width], src).then_inc(self.landed[slot], 16)

    def round_hi(self, act, n, slot, turn, width=BANK, rows=SLAB):
        act.wait_ge(self.landed[slot], (turn + 1) * 16)
        act.wait_ge(self.slot_free, n + 1)
        act.activation(self.hi[:, slot, :rows, :width], self.raw[:, slot, :rows, :width], ACT.Copy)\
            .then_inc(self.hi_ready, 1)

    def take_lo(self, pool, n, slot, width=BANK, rows=SLAB):
        pool.wait_ge(self.hi_ready, n + 1)
        pool.tensor_tensor(self.lo[:, slot, :rows, :width], self.raw[:, slot, :rows, :width],
                           self.hi[:, slot, :rows, :width].bitcast(F32), ALU.subtract)\
            .then_inc(self.lo_ready, 1)
        pool.wait_ge(self.lo_ready, n + 1)
        pool.sem_inc(self.raw_free, 1)


def split_products(pe, out, lhs, rhs, start, stop, skip=False, frees=None):
    first = pe.matmul(out, lhs[0], rhs[0], start=start, stop=False, skip_group_check=skip)
    if frees is not None:
        first.then_inc(frees, 1)
    pe.matmul(out, lhs[0], rhs[1], start=False, stop=False, skip_group_check=skip)
    return pe.matmul(out, lhs[1], rhs[0], start=False, stop=stop, skip_group_check=skip)


def weight_slab(w, s, c0, width=BANK, rows=SLAB):
    return w.rearrange("(k p) n -> p k n", p=P)[:, SLAB * s:SLAB * s + rows, bass.ds(c0, width)]


AHEAD, REST = slice(0, SLOTS - 1), slice(SLOTS - 1, None)


class Gemm:

    def __init__(self, s, ring, bank, name=""):
        self.ring, self.bank = ring, bank
        self.tile_done, self.bank_free = s.sem(name + "tile_done"), s.sem(name + "bank_free")
        self.slab0 = self.tile0 = 0

    def plan(self, blocks, turns=1):
        slab, tile = self.slab0, self.tile0
        for b in blocks:
            b["slab0"], b["slabs"] = slab, -(-b["ktiles"] // SLAB)
            slab += b["slabs"]
            b["ms"] = list(range(NT if b["kind"] == "rows" else b["width"] // P)) + [-1] * b["meta"]
            b["tile0"] = tile
            tile += len(b["ms"])
        if turns > 1:
            assert (slab - self.slab0) % SLOTS == 0 and (tile - self.tile0) % NBANK == 0
        per = (slab - self.slab0, tile - self.tile0)
        for b in blocks:
            b["per"] = per
        self.slab0 += turns * per[0]
        self.tile0 += turns * per[1]
        return blocks

    def open_banks(self, taker):
        taker.sem_inc(self.bank_free, NBANK)

    def on_sync(self, sp, b, turn=0):
        for i in range(b["slabs"]):
            n = b["slab0"] + i
            self.ring.load(sp, n + turn * b["per"][0], n % SLOTS, b["slab"](i, turn))

    def on_scalar(self, act, b, turn=0, part=slice(None)):
        for i in range(b["slabs"])[part]:
            n = b["slab0"] + i
            self.ring.round_hi(act, n + turn * b["per"][0], n % SLOTS,
                               n // SLOTS + turn * (b["per"][0] // SLOTS), b["width"])

    def on_gpsimd(self, pool, b, turn=0):
        for i in range(b["slabs"]):
            n = b["slab0"] + i
            self.ring.take_lo(pool, n + turn * b["per"][0], n % SLOTS, b["width"])

    def on_tensor(self, pe, b, turn=0):
        ring = self.ring
        pe.wait_ge(self.bank_free, b["tile0"] + len(b["ms"]) + turn * b["per"][1])
        for i in range(b["slabs"]):
            n = b["slab0"] + i
            pe.wait_ge(ring.lo_ready, n + 1 + turn * b["per"][0])
            for kk in range(SLAB):
                kt = i * SLAB + kk
                first, final = kt == 0, kt == b["ktiles"] - 1
                for j, m in enumerate(b["ms"]):
                    frees = ring.slot_free if kk == 0 and j == 0 else None
                    out = self.bank[:, (b["tile0"] + j) % NBANK, :]
                    wh, wl = ring.hi[:, n % SLOTS, kk, :], ring.lo[:, n % SLOTS, kk, :]
                    x = b["x"](kt, m)
                    if b["kind"] == "rows":
                        last = split_products(pe, out[:, 0:b["width"]], x, (wh[:, 0:b["width"]], wl[:, 0:b["width"]]),
                                              first, final, frees=frees)
                    elif m >= 0:
                        c = slice(m * P, (m + 1) * P)
                        last = split_products(pe, out, (wh[:, c], wl[:, c]), x, first, final, frees=frees)
                    else:
                        for mm in range(b["width"] // P):
                            c = slice(mm * P, (mm + 1) * P)
                            last = split_products(pe, out[:, mm * META:(mm + 1) * META], (wh[:, c], wl[:, c]), x,
                                                  first and mm == 0, final, True)
                    if final:
                        last.then_inc(self.tile_done, 1)

    def take(self, eng, b, use, turn=0):
        for j, m in enumerate(b["ms"]):
            n = b["tile0"] + j
            eng.wait_ge(self.tile_done, n + 1 + turn * b["per"][1])
            use(j, m, self.bank[:, n % NBANK, :]).then_inc(self.bank_free, 1)



class RowStats:

    def __init__(self, s, rows, meta, name="n_", junk=None):
        self.rows, self.meta, self.width = rows, meta, rows.shape[2]
        self.tiles = NT + (meta is not None)
        self.junk = s.sb(name + "junk", [P, self.width]) if junk is None else junk
        self.ss, self.root = s.sb(name + "ss", [P, NT + 1]), s.sb(name + "root", [P, NT + 1])
        self.rstd = s.sb(name + "rstd", [P, NT + 1])
        self.squared, self.meaned, self.rooted = s.sem(name + "squared"), s.sem(name + "mean"), s.sem(name + "root")

    def tile(self, t):
        return (self.rows[:, t, :], P) if t < NT else (self.meta[:, :], META)

    def on_scalar(self, act, ready):
        for t in range(self.tiles + 1):
            if t < self.tiles:
                ready(act, t)
                if t:
                    act.wait_ge(self.squared, t)
                src, n = self.tile(t)
                act.activation(self.junk[0:n, :], src, ACT.Square, accum_out=self.ss[0:n, t:t + 1])\
                    .then_inc(self.squared, 1)
            if t:
                n = self.tile(t - 1)[1]
                act.wait_ge(self.meaned, t)
                act.activation(self.root[0:n, t - 1:t], self.ss[0:n, t - 1:t], ACT.Sqrt).then_inc(self.rooted, 1)

    def on_vector(self, dve, chain, use):
        for t in range(self.tiles + 1):
            if t < self.tiles:
                n = self.tile(t)[1]
                dve.wait_ge(self.squared, t + 1)
                dve.tensor_scalar(self.ss[0:n, t:t + 1], self.ss[0:n, t:t + 1], 1.0 / self.width, EPS, ALU.mult,
                                  ALU.add).then_inc(self.meaned, 1)
            if t:
                n = self.tile(t - 1)[1]
                dve.wait_ge(self.rooted, t)
                chain(dve.reciprocal(self.rstd[0:n, t - 1:t], self.root[0:n, t - 1:t]))
                use(t - 1)


class NormColumns:

    def __init__(self, s, rows, meta, gain_col, hi, lo, ident, bank, xs=None, junk=None):
        self.stats = RowStats(s, rows, meta, junk=junk)
        self.meta, self.gain, self.hi, self.lo, self.ident, self.bank = meta, gain_col, hi, lo, ident, bank
        self.xs = s.sb("n_xs", [P, self.stats.tiles, D]) if xs is None else xs
        self.mtmp = s.sb("n_mtmp", [P, KD, META]) if meta is not None else None
        self.scaled, self.turned = s.sem("n_scaled"), s.sem("n_turned")
        self.hi_done, self.done = s.sem("n_hi"), s.sem("n_done")
        off = META if meta is not None else 0
        self.cols = slice(off, off + T)

    def on_scalar(self, act, ready):
        self.stats.on_scalar(act, ready)
        for k in range(KD):
            act.wait_ge(self.turned, k + 1)
            act.activation(self.hi[:, k, self.cols], self.bank[:, k, :], ACT.Copy,
                           scale=self.gain[:, k:k + 1]).then_inc(self.hi_done, 1)

    def on_vector(self, dve, chain):
        def scale(t):
            src, n = self.stats.tile(t)
            dve.tensor_scalar(self.xs[0:n, t, :], src, self.stats.rstd[0:n, t:t + 1], None, ALU.mult)\
                .then_inc(self.scaled, 1)

        self.stats.on_vector(dve, chain, scale)
        for k in range(KD):
            dve.wait_ge(self.hi_done, k + 1)
            dve.scalar_tensor_tensor(self.lo[:, k, self.cols], self.bank[:, k, :], self.gain[:, k:k + 1],
                                     self.hi[:, k, self.cols].bitcast(F32), ALU.mult, ALU.subtract)\
                .then_inc(self.done, 1)
        if self.meta is not None:
            dve.wait_ge(self.turned, KD + 1)
            src = self.bank[:, 0, 0:KD * META].rearrange("p (k m) -> p k m", k=KD)
            gain = self.gain[:, :].unsqueeze(2).to_broadcast([P, KD, META])
            chain(dve.tensor_tensor(self.mtmp[:, :, :], src, gain, ALU.mult))
            hi = self.hi[:, :, 0:META]
            chain(dve.tensor_copy(hi, self.mtmp[:, :, :]))
            dve.tensor_tensor(self.lo[:, :, 0:META], self.mtmp[:, :, :], hi.bitcast(F32), ALU.subtract)\
                .then_inc(self.done, 1)

    def total(self):
        return KD + (self.meta is not None)

    def on_tensor(self, pe):
        for t in range(NT):
            pe.wait_ge(self.scaled, t + 1)
            for k in range(KD):
                last = pe.transpose(self.bank[:, k, t * P:(t + 1) * P], self.xs[:, t, k * P:(k + 1) * P],
                                    self.ident)
                if t == NT - 1:
                    last.then_inc(self.turned, 1)
        if self.meta is not None:
            pe.wait_ge(self.scaled, NT + 1)
            pe.wait_ge(self.done, 1)
            for k in range(KD):
                last = pe.transpose(self.bank[:, 0, k * META:(k + 1) * META],
                                    self.xs[0:META, NT, k * P:(k + 1) * P], self.ident[0:META, 0:META])
            last.then_inc(self.turned, 1)



def phase_project_1(nc, bank, const, io, life):
    with ExitStack() as ctx:
        s = Scope(nc, ctx, "p1")
        h, hm = s.sb("h", [P, NT, D]), s.sb("h_meta", [META, D])
        xh, xl = s.sb("xh", [P, KD, TM], F32R), s.sb("xl", [P, KD, TM], F32R)
        gain = s.sb("gain", [P, KD])
        ring = WeightRing(s)
        gemm = Gemm(s, ring, bank)
        c_landed, g_landed = s.sem("const_landed"), s.sem("gain_landed")
        x_landed = [s.sem(f"x_landed{t}") for t in range(NT + 1)]
        vec = s.sem("vector_steps")
        ident = const[:, CONSTS["ident"][0]:CONSTS["ident"][1]]
        norm = NormColumns(s, h, hm, gain, xh, xl, ident, bank)

        def rows(kt, m):
            c = slice(META + m * P, META + (m + 1) * P) if m >= 0 else slice(0, P)
            return xh[:, kt, c], xl[:, kt, c]

        def columns(kt, m):
            c = slice(META, TM) if m >= 0 else slice(0, META)
            return xh[:, kt, c], xl[:, kt, c]

        def part(kind, c0, width, meta, dst, dst_meta):
            return dict(kind=kind, slab=lambda i, turn: weight_slab(io["w_in"], i, c0, width), width=width,
                        ktiles=KD, x=rows if kind == "rows" else columns, meta=meta, dst=dst, dst_meta=dst_meta)

        L = life
        blocks = gemm.plan([
            part("rows", 0, BANK, False, L["q"], None), part("rows", 512, BANK, True, L["k"], L["k_m"]),
            part("rows", 1024, BANK, True, L["v"], L["v_m"]), part("columns", 1536, BANK, True, L["gqk"], None),
            part("rows", 2048, BANK, True, L["gv"], L["gv_m"]), part("rows", 2560, BANK, False, L["gr"], None),
            part("columns", 2976, P, True, L["zT"], None)])
        block = s.block()

        @block.sync
        def _(sp):
            sp.dma_start(const[:, :], io["const"]).then_inc(c_landed, 16)
            for t in range(NT):
                sp.dma_start(h[:, t, :], io["x"][t * P:(t + 1) * P, :]).then_inc(x_landed[t], 16)
            sp.dma_start(hm[:, :], io["meta_tokens"]).then_inc(x_landed[NT], 16)
            sp.dma_start(gain[:, :], io["ln1_w"]).then_inc(g_landed, 16)
            for b in blocks:
                gemm.on_sync(sp, b)

        @block.gpsimd
        def _(pool):
            ring.open_raw(pool)
            for b in blocks:
                gemm.on_gpsimd(pool, b)

        @block.scalar
        def _(act):
            act.wait_ge(g_landed, 16)
            norm.on_scalar(act, lambda e, t: e.wait_ge(x_landed[t], 16))
            for b in blocks:
                gemm.on_scalar(act, b)

        @block.tensor
        def _(pe):
            ring.open_slots(pe)
            pe.wait_ge(c_landed, 16)
            norm.on_tensor(pe)
            pe.wait_ge(norm.done, norm.total())
            for b in blocks:
                gemm.on_tensor(pe, b)

        @block.vector
        def _(dve):
            chain = Chain(dve, vec)
            gemm.open_banks(dve)
            dve.wait_ge(g_landed, 16)
            for landed in x_landed:
                dve.wait_ge(landed, 16)
            norm.on_vector(dve, chain)
            for b in blocks:
                def use(j, m, got):
                    if b["kind"] == "rows" and m >= 0:
                        return dve.tensor_copy(b["dst"][:, m, :], got)
                    if b["kind"] == "rows":
                        return dve.tensor_copy(b["dst_meta"][:, :], got[0:META, :])
                    if m >= 0:
                        return dve.tensor_copy(b["dst"][:, m, META:TM], got)
                    n = b["width"] // P
                    return dve.tensor_copy(b["dst"][:, :, 0:META],
                                           got[:, 0:n * META].rearrange("p (m c) -> p m c", m=n))

                gemm.take(dve, b, use)



def phase_diff_attention(nc, bank, const, io, life):
    with ExitStack() as ctx:
        s = Scope(nc, ctx, "da")
        q, k, km, v, vm, mix = (life[n] for n in ("q", "k", "k_m", "v", "v_m", "mix"))
        qT = s.sb("qT", [P, DA_HEADS, T])
        kT = s.sb("kT", [P, DA_HEADS, TM])
        rot = s.sb("rot", [P, 4, NT * 8 * HALF])
        p = s.sb("p", [P, 2, 2, TM])
        a = s.sb("a", [P, 2, TM])
        aT = s.sb("aT", [P, 2, T])
        aTm = s.sb("aTm", [META, 2, P])
        nmax, total, inv = s.sb("nmax", [P, 4]), s.sb("total", [P, 4]), s.sb("inv", [P, 4])
        lam_in = s.sb("lam_in", [P, 4, DA_DIM])
        lam_prod = s.sb("lam_prod", [P, 2, DA_DIM])
        lam_sum, lam = s.sb("lam_sum", [P, 2]), s.sb("lam", [P, 2])
        sub_w = s.sb("sub_w", [P, DA_V])
        sq = s.sb("sq", [P, NT * DA_HEADS, DA_V])
        ss, root = s.sb("ss", [P, NT * DA_HEADS]), s.sb("root", [P, NT * DA_HEADS])
        in_landed = s.sem("in_landed")
        turned_q, turned_k, cols_ready = s.sem("rot_q"), s.sem("rot_k"), s.sem("cols_ready")
        tp, lam_exp, lam_done = s.sem("transposed"), s.sem("lam_exp"), s.sem("lam_done")
        scored, maxed, exped, pair_done = s.sem("scored"), s.sem("maxed"), s.sem("exped"), s.sem("pair_done")
        diffed, a_turned, aT_ready = s.sem("diffed"), s.sem("a_turned"), s.sem("aT_ready")
        o_done, o_taken, squared, rooted, ms = (s.sem("o_done"), s.sem("o_taken"), s.sem("squared"),
                                                s.sem("rooted"), s.sem("mean_square"))
        vec = s.sem("vector_steps")
        ident = const[:, CONSTS["ident"][0]:CONSTS["ident"][1]]

        def angles(name, t0, t1, n):
            c0 = CONSTS[name][0] + t0 * 8 * HALF
            return const[0:n, c0:c0 + (t1 - t0) * 8 * HALF].rearrange("p (t h c) -> p t h c", h=8, c=HALF)

        turns = [(hd, t) for hd in range(DA_HEADS) for t in range(NT)]

        def pair(r, c):
            return 2 * c

        def scores_of(r, c):
            return bank[:, pair(r, c):pair(r, c) + 2, :].rearrange("p b n -> p (b n)")[:, 0:TM]

        O_BANK, M_BANK, W_BANK = 4, 5, 6
        block = s.block()

        @block.sync
        def _(sp):
            for n, name in enumerate(("da_lambda_q1", "da_lambda_k1", "da_lambda_q2", "da_lambda_k2")):
                sp.dma_start(lam_in[:, n, :], io[name].to_broadcast([P, DA_DIM])).then_inc(in_landed, 16)
            sp.dma_start(sub_w[:, :], io["da_subln_w"].to_broadcast([P, DA_V])).then_inc(in_landed, 16)

        @block.scalar
        def _(act):
            act.wait_ge(lam_done, 1)
            act.activation(lam[:, :], lam_sum[:, :], ACT.Exp).then_inc(lam_exp, 1)
            for r in range(len(turns) + 3):
                if r >= 3:
                    e = r - 3
                    act.wait_ge(a_turned, e + 1)
                    if e >= 2:
                        act.wait_ge(o_done, e - 1)
                    act.activation(aTm[:, e % 2, :], bank[0:META, M_BANK, 0:P], ACT.Copy)
                    act.activation(aT[:, e % 2, :], bank[:, W_BANK + e % 2, :], ACT.Copy).then_inc(aT_ready, 1)
                if r < len(turns):
                    for c in range(2):
                        u = 2 * r + c
                        act.wait_ge(maxed, u + 1)
                        if r >= 2:
                            act.wait_ge(diffed, r - 1)
                        act.activation(p[:, r % 2, c, :], scores_of(r, c), ACT.Exp,
                                       bias=nmax[:, u % 4:u % 4 + 1], accum_out=total[:, u % 4:u % 4 + 1])\
                            .then_inc(exped, 1)
            act.wait_ge(o_taken, len(turns))
            act.activation(sq[:, :, :].rearrange("p (t h) v -> p t h v", t=NT),
                           mix[:, :, 0:DA_HEADS * DA_V].rearrange("p t (h v) -> p t h v", h=DA_HEADS),
                           ACT.Square).then_inc(squared, 1)
            act.wait_ge(ms, 1)
            act.activation(root[:, :], ss[:, :], ACT.Sqrt).then_inc(rooted, 1)

        @block.tensor
        def _(pe):
            def columns(n, src, sem, count):
                pe.wait_ge(sem, count)
                if n >= 4:
                    pe.wait_ge(cols_ready, n - 3)
                for t in range(NT):
                    last = pe.transpose(bank[:, n % 4, t * P:(t + 1) * P], src(t), ident)
                last.then_inc(tp, 1)

            for hd in range(DA_HEADS):
                columns(hd, lambda t: q[:, t, hd * P:(hd + 1) * P], turned_q, 1)
            for hd in range(DA_HEADS):
                columns(DA_HEADS + hd, lambda t: k[:, t, hd * P:(hd + 1) * P], turned_k, 2)
            for hd in range(DA_HEADS):
                last = pe.transpose(bank[:, 4, hd * META:(hd + 1) * META], km[:, hd * P:(hd + 1) * P],
                                    ident[0:META, 0:META])
            last.then_inc(tp, 1)
            pe.wait_ge(cols_ready, 2 * DA_HEADS + 1)
            for r in range(len(turns) + 3):
                if r < len(turns):
                    hd, t = turns[r]
                    for c in range(2):
                        u = 2 * r + c
                        if r:
                            pe.wait_ge(exped, u - 1)
                        cc = slice(c * DA_DIM, (c + 1) * DA_DIM)
                        b = pair(r, c)
                        pe.matmul(bank[:, b, :], qT[cc, hd, t * P:(t + 1) * P], kT[cc, hd, 0:BANK],
                                  start=True, stop=True)
                        pe.matmul(bank[:, b + 1, 0:TM - BANK], qT[cc, hd, t * P:(t + 1) * P],
                                  kT[cc, hd, BANK:TM], start=True, stop=True).then_inc(scored, 1)
                if 2 <= r <= len(turns) + 1:
                    e = r - 2
                    pe.wait_ge(diffed, e + 1)
                    pe.wait_ge(aT_ready, e)
                    pe.transpose(bank[0:META, M_BANK, 0:P], a[:, e % 2, 0:META], ident)
                    for kt in range(NT):
                        last = pe.transpose(bank[:, W_BANK + e % 2, kt * P:(kt + 1) * P],
                                            a[:, e % 2, META + kt * P:META + (kt + 1) * P], ident)
                    last.then_inc(a_turned, 1)
                if r >= 3:
                    e = r - 3
                    hd = turns[e][0]
                    pe.wait_ge(aT_ready, e + 1)
                    if e:
                        pe.wait_ge(o_taken, e)
                    o = bank[:, O_BANK, 0:DA_V]
                    pe.matmul(o, aTm[:, e % 2, :], vm[:, hd * DA_V:(hd + 1) * DA_V], start=True, stop=False)
                    for kt in range(NT):
                        last = pe.matmul(o, aT[:, e % 2, kt * P:(kt + 1) * P],
                                         v[:, kt, hd * DA_V:(hd + 1) * DA_V], start=False, stop=kt == NT - 1)
                    last.then_inc(o_done, 1)

        @block.vector
        def _(dve):
            chain = Chain(dve, vec)

            def rotate(rows, t0, t1, n):
                x1, x2 = rows[:, :, :, 0:HALF], rows[:, :, :, HALF:ROPE]
                cos, sin = angles("cos", t0, t1, n), angles("sin", t0, t1, n)
                w = (t1 - t0) * 8 * HALF
                r = [rot[0:n, i, 0:w].rearrange("p (t h c) -> p t h c", h=8, c=HALF) for i in range(4)]
                dve.tensor_tensor(r[0], x1, cos, ALU.mult)
                dve.tensor_tensor(r[1], x2, sin, ALU.mult)
                dve.tensor_tensor(r[2], x2, cos, ALU.mult)
                chain(dve.tensor_tensor(r[3], x1, sin, ALU.mult))
                dve.tensor_tensor(x1, r[0], r[1], ALU.subtract)
                return dve.tensor_tensor(x2, r[2], r[3], ALU.add)

            def split(ap):
                return ap.rearrange("p t (h c) -> p t h c", h=8)

            ins = rotate(split(q[:, :, :]), 0, NT, P)
            ins.then_inc(turned_q, 1)
            dve.wait_ge(turned_q, 1)
            ins = rotate(split(k[:, :, :]), 0, NT, P)
            ins.then_inc(turned_k, 1)
            dve.wait_ge(turned_k, 1)
            ins = rotate(km[:, :].rearrange("p (t h c) -> p t h c", t=1, h=8), NT, NT + 1, META)
            ins.then_inc(turned_k, 1)
            dve.wait_ge(in_landed, 16 * 5)
            for n in range(2):
                chain(dve.tensor_tensor(lam_prod[:, n, :], lam_in[:, 2 * n, :], lam_in[:, 2 * n + 1, :], ALU.mult))
            dve.tensor_reduce(lam_sum[:, :], lam_prod[:, :, :], AX.X, ALU.add).then_inc(lam_done, 1)
            chain(dve.tensor_scalar(sub_w[:, :], sub_w[:, :], 1.0 - LAM_INIT, None, ALU.mult))
            dve.wait_ge(lam_exp, 1)
            chain(dve.tensor_tensor(lam[:, 0:1], lam[:, 1:2], lam[:, 0:1], ALU.subtract))
            chain(dve.tensor_scalar(lam[:, 0:1], lam[:, 0:1], -LAM_INIT, None, ALU.add))

            for hd in range(DA_HEADS):
                dve.wait_ge(tp, hd + 1)
                dve.tensor_scalar(qT[:, hd, :], bank[:, hd % 4, :], DA_DIM ** -0.5, None, ALU.mult)\
                    .then_inc(cols_ready, 1)
            for hd in range(DA_HEADS):
                dve.wait_ge(tp, DA_HEADS + hd + 1)
                dve.tensor_copy(kT[:, hd, META:TM], bank[:, hd % 4, :]).then_inc(cols_ready, 1)
            dve.wait_ge(tp, 2 * DA_HEADS + 1)
            dve.tensor_copy(kT[:, :, 0:META],
                            bank[:, 4, 0:DA_HEADS * META].rearrange("p (h m) -> p h m", m=META))\
                .then_inc(cols_ready, 1)

            def take_output(e):
                hd, t = turns[e]
                dve.wait_ge(o_done, e + 1)
                dve.tensor_copy(mix[:, t, hd * DA_V:(hd + 1) * DA_V], bank[:, O_BANK, 0:DA_V])\
                    .then_inc(o_taken, 1)

            def maximum(r, c):
                u = 2 * r + c
                dve.wait_ge(scored, u + 1)
                if u >= 4:
                    dve.wait_ge(exped, u - 3)
                dve.tensor_reduce(nmax[:, u % 4:u % 4 + 1], scores_of(r, c), AX.X, ALU.max, negate=True)\
                    .then_inc(maxed, 1)

            for r in range(len(turns) + 4):
                if r >= 4:
                    take_output(r - 4)
                if r < len(turns):
                    maximum(r, 0)
                if 1 <= r <= len(turns):
                    e = r - 1
                    o = 2 * (e % 2)
                    dve.wait_ge(exped, 2 * e + 2)
                    if e >= 2:
                        dve.wait_ge(a_turned, e - 1)
                    chain(dve.reciprocal(inv[:, o:o + 2], total[:, o:o + 2]))
                    dve.tensor_scalar(a[:, e % 2, :], p[:, e % 2, 0, :], inv[:, o:o + 1], None, ALU.mult)
                    chain(dve.tensor_tensor(inv[:, o + 1:o + 2], inv[:, o + 1:o + 2], lam[:, 0:1], ALU.mult))
                    dve.scalar_tensor_tensor(a[:, e % 2, :], p[:, e % 2, 1, :], inv[:, o + 1:o + 2],
                                             a[:, e % 2, :], ALU.mult, ALU.add).then_inc(diffed, 1)
                if r < len(turns):
                    maximum(r, 1)
            dve.wait_ge(squared, 1)
            chain(dve.tensor_reduce(ss[:, :], sq[:, :, :], AX.X, ALU.add))
            dve.tensor_scalar(ss[:, :], ss[:, :], 1.0 / DA_V, EPS, ALU.mult, ALU.add).then_inc(ms, 1)
            dve.wait_ge(rooted, 1)
            chain(dve.reciprocal(root[:, :], root[:, :]))
            for t in range(NT):
                for hd in range(DA_HEADS):
                    o = mix[:, t, hd * DA_V:(hd + 1) * DA_V]
                    n = t * DA_HEADS + hd
                    dve.scalar_tensor_tensor(o, o, root[:, n:n + 1], sub_w[:, :], ALU.mult, ALU.mult)



def phase_linear_attention(nc, bank, const, io, life):
    with ExitStack() as ctx:
        s = Scope(nc, ctx, "gla")
        qk, zT, gv, gvm, gr, mix = (life[n] for n in ("gqk", "zT", "gv", "gv_m", "gr", "mix"))
        FW, BW = 0, 1
        GK = GLA_HEADS * GLA_DK
        w2 = s.sb("w2", [P, 2 * GK])
        w2_bias = s.sb("w2_bias", [P, 2 * GK])
        norm_w = s.sb("norm_w", [P, GLA_DV])
        y, e = s.sb("y", [P, NT + 1, 2 * GK]), s.sb("e", [P, NT + 1, 2 * GK])
        grow, shrink = life["q"], life["k"]
        qs, ks = s.sb("qs", [P, 4, T]), s.sb("ks", [P, 4, T])
        mid, decay = s.sb("mid", [P, 4, NCHUNK]), s.sb("decay", [P, 4, NCHUNK])
        decay_m = s.sb("decay_m", [P, 2])
        km, kmT = s.sb("km", [P, 2, META]), s.sb("kmT", [META, GK])
        ksT = s.sb("ksT", [P, 4, NT, P])
        at = s.sb("at", [P, 2, NT, GLA_HEADS * P])
        kv = s.sb("kv", [P, 4, NCHUNK, GLA_DV])
        st = s.sb("st", [P, 4, NCHUNK, GLA_DV])
        sq = kv[:, 0:2, :, :].rearrange("p g c v -> p (g c) v")
        gate = gr
        ss = s.sb("ss", [P, NT * GLA_HEADS])
        names = ("w2_landed", "zeroed", "z_done", "y_done", "e_done", "ln_done", "lg_done", "b_done", "grown",
                 "qk_done", "mid_taken", "decay_sum", "decayed", "km_done", "k_turned", "k_taken", "a_done",
                 "a_taken", "kv_done", "kv_taken", "states", "o_done", "o_taken", "squared", "mean", "rooted",
                 "gated", "vector_steps")
        S = {n: s.sem(n) for n in names}
        ident = const[:, CONSTS["ident"][0]:CONSTS["ident"][1]]

        def c(name, n=P):
            return const[0:n, CONSTS[name][0]:CONSTS[name][1]]

        sums = [c("sum_f"), c("sum_b")]
        rows96 = slice(96, 96 + 2 * RANK)
        tiles = [(t, P) for t in range(NT)] + [(NT, META)]
        block = s.block()

        @block.sync
        def _(sp):
            sp.wait_ge(S["zeroed"], 1)
            sp.dma_start(w2[96:96 + RANK, 0:GK], io["gla_gate_w2_f"]).then_inc(S["w2_landed"], 16)
            sp.dma_start(w2[96 + RANK:P, GK:2 * GK], io["gla_gate_w2_b"]).then_inc(S["w2_landed"], 16)
            sp.dma_start(w2_bias[:, 0:GK], io["gla_gate_b_f"].to_broadcast([P, GK])).then_inc(S["w2_landed"], 16)
            sp.dma_start(w2_bias[:, GK:2 * GK], io["gla_gate_b_b"].to_broadcast([P, GK]))\
                .then_inc(S["w2_landed"], 16)
            sp.dma_start(norm_w[:, :], io["gla_norm_w"].to_broadcast([P, GLA_DV])).then_inc(S["w2_landed"], 16)

        @block.tensor
        def _(pe):
            pe.wait_ge(S["w2_landed"], 16 * 5)
            for t, n in tiles:
                cols = slice(META + t * P, META + (t + 1) * P) if t < NT else slice(0, META)
                pe.matmul(bank[0:n, t, :], zT[rows96, 0, cols], w2[rows96, :], start=True, stop=True)\
                    .then_inc(S["z_done"], 1)
            pe.wait_ge(S["lg_done"], 2)
            for g in range(4):
                for t in range(NT):
                    lg = y[:, t, g * P:(g + 1) * P]
                    last = pe.matmul(bank[:, g, t * P:(t + 1) * P], lg, sums[g // 2][:, 0:P], start=True, stop=True)
                last.then_inc(S["b_done"], 1)
            for g in range(4):
                for t in range(NT):
                    lg = y[:, t, g * P:(g + 1) * P]
                    pe.matmul(bank[:, 5, 2 * (g * NT + t):2 * (g * NT + t) + 2], lg, sums[g // 2][:, P:P + 2],
                              start=True, stop=True)
            for m in range(2):
                last = pe.matmul(bank[:, 5, 64 + m * META:64 + (m + 1) * META], y[0:META, NT, m * P:(m + 1) * P],
                                 c("sum_m", META), start=True, stop=True)
            last.then_inc(S["b_done"], 1)
            for g in range(4):
                pe.wait_ge(S["qk_done"], g + 1)
                if g >= 2:
                    pe.wait_ge(S["k_taken"], g - 1)
                for t in range(NT):
                    last = pe.transpose(bank[:, 6 + g % 2, t * P:(t + 1) * P], ks[:, g, t * P:(t + 1) * P], ident)
                last.then_inc(S["k_turned"], 1)
            pe.wait_ge(S["km_done"], 1)
            pe.wait_ge(S["k_taken"], 4)
            for m in range(2):
                last = pe.transpose(bank[0:META, 6, m * P:(m + 1) * P], km[:, m, :], ident)
            last.then_inc(S["k_turned"], 1)
            for t in range(NT):
                if t == 0:
                    pe.wait_ge(S["grown"], 5)
                    pe.wait_ge(S["mid_taken"], 2)
                else:
                    pe.wait_ge(S["a_taken"], t)
                for d in range(2):
                    for hd in range(GLA_HEADS):
                        g, hp = 2 * d + hd // 2, hd % 2
                        r = slice(hp * GLA_DK, (hp + 1) * GLA_DK)
                        last = pe.matmul(bank[:, 2 * d + hp, (hd // 2) * P:(hd // 2 + 1) * P],
                                         ks[r, g, t * P:(t + 1) * P], qs[r, g, t * P:(t + 1) * P],
                                         start=True, stop=True)
                last.then_inc(S["a_done"], 1)
            pe.wait_ge(S["k_taken"], 5)
            for hd in range(GLA_HEADS):
                out = bank[(hd % 2) * GLA_DK:(hd % 2 + 1) * GLA_DK, 7, (hd // 2) * GLA_DV:(hd // 2 + 1) * GLA_DV]
                last = pe.matmul(out, kmT[:, hd * GLA_DK:(hd + 1) * GLA_DK],
                                 gvm[:, hd * GLA_DV:(hd + 1) * GLA_DV], start=True, stop=True)
            last.then_inc(S["kv_done"], 1)
            pe.wait_ge(S["a_taken"], NT)
            for d in range(2):
                for cp in range(2):
                    for half in range(2):
                        n = (d * 2 + cp) * 2 + half
                        b = n % 4
                        if n >= 4:
                            pe.wait_ge(S["kv_taken"], 1 + n - 3)
                        for i in range(2):
                            t = 2 * half + i
                            r = slice(cp * CHUNK, (cp + 1) * CHUNK)
                            for hd in range(GLA_HEADS):
                                m, hp = hd // 2, hd % 2
                                out = bank[hp * GLA_DK:(hp + 1) * GLA_DK, b,
                                           (i * 2 + m) * GLA_DV:(i * 2 + m + 1) * GLA_DV]
                                last = pe.matmul(out, ksT[r, 2 * d + m, t, hp * GLA_DK:(hp + 1) * GLA_DK],
                                                 gv[r, t, hd * GLA_DV:(hd + 1) * GLA_DV], start=True, stop=True)
                        last.then_inc(S["kv_done"], 1)
            pe.wait_ge(S["kv_taken"], 9)
            pe.wait_ge(S["states"], 2)
            for t in range(NT):
                for hp in range(2):
                    b = (2 * t + hp) % NBANK
                    for m in range(2):
                        hd = 2 * m + hp
                        r = slice(hp * GLA_DK, (hp + 1) * GLA_DK)
                        cols = slice(m * GLA_DV, (m + 1) * GLA_DV)
                        pe.matmul(bank[:, b, cols], at[:, 0, t, (hp * 2 + m) * P:(hp * 2 + m + 1) * P],
                                  gv[:, t, hd * GLA_DV:(hd + 1) * GLA_DV], start=True, stop=False,
                                  skip_group_check=True)
                        for cp in range(2):
                            ch = 2 * t + cp
                            out = bank[cp * CHUNK:(cp + 1) * CHUNK, b, cols]
                            toks = slice(ch * CHUNK, (ch + 1) * CHUNK)
                            for d in range(2):
                                if d == BW and ch == NCHUNK - 1:
                                    continue
                                last = pe.matmul(out, qs[r, 2 * d + m, toks], st[r, 2 * d + m, ch, :],
                                                 start=False, stop=True, skip_group_check=True)
                    last.then_inc(S["o_done"], 1)

        @block.scalar
        def _(act):
            act.activation(gate[:, :, :], gr[:, :, :], ACT.Silu).then_inc(S["gated"], 1)
            for i, (n, ts) in enumerate(((P, slice(0, NT)), (META, slice(NT, NT + 1)))):
                act.wait_ge(S["y_done"], i + 1)
                act.activation(e[0:n, ts, :], e[0:n, ts, :], ACT.Exp, scale=-1.0).then_inc(S["e_done"], 1)
            for i, (n, ts) in enumerate(((P, slice(0, NT)), (META, slice(NT, NT + 1)))):
                act.wait_ge(S["e_done"], i + 1)
                act.activation(e[0:n, ts, :], e[0:n, ts, :], ACT.Ln, bias=1.0).then_inc(S["ln_done"], 1)
            for g in range(4):
                act.wait_ge(S["b_done"], g + 1)
                act.activation(grow[:, g, :], bank[:, g, :], ACT.Exp)
                act.activation(shrink[:, g, :], bank[:, g, :], ACT.Exp, scale=-1.0).then_inc(S["grown"], 1)
            act.wait_ge(S["b_done"], 5)
            act.activation(km[:, :, :], bank[:, 5, 64:64 + 2 * META].rearrange("p (m c) -> p m c", m=2), ACT.Exp,
                           scale=-1.0).then_inc(S["grown"], 1)
            act.wait_ge(S["decay_sum"], 1)
            act.activation(decay[:, :, :], decay[:, :, :], ACT.Exp)
            act.activation(decay_m[:, :], decay_m[:, :], ACT.Exp).then_inc(S["decayed"], 1)
            for g in range(4):
                act.wait_ge(S["k_turned"], g + 1)
                act.activation(ksT[:, g, :, :].rearrange("p t c -> p (t c)"), bank[:, 6 + g % 2, :], ACT.Copy)\
                    .then_inc(S["k_taken"], 1)
            act.wait_ge(S["k_turned"], 5)
            act.activation(kmT[:, :], bank[0:META, 6, 0:GK], ACT.Copy).then_inc(S["k_taken"], 1)
            act.wait_ge(S["decayed"], 1)
            act.wait_ge(S["kv_done"], 1)
            for m in range(2):
                last = act.activation(st[:, m, 0, :], bank[:, 7, m * GLA_DV:(m + 1) * GLA_DV], ACT.Copy,
                                      scale=decay_m[:, m:m + 1])
            last.then_inc(S["kv_taken"], 1)
            for d in range(2):
                for cp in range(2):
                    for half in range(2):
                        n = (d * 2 + cp) * 2 + half
                        act.wait_ge(S["kv_done"], n + 2)
                        for i in range(2):
                            for m in range(2):
                                g, ch = 2 * d + m, 2 * (2 * half + i) + cp
                                last = act.activation(kv[:, g, ch, :],
                                                      bank[:, n % 4, (i * 2 + m) * GLA_DV:(i * 2 + m + 1) * GLA_DV],
                                                      ACT.Copy, scale=decay[:, g, ch:ch + 1])
                        last.then_inc(S["kv_taken"], 1)
            act.wait_ge(S["o_taken"], 2 * NT)
            act.activation(sq.rearrange("p (t h) v -> p t h v", t=NT),
                           mix[:, :, 512:1024].rearrange("p t (h v) -> p t h v", h=GLA_HEADS),
                           ACT.Square).then_inc(S["squared"], 1)
            act.wait_ge(S["mean"], 1)
            act.activation(ss[:, :], ss[:, :], ACT.Sqrt).then_inc(S["rooted"], 1)

        @block.vector
        def _(dve):
            chain = Chain(dve, S["vector_steps"])
            dve.memset(w2[96:P, :], 0.0).then_inc(S["zeroed"], 1)
            dve.wait_ge(S["w2_landed"], 16 * 5)
            for t, n in tiles:
                dve.wait_ge(S["z_done"], t + 1)
                last = dve.tensor_tensor(y[0:n, t, :], bank[0:n, t, :], w2_bias[0:n, :], ALU.add)
            chain(last)
            groups = ((P, slice(0, NT)), (META, slice(NT, NT + 1)))
            for n, ts in groups:
                dve.scalar_tensor_tensor(e[0:n, ts, :], y[0:n, ts, :], -1.0, y[0:n, ts, :], ALU.mult, ALU.max)\
                    .then_inc(S["y_done"], 1)
            for i, (n, ts) in enumerate(groups):
                dve.wait_ge(S["ln_done"], i + 1)
                dve.scalar_tensor_tensor(y[0:n, ts, :], y[0:n, ts, :], 0.0, e[0:n, ts, :], ALU.min, ALU.subtract)\
                    .then_inc(S["lg_done"], 1)
            for g in range(4):
                m = g % 2
                dve.wait_ge(S["grown"], g + 1)
                dve.scalar_tensor_tensor(qs[:, g, :], qk[:, m, META:TM], GLA_DK ** -0.5, grow[:, g, :],
                                         ALU.mult, ALU.mult)
                dve.tensor_tensor(ks[:, g, :], qk[:, 2 + m, META:TM], shrink[:, g, :], ALU.mult)\
                    .then_inc(S["qk_done"], 1)
            dve.wait_ge(S["grown"], 5)
            dve.tensor_tensor(km[:, :, :], km[:, :, :], qk[:, 2:4, 0:META], ALU.mult).then_inc(S["km_done"], 1)
            dve.wait_ge(S["b_done"], 5)
            dve.tensor_copy(mid[:, :, :], bank[:, 5, 0:4 * NCHUNK].rearrange("p (g c) -> p g c", g=4))\
                .then_inc(S["mid_taken"], 1)
            dve.wait_ge(S["mid_taken"], 1)
            dve.tensor_copy(decay_m[:, :], mid[:, 0:2, 0])
            ends = [bank[:, g, :].rearrange("p (c i) -> p c i", i=CHUNK)[:, :, CHUNK - 1 if g < 2 else 0]
                    for g in range(4)]
            for g in range(4):
                if g < 2:
                    dve.tensor_tensor(decay[:, g, 0:NCHUNK - 1], ends[g][:, 0:NCHUNK - 1], mid[:, g, 1:NCHUNK], ALU.add)
                    last = dve.tensor_copy(decay[:, g, NCHUNK - 1:NCHUNK], ends[g][:, NCHUNK - 1:NCHUNK])
                else:
                    dve.tensor_tensor(decay[:, g, 1:NCHUNK], ends[g][:, 1:NCHUNK], mid[:, g, 0:NCHUNK - 1], ALU.add)
                    last = dve.tensor_copy(decay[:, g, 0:1], ends[g][:, 0:1])
            last.then_inc(S["mid_taken"], 1)
            dve.wait_ge(S["mid_taken"], 2)
            dve.sem_inc(S["decay_sum"], 1)
            for t in range(NT):
                dve.wait_ge(S["a_done"], t + 1)
                for d, keep in ((FW, c("keep_f")), (BW, c("keep_b"))):
                    last = dve.tensor_tensor(
                        at[:, d, t, :].rearrange("p (b n) -> p b n", b=2), bank[:, 2 * d:2 * d + 2, 0:2 * P],
                        keep.rearrange("p (b n) -> p b n", b=2), ALU.mult)
                last.then_inc(S["a_taken"], 1)
                dve.wait_ge(S["a_taken"], t + 1)
                last = dve.tensor_tensor(at[:, 0, t, :], at[:, 0, t, :], at[:, 1, t, :], ALU.add)
            chain(last)
            dve.wait_ge(S["kv_taken"], 1)
            dve.wait_ge(S["decayed"], 1)
            for i in range(NCHUNK - 1):
                f, b = i, NCHUNK - 1 - i
                if i == 0:
                    dve.wait_ge(S["kv_taken"], 9)
                for m in range(2):
                    last = dve.scalar_tensor_tensor(st[:, m, f + 1, :], st[:, m, f, :], decay[:, m, f:f + 1],
                                                    kv[:, m, f, :], ALU.mult, ALU.add)
                for m in range(2, 4):
                    if i == 0:
                        last = dve.tensor_copy(st[:, m, b - 1, :], kv[:, m, b, :])
                    else:
                        last = dve.scalar_tensor_tensor(st[:, m, b - 1, :], st[:, m, b, :], decay[:, m, b:b + 1],
                                                        kv[:, m, b, :], ALU.mult, ALU.add)
                chain(last)
            dve.sem_inc(S["states"], 2)
            for t in range(NT):
                for hp in range(2):
                    dve.wait_ge(S["o_done"], 2 * t + hp + 1)
                    out = mix[:, t, 512:1024].rearrange("p (m hp v) -> p m hp v", m=2, hp=2)[:, :, hp, :]
                    dve.tensor_copy(out, bank[:, 2 * t + hp, 0:2 * GLA_DV].rearrange("p (m v) -> p m v", m=2))\
                        .then_inc(S["o_taken"], 1)
            dve.wait_ge(S["squared"], 1)
            chain(dve.tensor_reduce(ss[:, :], sq, AX.X, ALU.add))
            dve.tensor_scalar(ss[:, :], ss[:, :], 1.0 / GLA_DV, EPS, ALU.mult, ALU.add).then_inc(S["mean"], 1)
            dve.wait_ge(S["rooted"], 1)
            chain(dve.reciprocal(ss[:, :], ss[:, :]))
            for t in range(NT):
                for hd in range(GLA_HEADS):
                    o = mix[:, t, 512 + hd * GLA_DV:512 + (hd + 1) * GLA_DV]
                    n = t * GLA_HEADS + hd
                    last = dve.scalar_tensor_tensor(o, o, ss[:, n:n + 1], norm_w[:, :], ALU.mult, ALU.mult)
            chain(last)
            dve.wait_ge(S["gated"], 1)
            dve.tensor_tensor(mix[:, :, 512:1024], mix[:, :, 512:1024], gate[:, :, :], ALU.mult)


class TurnColumns:

    def __init__(self, s, rows, hi, lo, ident, bank, name="t_"):
        self.rows, self.hi, self.lo, self.ident, self.bank = rows, hi, lo, ident, bank
        self.tiles = rows.shape[2] // P
        self.turned, self.hi_done, self.done = s.sem(name + "turned"), s.sem(name + "hi"), s.sem(name + "done")

    def on_tensor(self, pe):
        for k in range(self.tiles):
            for t in range(NT):
                last = pe.transpose(self.bank[:, k, t * P:(t + 1) * P], self.rows[:, t, k * P:(k + 1) * P],
                                    self.ident)
            last.then_inc(self.turned, 1)

    def on_scalar(self, act):
        for k in range(self.tiles):
            act.wait_ge(self.turned, k + 1)
            act.activation(self.hi[:, k, :], self.bank[:, k, :], ACT.Copy).then_inc(self.hi_done, 1)

    def on_vector(self, dve):
        for k in range(self.tiles):
            dve.wait_ge(self.hi_done, k + 1)
            dve.tensor_tensor(self.lo[:, k, :], self.bank[:, k, :], self.hi[:, k, :].bitcast(F32), ALU.subtract)\
                .then_inc(self.done, 1)


PEER_H, PEER_KEYS, PEER_K = 8, 128, 16
HP = 2 * PEER_H



def phase_mix_out(nc, bank, const, io, life):
    with ExitStack() as ctx:
        s = Scope(nc, ctx, "mo")
        mix, h = life["mix"], life["h"]
        xh, xl = s.sb("xh", [P, KD, T], F32R), s.sb("xl", [P, KD, T], F32R)
        x_in = s.sb("x_in", [P, NT, D])
        ring = WeightRing(s)
        gemm = Gemm(s, ring, bank)
        x_landed, stored, done = s.sem("x_landed"), s.sem("stored"), s.sem("h_done")
        ident = const[:, CONSTS["ident"][0]:CONSTS["ident"][1]]
        turn = TurnColumns(s, mix, xh, xl, ident, bank)

        def part(c0):
            return dict(kind="rows", slab=lambda i, _: weight_slab(io["w_out"], i, c0), width=BANK, ktiles=KD,
                        x=lambda kt, m: (xh[:, kt, m * P:(m + 1) * P], xl[:, kt, m * P:(m + 1) * P]),
                        meta=False, c0=c0)

        blocks = gemm.plan([part(0), part(BANK)])
        block = s.block()

        @block.sync
        def _(sp):
            sp.dma_start(x_in[:, :, :], io["x"].rearrange("(t p) d -> p t d", p=P)).then_inc(x_landed, 16)
            for b in blocks:
                gemm.on_sync(sp, b)
            sp.wait_ge(done, 1)
            sp.dma_start(io["h1"].rearrange("(t p) d -> p t d", p=P), h[:, :, :]).then_inc(stored, 16)
            sp.wait_ge(stored, 16)

        @block.gpsimd
        def _(pool):
            ring.open_raw(pool)
            for b in blocks:
                gemm.on_gpsimd(pool, b)

        @block.scalar
        def _(act):
            turn.on_scalar(act)
            for b in blocks:
                gemm.on_scalar(act, b)

        @block.tensor
        def _(pe):
            ring.open_slots(pe)
            turn.on_tensor(pe)
            pe.wait_ge(turn.done, KD)
            for b in blocks:
                gemm.on_tensor(pe, b)

        @block.vector
        def _(dve):
            gemm.open_banks(dve)
            turn.on_vector(dve)
            dve.wait_ge(x_landed, 16)
            for b in blocks:
                gemm.take(dve, b, lambda j, m, got: dve.tensor_tensor(
                    h[:, m, b["c0"]:b["c0"] + BANK], got, x_in[:, m, b["c0"]:b["c0"] + BANK], ALU.add))
            dve.wait_ge(gemm.bank_free, NBANK + gemm.tile0)
            dve.sem_inc(done, 1)



def phase_peer_pick(nc, bank, const, io, life):
    with ExitStack() as ctx:
        s = Scope(nc, ctx, "pp")
        h = life["h"]
        K, H, B = PEER_K, PEER_H, HP // 4
        G = NT * 2
        xh, xl = s.sb("xh", [P, KD, T], F32R), s.sb("xl", [P, KD, T], F32R)
        gain = s.sb("gain", [P, KD])
        keys = s.sb("keys", [P, HP, PEER_KEYS])
        qT = s.sb("qT", [P, 4, T])
        sc = s.sb("sc", [P, 2, NT * 4, PEER_KEYS])
        ts, ti = s.sb("ts", [P, NT * 4, K]), s.sb("ti", [P, NT * 4, K], U32)
        tif = s.sb("tif", [P, 2, NT * 4, K])
        cand = s.sb("cand", [P, G, K, K])
        bs, bp = s.sb("bs", [P, 2, G, K]), s.sb("bp", [P, G, K], U32)
        place = s.sb("place", [P, 2, G, K], U32)
        placef = s.sb("placef", [P, 2, G, K])
        hot = s.sb("hot", [P, 2, G, K, K])
        tsum = s.sb("tsum", [P, G])
        pick = s.sb("pick", [P, NT, 3, P])
        ring = WeightRing(s)
        gemm = Gemm(s, ring, bank)
        names = ("stored", "scored", "score_taken", "vector_steps", "sc_used", "shifted", "exped", "hot_done",
                 "hot_scaled", "picked", "turned")
        S = {n: s.sem(n) for n in names}
        gain_landed, keys_landed = s.sem("gain_landed"), s.sem("keys_landed")
        ident = const[:, CONSTS["ident"][0]:CONSTS["ident"][1]]
        iota = const[:, CONSTS["iota"][0]:CONSTS["iota"][0] + K]
        norm = NormColumns(s, h, None, gain, xh, xl, ident, bank)

        def part(b):
            return dict(kind="columns", width=BANK, ktiles=KD, meta=False,
                        slab=lambda i, _: weight_slab(io["peer_w_q"], i, b * BANK),
                        x=lambda kt, m: (xh[:, kt, :], xl[:, kt, :]))

        blocks = gemm.plan([part(b) for b in range(B)])
        block = s.block()

        @block.sync
        def _(sp):
            sp.dma_start(gain[:, :], io["ln2_w"]).then_inc(gain_landed, 16)
            sp.dma_start(keys[:, :, :], io["peer_keys"]).then_inc(keys_landed, 16)
            for n, b in enumerate(blocks):
                gemm.on_sync(sp, b)
                if n == 0:
                    sp.wait_ge(norm.done, norm.total())
                    sp.dma_start(io["hn_hi"], xh[:, :, :].bitcast(F32)).then_inc(S["stored"], 16)
                    sp.dma_start(io["hn_lo"], xl[:, :, :].bitcast(F32)).then_inc(S["stored"], 16)
            sp.wait_ge(S["stored"], 32)

        @block.gpsimd
        def _(pool):
            ring.open_raw(pool)

            def key_rows(b):
                pool.wait_ge(S["hot_done"], b + 1)
                for j in range(2):
                    key = tif[:, b % 2, :, :].rearrange("p (g two) k -> p g two k", two=2)[:, :, j, :]
                    pool.tensor_tensor(hot[:, j, :, :, :], hot[:, j, :, :, :],
                                       key.unsqueeze(2).to_broadcast([P, G, K, K]), ALU.mult)\
                        .then_inc(S["hot_scaled"], 1)

            gemm.on_gpsimd(pool, blocks[0])
            for n in range(1, B):
                gemm.on_gpsimd(pool, blocks[n])
                key_rows(n - 1)
            key_rows(B - 1)

        @block.scalar
        def _(act):
            act.wait_ge(gain_landed, 16)
            gemm.open_banks(act)
            norm.on_scalar(act, lambda e, t: None)
            gemm.on_scalar(act, blocks[0], 0, AHEAD)

            def exp(b):
                act.wait_ge(S["shifted"], b + 1)
                act.activation(bs[:, b % 2, :, :], bs[:, b % 2, :, :], ACT.Exp).then_inc(S["exped"], 1)

            for n, b in enumerate(blocks):
                gemm.on_scalar(act, b, 0, REST)
                if n + 1 < B:
                    gemm.on_scalar(act, blocks[n + 1], 0, AHEAD)
                if n:
                    act.wait_ge(S["scored"], NT * n)
                gemm.take(act, b, lambda j, m, got: act.activation(qT[:, m, :], got, ACT.Copy))
                if n >= 2:
                    act.wait_ge(S["sc_used"], n - 1)
                for t in range(NT):
                    act.wait_ge(S["scored"], NT * n + t + 1)
                    act.activation(sc[:, n % 2, 4 * t:4 * t + 4, :].rearrange("p a k -> p (a k)"),
                                   bank[:, 4 * (n % 2) + t, :], ACT.Copy).then_inc(S["score_taken"], 1)
                if n:
                    exp(n - 1)
            exp(B - 1)

        @block.tensor
        def _(pe):
            ring.open_slots(pe)
            norm.on_tensor(pe)
            pe.wait_ge(norm.done, norm.total())
            pe.wait_ge(keys_landed, 16)
            for n, b in enumerate(blocks):
                if n >= 2:
                    pe.wait_ge(S["score_taken"], NT * (n - 1))
                gemm.on_tensor(pe, b)
                pe.wait_ge(gemm.bank_free, NBANK + 4 * (n + 1))
                for t in range(NT):
                    for i in range(4):
                        last = pe.matmul(bank[:, 4 * (n % 2) + t, i * P:(i + 1) * P], qT[:, i, t * P:(t + 1) * P],
                                         keys[:, 4 * n + i, :], start=True, stop=True)
                    last.then_inc(S["scored"], 1)
            pe.wait_ge(S["score_taken"], NT * B)
            pe.wait_ge(S["picked"], B)
            for t in range(NT):
                for j in range(3):
                    last = pe.transpose(bank[:, j, t * P:(t + 1) * P], pick[:, t, j, :], ident)
            last.then_inc(S["turned"], 1)

        @block.vector
        def _(dve):
            chain = Chain(dve, S["vector_steps"])
            dve.wait_ge(gain_landed, 16)
            norm.on_vector(dve, chain)

            def best_16(groups, values, scores, index):
                for half in (slice(0, 8), slice(8, K)):
                    for g in range(groups):
                        last = dve.max(scores(g)[:, half], values(g))
                    chain(last)
                    for g in range(groups):
                        last = dve.max_index(index(g)[:, half], scores(g)[:, half], values(g))
                    chain(last)
                    if half.start == 0:
                        for g in range(groups):
                            last = dve.match_replace(values(g), scores(g)[:, half], values(g), NEG)
                        chain(last)

            def picks(b, j):
                return pick[:, :, j, 2 * b * K:2 * (b + 1) * K]

            def finish(b):
                dve.wait_ge(S["hot_scaled"], 2 * b + 2)
                for j in range(2):
                    dve.tensor_reduce(picks(b, j).rearrange("p t (h r) -> p t h r", h=2),
                                      hot[:, j, :, :, :].rearrange("p (t h) r k -> p t h r k", h=2), AX.X, ALU.add)
                gates = bs[:, b % 2, :, :]
                dve.wait_ge(S["exped"], b + 1)
                chain(dve.tensor_reduce(tsum[:, :], gates, AX.X, ALU.add))
                chain(dve.reciprocal(tsum[:, :], tsum[:, :]))
                dve.tensor_tensor(picks(b, 2).rearrange("p t (h r) -> p t h r", h=2),
                                  gates.rearrange("p (t h) r -> p t h r", h=2),
                                  tsum[:, :].rearrange("p (t h) -> p t h", h=2).unsqueeze(3)
                                  .to_broadcast([P, NT, 2, K]), ALU.mult).then_inc(S["picked"], 1)
                dve.wait_ge(S["picked"], b + 1)

            for b in range(B):
                values, best = sc[:, b % 2, :, :], bs[:, b % 2, :, :]
                dve.wait_ge(S["score_taken"], NT * (b + 1))
                best_16(NT * 4, lambda g: values[:, g, :], lambda g: ts[:, g, :], lambda g: ti[:, g, :])
                dve.sem_inc(S["sc_used"], 1)
                chain(dve.tensor_copy(tif[:, b % 2, :, :], ti[:, :, :]))
                if b:
                    finish(b - 1)
                pair = ts[:, :, :].rearrange("p (g two) k -> p g two k", two=2)
                chain(dve.tensor_tensor(cand[:, :, :, :], pair[:, :, 0, :].unsqueeze(3).to_broadcast([P, G, K, K]),
                                        pair[:, :, 1, :].unsqueeze(2).to_broadcast([P, G, K, K]), ALU.add))
                best_16(G, lambda g: cand[:, g, :, :].rearrange("p a b -> p (a b)"), lambda g: best[:, g, :],
                        lambda g: bp[:, g, :])
                chain(dve.tensor_copy(tsum[:, :], best[:, :, 0]))
                dve.tensor_tensor(best, best, tsum[:, :].unsqueeze(2).to_broadcast([P, G, K]), ALU.subtract)\
                    .then_inc(S["shifted"], 1)
                dve.tensor_single_scalar(place[:, 0, :, :], bp[:, :, :], 4, ALU.logical_shift_right)
                chain(dve.tensor_single_scalar(place[:, 1, :, :], bp[:, :, :], K - 1, ALU.bitwise_and))
                chain(dve.tensor_copy(placef[:, :, :, :], place[:, :, :, :]))
                for j in range(2):
                    last = dve.tensor_tensor(
                        hot[:, j, :, :, :].rearrange("p h r k -> p (h r) k"),
                        iota.unsqueeze(1).to_broadcast([P, G * K, K]),
                        placef[:, j, :, :].rearrange("p h r -> p (h r)").unsqueeze(2).to_broadcast([P, G * K, K]),
                        ALU.is_equal)
                last.then_inc(S["hot_done"], 1)
            finish(B - 1)
            dve.wait_ge(S["turned"], 1)
            dve.tensor_copy(life["pick_keys"][:, :, :], bank[:, 0:2, :])
            left, parts = cand[:, :, :, :].rearrange("p h r k -> p (h r k)")[:, 0:T], life["pick_gates"]
            chain(dve.tensor_copy(left, bank[:, 2, :]))
            for n in range(3):
                chain(dve.tensor_copy(parts[:, :, n], left))
                if n < 2:
                    chain(dve.tensor_tensor(left, left, parts[:, :, n], ALU.subtract))



SWEEPS = 2
ST = T // SWEEPS
ROUND = 32
ROUNDS = PEER_KEYS // ROUND
GROUP = ST // ROUND
HALF_GROUP = GROUP // 2
FIRST = ROUND // 4
RAW = 4
PARTS = 3


def phase_peer_experts(nc, bank, io, life):
    with ExitStack() as ctx:
        s = Scope(nc, ctx, "pe")
        keys, parts = life["pick_keys"], life["pick_gates"]
        iota = s.sb("iota", [P, P])
        counting = s.sb("counting", [P, P], BF16)
        zero = s.sb("zero", [P, P], F32R)
        gates = [s.sb(f"gates{k}", [P, ROUND, ST]) for k in range(2)]
        xh, xl = s.sb("xh", [P, KD, T], F32R), s.sb("xl", [P, KD, T], F32R)
        u_raw, v_raw = s.sb("u_raw", [P, RAW, KD, P]), s.sb("v_raw", [P, RAW, D])
        uh, ul = s.sb("uh", [P, 2, KD, P], F32R), s.sb("ul", [P, 2, KD, P], F32R)
        vh, vl = s.sb("vh", [P, 2, D], F32R), s.sb("vl", [P, 2, D], F32R)
        hid = s.sb("hid", [P, 2, ST])
        hh, hl = s.sb("hh", [P, 2, ST], F32R), s.sb("hl", [P, 2, ST], F32R)
        eq1 = s.sb("eq1", [P, 2, GROUP, ROUND], BF16)
        hot1 = s.sb("hot1", [P, 2, GROUP, PARTS, ROUND], BF16)
        hot2 = s.sb("hot2", [P, 2, GROUP, P], BF16)
        out = s.sb("out", [P, 4, BANK])
        names = ("iota_landed", "x_landed", "u_hi", "u_lo", "v_hi", "v_lo", "a_done", "a_taken", "hid_ready",
                 "h_hi", "h_lo", "v_done", "eq1_ready", "hot1_ready", "hot2_ready", "hot_read", "first_taken",
                 "spread", "gates_taken", "zeroed", "out_done", "out_taken", "out_stored", "vector_steps")
        S = {n: s.sem(n) for n in names}
        u_landed = [s.sem(f"u_landed{k}") for k in range(RAW)]
        v_landed = [s.sem(f"v_landed{k}") for k in range(RAW)]
        A_BANK, G_BANK = 4, 6
        N = SWEEPS * PEER_KEYS
        block = s.block()


        def rounds(eng, body, at_round=None, at_sweep=None):
            for r in range(SWEEPS * ROUNDS):
                if at_round:
                    at_round(r)
                peel = r % ROUNDS == ROUNDS - 1
                turns = ROUND // RAW - peel
                with eng.Fori(0, turns) as i:
                    for c in range(RAW):
                        body(r, r * ROUND + c, i, c)
                if peel:
                    for c in range(RAW):
                        body(r, r * ROUND + turns * RAW + c, None, c)
                    if at_sweep:
                        at_sweep(r // ROUNDS)

        def at(n, i):
            return n if i is None else i * RAW + n

        def spread_here(r):
            return r < SWEEPS * ROUNDS - 1

        @block.sync
        def _(sp):
            sp.dma_start(iota[:, :], io["const"][:, CONSTS["iota"][0]:CONSTS["iota"][1]])\
                .then_inc(S["iota_landed"], 16)
            sp.dma_start(xh[:, :, :].bitcast(F32), io["hn_hi"]).then_inc(S["x_landed"], 16)
            sp.dma_start(xl[:, :, :].bitcast(F32), io["hn_lo"]).then_inc(S["x_landed"], 16)
            for sweep in range(SWEEPS):
                with sp.Fori(0, PEER_KEYS // RAW) as i:
                    for c in range(RAW):
                        q = at(sweep * PEER_KEYS + c, i)
                        sp.wait_ge(S["u_lo"], q + 1)
                        sp.dma_start(u_raw[:, c, :, :].rearrange("p k j -> p (k j)"),
                                     io["peer_u"][bass.ds(RAW * i + c, 1), :, :].rearrange("a p n -> p (a n)"))\
                            .then_inc(u_landed[c], 16)
                        sp.wait_ge(S["v_lo"], q + 1)
                        sp.dma_start(v_raw[:, c, :],
                                     io["peer_v"][bass.ds(RAW * i + c, 1), :, :].rearrange("a p n -> p (a n)"))\
                            .then_inc(v_landed[c], 16)

        @block.scalar
        def _(act):
            def split_u(n, i):
                turn = n // RAW if i is None else i + n // RAW
                act.wait_ge(u_landed[n % RAW], 16 * turn + 16)
                act.wait_ge(S["a_done"], at(n, i) + 1)
                act.activation(uh[:, n % 2, :, :], u_raw[:, n % RAW, :, :], ACT.Copy).then_inc(S["u_hi"], 1)

            def split_v(n, i):
                turn = n // RAW if i is None else i + n // RAW
                act.wait_ge(v_landed[n % RAW], 16 * turn + 16)
                act.wait_ge(S["v_done"], at(n, i) + 1)
                act.activation(vh[:, n % 2, :], v_raw[:, n % RAW, :], ACT.Copy).then_inc(S["v_hi"], 1)

            def take_gates(g, k):
                act.wait_ge(S["hot_read"], g + 3)
                act.activation(gates[0][:, :, bass.ds(g * GROUP, GROUP)].rearrange("p i n -> p n i"),
                               bank[:, G_BANK + k, 0:GROUP * ROUND].rearrange("p (n i) -> p n i", n=GROUP),
                               ACT.Copy).then_inc(S["first_taken"], 1)

            act.sem_inc(S["a_taken"], 2)
            act.sem_inc(S["first_taken"], 2)
            with act.Fori(0, FIRST) as i:
                for k in range(2):
                    take_gates(2 * i + k, k)
            split_u(0, None)
            split_u(1, None)
            split_v(0, None)
            with act.Fori(FIRST, ROUND // 2) as i:
                for k in range(2):
                    take_gates(2 * i + k, k)

            def body(r, n, i, c):
                q, k = at(n, i), c % 2
                act.wait_ge(S["a_done"], q + 3)
                act.wait_ge(S["h_lo"], q + 1)
                act.activation(hid[:, k, :], bank[:, A_BANK + k, 0:ST], ACT.Gelu).then_inc(S["a_taken"], 1)
                if i is not None or n + 2 < N:
                    split_u(n + 2, i)
                act.wait_ge(S["hid_ready"], q + 1)
                act.wait_ge(S["v_done"], q + 1)
                act.activation(hh[:, k, :], hid[:, k, :], ACT.Copy).then_inc(S["h_hi"], 1)
                if i is not None or n + 1 < N:
                    split_v(n + 1, i)

            rounds(act, body)

        @block.gpsimd
        def _(pool):
            pool.sem_inc(S["v_lo"], RAW)
            pool.sem_inc(S["hot1_ready"], 2)

            def split_v(n, i):
                pool.wait_ge(S["v_hi"], at(n, i) + 1)
                pool.tensor_tensor(vl[:, n % 2, :], v_raw[:, n % RAW, :], vh[:, n % 2, :].bitcast(F32),
                                   ALU.subtract).then_inc(S["v_lo"], 1)

            def times_gates(g, n0, k):
                pool.wait_ge(S["eq1_ready"], g + 1)
                pool.tensor_tensor(hot1[:, k, :, :, :],
                                   eq1[:, k, :, :].unsqueeze(2).to_broadcast([P, GROUP, PARTS, ROUND]),
                                   parts[:, bass.ds(n0, GROUP), :].unsqueeze(3)
                                   .to_broadcast([P, GROUP, PARTS, ROUND]), ALU.mult).then_inc(S["hot1_ready"], 1)

            with pool.Fori(0, FIRST) as i:
                for k in range(2):
                    times_gates(2 * i + k, (2 * i + k) * GROUP, k)
            split_v(0, None)
            with pool.Fori(FIRST, ROUND // 2) as i:
                for k in range(2):
                    times_gates(2 * i + k, (2 * i + k) * GROUP, k)

            def body(r, n, i, c):
                q = at(n, i)
                if spread_here(r):
                    times_gates(q + ROUND, (q - r * ROUND) * GROUP + (r + 1) // ROUNDS * ST, c % 2)
                if i is not None or n + 1 < N:
                    split_v(n + 1, i)

            def at_sweep(sweep):
                for m in range(2):
                    pool.wait_ge(S["out_taken"], 2 * sweep + m + 1)
                    pool.dma_start(io["experts"][(2 * sweep + m) * P:(2 * sweep + m + 1) * P, :]
                                   .rearrange("p (c n) -> p c n", c=2), out[:, 2 * m:2 * m + 2, :])\
                        .then_inc(S["out_stored"], 16)

            rounds(pool, body, None, at_sweep)
            pool.wait_ge(S["out_stored"], 16 * 2 * SWEEPS)

        @block.vector
        def _(dve):
            dve.sem_inc(S["u_lo"], RAW)
            dve.sem_inc(S["h_lo"], 2)
            dve.memset(zero[:, :].bitcast(F32), 0.0).then_inc(S["zeroed"], 1)
            dve.wait_ge(S["iota_landed"], 16)
            dve.tensor_copy(counting[:, :], iota[:, :]).then_inc(S["vector_steps"], 1)
            dve.wait_ge(S["vector_steps"], 1)

            def one_hots(r, g, n0, k):
                n = bass.ds(n0, GROUP)
                first = (r % ROUNDS) * ROUND
                dve.wait_ge(S["hot_read"], g + 1)
                dve.wait_ge(S["hot1_ready"], g + 1)
                dve.tensor_tensor(eq1[:, k, :, :], counting[:, first:first + ROUND].unsqueeze(1)
                                  .to_broadcast([P, GROUP, ROUND]),
                                  keys[:, 0, n].unsqueeze(2).to_broadcast([P, GROUP, ROUND]), ALU.is_equal)\
                    .then_inc(S["eq1_ready"], 1)
                dve.tensor_tensor(hot2[:, k, :, :], counting[:, :].unsqueeze(1).to_broadcast([P, GROUP, P]),
                                  keys[:, 1, n].unsqueeze(2).to_broadcast([P, GROUP, P]), ALU.is_equal)\
                    .then_inc(S["hot2_ready"], 1)

            def take_gates(r, q):
                for half in range(2):
                    dve.wait_ge(S["spread"], 2 * q + half + 1)
                    n = bass.ds((q - (r - 1) * ROUND) * GROUP + half * HALF_GROUP, HALF_GROUP)
                    dve.tensor_reduce(gates[r % 2][:, :, n].rearrange("p i n -> p n i"),
                                      bank[:, G_BANK + half, 0:HALF_GROUP * PARTS * ROUND]
                                      .rearrange("p (n w i) -> p n i w", n=HALF_GROUP, w=PARTS), AX.X, ALU.add)\
                        .then_inc(S["gates_taken"], 1)

            def split_u(n, i):
                dve.wait_ge(S["u_hi"], at(n, i) + 1)
                dve.tensor_tensor(ul[:, n % 2, :, :], u_raw[:, n % RAW, :, :], uh[:, n % 2, :, :].bitcast(F32),
                                  ALU.subtract).then_inc(S["u_lo"], 1)

            dve.sem_inc(S["gates_taken"], 2)
            with dve.Fori(0, FIRST) as i:
                for k in range(2):
                    one_hots(0, 2 * i + k, (2 * i + k) * GROUP, k)
            split_u(0, None)
            split_u(1, None)
            with dve.Fori(FIRST, ROUND // 2) as i:
                for k in range(2):
                    one_hots(0, 2 * i + k, (2 * i + k) * GROUP, k)

            def at_round(r):
                if r:
                    dve.wait_ge(S["gates_taken"], 2 * r * ROUND + 2)
                    dve.wait_ge(S["hid_ready"], r * ROUND)
                else:
                    dve.wait_ge(S["first_taken"], ROUND + 2)

            def body(r, n, i, c):
                q, k = at(n, i), c % 2
                dve.wait_ge(S["a_taken"], q + 3)
                g = gates[r % 2][:, bass.ds(q - r * ROUND, 1), :].rearrange("p a n -> p (a n)")
                dve.tensor_tensor(hid[:, k, :], hid[:, k, :], g, ALU.mult).then_inc(S["hid_ready"], 1)
                if spread_here(r):
                    one_hots(r + 1, q + ROUND, (q - r * ROUND) * GROUP + (r + 1) // ROUNDS * ST, k)
                dve.wait_ge(S["h_hi"], q + 1)
                dve.tensor_tensor(hl[:, k, :], hid[:, k, :], hh[:, k, :].bitcast(F32), ALU.subtract)\
                    .then_inc(S["h_lo"], 1)
                if i is not None or n + 2 < N:
                    split_u(n + 2, i)
                if spread_here(r):
                    take_gates(r + 1, q)

            def at_sweep(sweep):
                dve.wait_ge(S["out_done"], sweep + 1)
                for m in range(2):
                    if sweep:
                        dve.wait_ge(S["out_stored"], 16 * 2 * sweep)
                    dve.tensor_copy(out[:, 2 * m:2 * m + 2, :], bank[:, 2 * m:2 * m + 2, :])\
                        .then_inc(S["out_taken"], 1)

            rounds(dve, body, at_round, at_sweep)

        @block.tensor
        def _(pe):
            pe.sem_inc(S["a_done"], 2)
            pe.sem_inc(S["v_done"], 2)
            pe.sem_inc(S["hot_read"], 2)

            def add_gates(g, k):
                pe.wait_ge(S["hot1_ready"], g + 3)
                pe.wait_ge(S["hot2_ready"], g + 1)
                pe.wait_ge(S["first_taken"], g + 1)
                for j in range(GROUP):
                    for p in range(PARTS):
                        last = pe.matmul(bank[:, G_BANK + k, j * ROUND:(j + 1) * ROUND], hot2[:, k, j, :],
                                         hot1[:, k, j, p, :], start=p == 0, stop=p == PARTS - 1)
                last.then_inc(S["hot_read"], 1)

            def spread_gates(q, k):
                pe.wait_ge(S["hot1_ready"], q + ROUND + 3)
                pe.wait_ge(S["hot2_ready"], q + ROUND + 1)
                for half in range(2):
                    pe.wait_ge(S["gates_taken"], 2 * q + half + 1)
                    for j in range(HALF_GROUP):
                        n = half * HALF_GROUP + j
                        last = pe.matmul(bank[:, G_BANK + half, j * PARTS * ROUND:(j + 1) * PARTS * ROUND],
                                         hot2[:, k, n, :], hot1[:, k, n, :, :].rearrange("p w i -> p (w i)"),
                                         start=True, stop=True)
                    last.then_inc(S["spread"], 1)

            def scores(q, k, sweep):
                pe.wait_ge(S["u_lo"], q + RAW + 1)
                pe.wait_ge(S["a_taken"], q + 1)
                t = slice(sweep * ST, (sweep + 1) * ST)
                for kt in range(KD):
                    last = split_products(pe, bank[:, A_BANK + k, 0:ST], (uh[:, k, kt, :], ul[:, k, kt, :]),
                                          (xh[:, kt, t], xl[:, kt, t]), kt == 0, kt == KD - 1)
                last.then_inc(S["a_done"], 1)

            def values(q, k, frees):
                pe.wait_ge(S["h_lo"], q + 3)
                pe.wait_ge(S["v_lo"], q + RAW + 1)
                for m in range(2):
                    for c in range(2):
                        t, d = slice(m * P, (m + 1) * P), slice(c * BANK, (c + 1) * BANK)
                        last = split_products(pe, bank[:, 2 * m + c, :], (hh[:, k, t], hl[:, k, t]),
                                              (vh[:, k, d], vl[:, k, d]), False, False, True,
                                              frees if m == c == 0 else None)
                last.then_inc(S["v_done"], 1)

            def zero_products(start):
                for b in range(4):
                    for c in range(BANK // P):
                        last = pe.matmul(bank[:, b, c * P:(c + 1) * P], zero[:, :], zero[:, :],
                                         start=start and c == 0, stop=not start, skip_group_check=True)
                return last

            pe.wait_ge(S["zeroed"], 1)
            zero_products(True)
            with pe.Fori(0, FIRST) as i:
                for k in range(2):
                    add_gates(2 * i + k, k)
            pe.wait_ge(S["x_landed"], 32)
            scores(0, 0, 0)
            with pe.Fori(FIRST, ROUND // 2) as i:
                for k in range(2):
                    add_gates(2 * i + k, k)
            pe.wait_ge(S["first_taken"], ROUND + 2)

            def body(r, n, i, c):
                q, k = at(n, i), c % 2
                if i is not None or n + 1 < N:
                    last_of_sweep = i is None and (n + 1) % PEER_KEYS == 0
                    scores(q + 1, 1 - k, r // ROUNDS + last_of_sweep)
                if spread_here(r):
                    spread_gates(q, k)
                values(q, k, S["hot_read"] if spread_here(r) else None)

            def at_sweep(sweep):
                zero_products(False).then_inc(S["out_done"], 1)
                if sweep + 1 < SWEEPS:
                    pe.wait_ge(S["out_taken"], 2 * (sweep + 1))
                    zero_products(True)

            rounds(pe, body, None, at_sweep)



POOL_GROUPS, POOL_D = 4, 512
AH, LAT = 8, 128
IDX_H, IDX_D = 8, 32
INDEX_SCALE = (IDX_H ** -0.5) * (IDX_D ** -0.5)
ATTN_SCALE = LAT ** -0.5
TOP = min(256, T // 4)
FF = 2816
KF = FF // P


def seen(t):
    return META + (t + 1) * P


def phase_project_2(nc, bank, const, io, life):
    with ExitStack() as ctx:
        s = Scope(nc, ctx, "p2")
        xh, xl = life["xh"], life["xl"]
        bias = life["bias"]
        h = life["h_rows"]
        hm = s.sb("h_meta", [META, D])
        gain, gain_row = s.sb("gain", [P, KD]), s.sb("gain_row", [P, D])
        add = life["xs"]
        kv_g = s.sb("kv_g", [P, LAT])
        qi = s.sb("qi", [P, 2, T])
        ki = s.sb("ki", [P, TM])
        wi = s.sb("wi", [P, NT, IDX_H])
        rel = s.sb("rel", [P, 2, TM])
        score = s.sb("score", [P, NT, TM])
        best = s.sb("best", [P, 8])
        c, cm, cT = life["c"], life["c_m"], life["cT"]
        ring = WeightRing(s)
        early = Gemm(s, ring, bank, "early_")
        late = Gemm(s, ring, bank, "late_")
        g_landed, stored = s.sem("gains_landed"), s.sem("stored")
        h_landed = [s.sem(f"h_landed{t}") for t in range(NT)]
        added, y_done, vec = s.sem("added"), s.sem("y_done"), s.sem("vector_steps")
        scored, relued, summed = s.sem("scored"), s.sem("relued"), s.sem("summed")
        c_done, c_turned, c_taken = s.sem("c_done"), s.sem("c_turned"), s.sem("c_taken")
        ident = const[:, CONSTS["ident"][0]:CONSTS["ident"][1]]
        causal = const[:, CONSTS["causal"][0]:CONSTS["causal"][1]]
        causal_fill = const[:, CONSTS["causal_fill"][0]:CONSTS["causal_fill"][1]]
        out_stats = RowStats(s, h, None, "o_")
        norm = NormColumns(s, h, hm, gain, xh, xl, ident, bank, life["xs"], out_stats.junk)
        c_stats = RowStats(s, c, cm, "c_")

        def rows(kt, m):
            cc = slice(META + m * P, META + (m + 1) * P) if m >= 0 else slice(0, P)
            return xh[:, kt, cc], xl[:, kt, cc]

        def columns(kt, m):
            cc = slice(META, TM) if m >= 0 else slice(0, META)
            return xh[:, kt, cc], xl[:, kt, cc]

        def part(kind, w, c0, width, meta, dst=None, first=0):
            return dict(kind=kind, slab=lambda i, turn: weight_slab(w, i, c0, width), width=width, ktiles=KD,
                        x=rows if kind == "rows" else columns, meta=meta, dst=dst, first=first)

        b_index, b_lat = early.plan([part("columns", io["w_index"], 0, 3 * P, True),
                                     part("rows", io["w_latent"], 0, LAT + IDX_H, True)])
        late.slab0 = early.slab0
        w = io["w_in_2"]
        c_conv = 1960
        blocks = late.plan([
            part("columns", w, 0, BANK, True, life["u"]), part("columns", w, 512, BANK, False, life["q2"], 0),
            part("columns", w, 1024, BANK, False, life["q2"], 4), part("columns", w, c_conv, BANK, False, life["cb"]),
            part("columns", w, c_conv + 512, BANK, True, life["cc"]),
            part("columns", w, c_conv + 1024, BANK, True, life["cu"])])
        units = [(t, hd) for t in range(NT) for hd in range(IDX_H)]
        block = s.block()

        @block.sync
        def _(sp):
            for t in range(NT):
                rows_t = slice(t * P, (t + 1) * P)
                sp.dma_start(h[:, t, :], io["h1"][rows_t, :]).then_inc(h_landed[t], 16)
                sp.dma_start(add[:, t, :], io["experts"][rows_t, :]).then_inc(h_landed[t], 16)
                if t == 0:
                    sp.dma_start(gain_row[:, :], io["final_norm_w"].to_broadcast([P, D])).then_inc(g_landed, 16)
            sp.dma_start(const[:, :], io["const"][:, 0:CONST_2_W]).then_inc(g_landed, 16)
            sp.dma_start(gain[:, :], io["norm1_g"]).then_inc(g_landed, 16)
            sp.dma_start(kv_g[:, :], io["kv_norm_g"].to_broadcast([P, LAT])).then_inc(g_landed, 16)
            sp.dma_start(hm[:, :], io["meta_2"]).then_inc(g_landed, 16)
            for b in (b_index, b_lat):
                early.on_sync(sp, b)
            sp.wait_ge(y_done, NT)
            sp.dma_start(io["x2"].rearrange("(t p) d -> p t d", p=P), h[:, :, :]).then_inc(stored, 16)
            for b in blocks:
                late.on_sync(sp, b)
            sp.wait_ge(stored, 16)

        @block.gpsimd
        def _(pool):
            ring.open_raw(pool)
            for b in (b_index, b_lat):
                early.on_gpsimd(pool, b)
            for b in blocks:
                late.on_gpsimd(pool, b)

        @block.scalar
        def _(act):
            late.open_banks(act)
            out_stats.on_scalar(act, lambda e, t: e.wait_ge(added, t + 1))
            act.wait_ge(g_landed, 16 * 5)
            norm.on_scalar(act, lambda e, t: e.wait_ge(y_done, min(t + 1, NT)))
            for b in (b_index, b_lat):
                early.on_scalar(act, b)
            c_stats.on_scalar(act, lambda e, t: e.wait_ge(early.bank_free, NBANK + early.tile0))
            for n, (t, hd) in enumerate(units):
                act.wait_ge(scored, n + 1)
                if n >= 2:
                    act.wait_ge(summed, n - 1)
                pair = bank[:, 2 * (n % 4):2 * (n % 4) + 2, :].rearrange("p b n -> p (b n)")
                act.activation(rel[:, n % 2, 0:seen(t)], pair[:, 0:seen(t)], ACT.Relu).then_inc(relued, 1)
            act.wait_ge(c_turned, 1)
            act.activation(cT[:, META:TM], bank[:, 0, :], ACT.Copy)
            act.activation(cT[:, 0:META], bank[:, 1, 0:META], ACT.Copy).then_inc(c_taken, 1)

            def use(b):
                def one(j, m, got):
                    if m >= 0:
                        off = META if b["meta"] else 0
                        return act.activation(b["dst"][:, b["first"] + m, off:off + T], got, ACT.Copy)
                    return act.activation(b["dst"][:, :, 0:META],
                                          got[:, 0:4 * META].rearrange("p (m c) -> p m c", m=4), ACT.Copy)
                return one

            late.on_scalar(act, blocks[0])
            for n, b in enumerate(blocks):
                if n + 1 < len(blocks):
                    late.on_scalar(act, blocks[n + 1], 0, AHEAD)
                if b["dst"] is life["cb"]:
                    act.wait_ge(stored, 16)
                late.take(act, b, use(b))
                if n + 1 < len(blocks):
                    late.on_scalar(act, blocks[n + 1], 0, REST)

        @block.tensor
        def _(pe):
            ring.open_slots(pe)
            pe.wait_ge(g_landed, 16 * 5)
            norm.on_tensor(pe)
            pe.wait_ge(norm.done, norm.total())
            for b in (b_index, b_lat):
                early.on_tensor(pe, b)
            pe.wait_ge(early.bank_free, NBANK + early.tile0)
            for n, (t, hd) in enumerate(units):
                if n >= 4:
                    pe.wait_ge(relued, n - 3)
                r = slice((hd % 4) * IDX_D, (hd % 4 + 1) * IDX_D)
                lhs = qi[r, hd // 4, t * P:(t + 1) * P]
                b0, w0 = 2 * (n % 4), min(seen(t), BANK)
                last = pe.matmul(bank[:, b0, 0:w0], lhs, ki[r, 0:w0], start=True, stop=True)
                if seen(t) > BANK:
                    last = pe.matmul(bank[:, b0 + 1, 0:seen(t) - BANK], lhs, ki[r, BANK:seen(t)],
                                     start=True, stop=True)
                last.then_inc(scored, 1)
            pe.wait_ge(relued, len(units))
            pe.wait_ge(c_done, NT + 1)
            for t in range(NT):
                pe.transpose(bank[:, 0, t * P:(t + 1) * P], c[:, t, :], ident)
            pe.transpose(bank[:, 1, 0:META], cm[:, :], ident[0:META, 0:META]).then_inc(c_turned, 1)
            pe.wait_ge(c_taken, 1)
            for b in blocks:
                late.on_tensor(pe, b)

        @block.vector
        def _(dve):
            chain = Chain(dve, vec)
            early.open_banks(dve)
            for t in range(NT):
                dve.wait_ge(h_landed[t], 32)
                dve.tensor_tensor(h[:, t, :], h[:, t, :], add[:, t, :], ALU.add).then_inc(added, 1)
            dve.wait_ge(g_landed, 16 * 5)
            out_stats.on_vector(dve, chain, lambda t: dve.scalar_tensor_tensor(
                h[:, t, :], h[:, t, :], out_stats.rstd[:, t:t + 1], gain_row[:, :], ALU.mult, ALU.mult)
                .then_inc(y_done, 1))
            dve.wait_ge(y_done, NT)
            norm.on_vector(dve, chain)

            def use_index(j, m, got):
                if m < 0:
                    return dve.tensor_copy(ki[:, 0:META], got[:, 2 * META:3 * META])
                return dve.tensor_copy(qi[:, m, :] if m < 2 else ki[:, META:TM], got)

            def use_latent(j, m, got):
                if m < 0:
                    return dve.tensor_copy(cm[:, :], got[0:META, 0:LAT])
                dve.tensor_scalar(wi[:, m, :], got[:, LAT:LAT + IDX_H], INDEX_SCALE, None, ALU.mult)
                return dve.tensor_copy(c[:, m, :], got[:, 0:LAT])

            early.take(dve, b_index, use_index)
            early.take(dve, b_lat, use_latent)
            dve.wait_ge(early.bank_free, NBANK + early.tile0)

            def normed(t):
                rows_t, n = c_stats.tile(t)
                dve.scalar_tensor_tensor(rows_t, rows_t, c_stats.rstd[0:n, t:t + 1], kv_g[0:n, :], ALU.mult,
                                         ALU.mult).then_inc(c_done, 1)

            c_stats.on_vector(dve, chain, normed)
            for n, (t, hd) in enumerate(units):
                dve.wait_ge(relued, n + 1)
                got, acc = rel[:, n % 2, 0:seen(t)], score[:, t, 0:seen(t)]
                if hd == 0:
                    last = dve.tensor_scalar(acc, got, wi[:, t, 0:1], None, ALU.mult)
                else:
                    dve.wait_ge(summed, n)
                    last = dve.scalar_tensor_tensor(acc, got, wi[:, t, hd:hd + 1], acc, ALU.mult, ALU.add)
                last.then_inc(summed, 1)
            dve.wait_ge(summed, len(units))
            for t in range(NT):
                own = score[:, t, META + t * P:seen(t)]
                chain(dve.tensor_tensor(own, own, causal, ALU.mult))
                last = dve.tensor_tensor(own, own, causal_fill, ALU.add)
            chain(last)
            for t in range(NT):
                work = score[:, t, 0:seen(t)]
                for _ in range(TOP // 8):
                    chain(dve.max(best[:, :], work))
                    chain(dve.match_replace(work, best[:, :], work, NEG))
                b = bias[:, t, 0:seen(t)]
                chain(dve.tensor_scalar(b, work, 2 * NEG / 3, 1.0, ALU.is_lt, ALU.subtract))
                chain(dve.tensor_scalar(b, b, -FILL, None, ALU.mult))
                own = bias[:, t, META + t * P:seen(t)]
                last = dve.tensor_tensor(own, own, causal_fill, ALU.add)
            chain(last)


def phase_sparse_attention(nc, bank, const, io, life):
    with ExitStack() as ctx:
        s = Scope(nc, ctx, "sa")
        q, c, cm, cT, bias = (life[n] for n in ("q2", "c", "c_m", "cT", "bias"))
        oh, ol = life["attn_hi"], life["attn_lo"]
        masked = s.sb("masked", [P, 2, TM])
        p = s.sb("p", [P, 3, TM])
        pT, pTm = s.sb("pT", [P, 2, T]), s.sb("pTm", [META, 2, P])
        mx, total = s.sb("mx", [P, 2]), s.sb("total", [P, 3])
        names = ("scored", "masked_done", "maxed", "exped", "scaled", "turned", "taken", "o_done", "o_hi", "o_lo",
                 "vector_steps")
        S = {n: s.sem(n) for n in names}
        ident = const[:, CONSTS["ident"][0]:CONSTS["ident"][1]]
        units = [(t, hd) for t in range(NT) for hd in range(AH)]
        N = len(units)
        block = s.block()

        @block.tensor
        def _(pe):
            for n in range(N + 3):
                if n < N:
                    t, hd = units[n]
                    if n >= 2:
                        pe.wait_ge(S["masked_done"], n - 1)
                    b0, w0 = 2 * (n % 2), min(seen(t), BANK)
                    lhs = q[:, hd, t * P:(t + 1) * P]
                    last = pe.matmul(bank[:, b0, 0:w0], lhs, cT[:, 0:w0], start=True, stop=True)
                    if seen(t) > BANK:
                        last = pe.matmul(bank[:, b0 + 1, 0:seen(t) - BANK], lhs, cT[:, BANK:seen(t)],
                                         start=True, stop=True)
                    last.then_inc(S["scored"], 1)
                if 2 <= n <= N + 1:
                    e = n - 2
                    t = units[e][0]
                    pe.wait_ge(S["scaled"], e + 1)
                    if e >= 1:
                        pe.wait_ge(S["taken"], e)
                    pe.transpose(bank[0:META, 6, 0:P], p[:, e % 3, 0:META], ident)
                    for kt in range(t + 1):
                        last = pe.transpose(bank[:, 4 + e % 2, kt * P:(kt + 1) * P],
                                            p[:, e % 3, META + kt * P:META + (kt + 1) * P], ident)
                    last.then_inc(S["turned"], 1)
                if n >= 3:
                    e = n - 3
                    t = units[e][0]
                    pe.wait_ge(S["taken"], e + 1)
                    if e >= 1:
                        pe.wait_ge(S["o_lo"], e)
                    o = bank[:, 7, 0:P]
                    pe.matmul(o, cm[:, :], pTm[:, e % 2, :], start=True, stop=False)
                    for kt in range(t + 1):
                        last = pe.matmul(o, c[:, kt, :], pT[:, e % 2, kt * P:(kt + 1) * P], start=False,
                                         stop=kt == t)
                    last.then_inc(S["o_done"], 1)

        @block.scalar
        def _(act):
            for n in range(N + 4):
                if n >= 4:
                    e = n - 4
                    t, hd = units[e]
                    act.wait_ge(S["o_done"], e + 1)
                    act.activation(oh[:, hd, t * P:(t + 1) * P], bank[:, 7, 0:P], ACT.Copy).then_inc(S["o_hi"], 1)
                if 3 <= n <= N + 2:
                    e = n - 3
                    t = units[e][0]
                    act.wait_ge(S["turned"], e + 1)
                    if e >= 2:
                        act.wait_ge(S["o_done"], e - 1)
                    act.activation(pTm[:, e % 2, :], bank[0:META, 6, 0:P], ACT.Copy)
                    act.activation(pT[:, e % 2, 0:(t + 1) * P], bank[:, 4 + e % 2, 0:(t + 1) * P], ACT.Copy)\
                        .then_inc(S["taken"], 1)
                if n < N:
                    t = units[n][0]
                    act.wait_ge(S["maxed"], n + 1)
                    if n >= 3:
                        act.wait_ge(S["turned"], n - 2)
                    act.activation(p[:, n % 3, 0:seen(t)], masked[:, n % 2, 0:seen(t)], ACT.Exp,
                                   bias=mx[:, n % 2:n % 2 + 1], scale=ATTN_SCALE,
                                   accum_out=total[:, n % 3:n % 3 + 1]).then_inc(S["exped"], 1)

        @block.vector
        def _(dve):
            chain = Chain(dve, S["vector_steps"])
            for n in range(N + 4):
                if n >= 4:
                    e = n - 4
                    t, hd = units[e]
                    cols = slice(t * P, (t + 1) * P)
                    dve.wait_ge(S["o_hi"], e + 1)
                    dve.tensor_tensor(ol[:, hd, cols], bank[:, 7, 0:P], oh[:, hd, cols].bitcast(F32), ALU.subtract)\
                        .then_inc(S["o_lo"], 1)
                if n < N:
                    t = units[n][0]
                    dve.wait_ge(S["scored"], n + 1)
                    if n >= 2:
                        dve.wait_ge(S["exped"], n - 1)
                    pair = bank[:, 2 * (n % 2):2 * (n % 2) + 2, :].rearrange("p b n -> p (b n)")
                    dve.tensor_tensor_reduce(masked[:, n % 2, 0:seen(t)], pair[:, 0:seen(t)], bias[:, t, 0:seen(t)],
                                             1.0, NEG, ALU.add, ALU.max, mx[:, n % 2:n % 2 + 1])\
                        .then_inc(S["masked_done"], 1)
                    dve.wait_ge(S["masked_done"], n + 1)
                    dve.tensor_scalar(mx[:, n % 2:n % 2 + 1], mx[:, n % 2:n % 2 + 1], -ATTN_SCALE, None,
                                      ALU.mult).then_inc(S["maxed"], 1)
                if n >= 1 and n - 1 < N:
                    e = n - 1
                    t = units[e][0]
                    dve.wait_ge(S["exped"], e + 1)
                    chain(dve.reciprocal(total[:, e % 3:e % 3 + 1], total[:, e % 3:e % 3 + 1]))
                    dve.tensor_scalar(p[:, e % 3, 0:seen(t)], p[:, e % 3, 0:seen(t)], total[:, e % 3:e % 3 + 1],
                                      None, ALU.mult).then_inc(S["scaled"], 1)


def phase_pool_and_conv(nc, bank, io, life):
    with ExitStack() as ctx:
        s = Scope(nc, ctx, "pc")
        u, cb, cc, cu = (life[n] for n in ("u", "cb", "cc", "cu"))
        ph, pl, vh, vl = (life[n] for n in ("pool_hi", "pool_lo", "conv_hi", "conv_lo"))
        sums = s.sb("sums", [P, 2, TM])
        pooled = s.sb("pooled", [P, POOL_GROUPS, T])
        y = cu[:, :, 0:T]
        pool_w = s.sb("pool_w", [P, POOL_GROUPS, P])
        scale, conv_w = s.sb("scale", [P, POOL_GROUPS]), s.sb("conv_w", [P, 3, POOL_GROUPS])
        landed, pooled_done, mixed_done, vec = (s.sem("landed"), s.sem("pooled"), s.sem("mixed"),
                                                s.sem("vector_steps"))
        v_done = s.sem("v_done")
        block = s.block()

        @block.sync
        def _(sp):
            sp.dma_start(pool_w[:, :, :], io["pool_w"]).then_inc(landed, 16)
            sp.dma_start(scale[:, :], io["pool_scale"]).then_inc(landed, 16)
            sp.dma_start(conv_w[:, :, :], io["conv_w"]).then_inc(landed, 16)

        @block.tensor
        def _(pe):
            pe.wait_ge(landed, 48)
            for g in range(POOL_GROUPS):
                pe.wait_ge(pooled_done, g + 1)
                pe.matmul(bank[:, g, :], pool_w[:, g, :], pooled[:, g, :], start=True, stop=True)\
                    .then_inc(mixed_done, 1)

        @block.gpsimd
        def _(pool):
            pool.tensor_tensor(cc[:, :, :], cc[:, :, :], cu[:, :, :], ALU.mult).then_inc(v_done, 1)

        @block.vector
        def _(dve):
            chain = Chain(dve, vec)
            dve.wait_ge(landed, 48)
            for g in range(POOL_GROUPS):
                src, lo = u[:, g, :], 0
                for j in range(g + 1):
                    dst, step = sums[:, j % 2, :], 1 << j
                    lo += step
                    chain(dve.tensor_tensor(dst[:, lo:TM], src[:, lo:TM], src[:, lo - step:TM - step], ALU.add))
                    src = dst
                last = dve.scalar_tensor_tensor(pooled[:, g, :], src[:, META:TM], 1.0 / (2 << g), u[:, g, META:TM],
                                                ALU.mult, ALU.subtract)
                last.then_inc(pooled_done, 1)
                dve.wait_ge(pooled_done, g + 1)
            for g in range(POOL_GROUPS):
                dve.wait_ge(mixed_done, g + 1)
                last = dve.tensor_scalar(pooled[:, g, :], bank[:, g, :], scale[:, g:g + 1], None, ALU.mult)
            chain(last)
            chain(dve.tensor_copy(ph[:, :, :], pooled[:, :, :]))
            dve.tensor_tensor(pl[:, :, :], pooled[:, :, :], ph[:, :, :].bitcast(F32), ALU.subtract)
            dve.wait_ge(v_done, 1)
            for g in range(POOL_GROUPS):
                last = dve.tensor_scalar(y[:, g, :], cc[:, g, META - 2:TM - 2], conv_w[:, 0, g:g + 1], None,
                                         ALU.mult)
            for k in (1, 2):
                chain(last)
                for g in range(POOL_GROUPS):
                    last = dve.scalar_tensor_tensor(y[:, g, :], cc[:, g, META - 2 + k:TM - 2 + k],
                                                    conv_w[:, k, g:g + 1], y[:, g, :], ALU.mult, ALU.add)
            chain(last)
            chain(dve.tensor_tensor(y[:, :, :], y[:, :, :], cb[:, :, :], ALU.mult))
            chain(dve.tensor_copy(vh[:, :, :], y[:, :, :]))
            dve.tensor_tensor(vl[:, :, :], y[:, :, :], vh[:, :, :].bitcast(F32), ALU.subtract)


def phase_branches(nc, bank, io, life):
    with ExitStack() as ctx:
        s = Scope(nc, ctx, "br")
        xh, xl, mh, ml = (life[n] for n in ("xh", "xl", "m_hi", "m_lo"))
        sg, y = s.sb("sg", [P, 4, T]), s.sb("y", [P, 4, T])
        m_sum = s.sb("m_sum", [P, 4, T])
        b_gate = s.sb("b_gate", [P, 3 * KD])
        ring = WeightRing(s)
        gemm = Gemm(s, ring, bank)
        landed, y_ready, y_used, vec = s.sem("landed"), s.sem("y_ready"), s.sem("y_used"), s.sem("vector_steps")
        G0 = 3496

        def part(w, c0, kt, x, gate):
            return dict(kind="columns", slab=lambda i, turn: weight_slab(w, i, c0 + turn * BANK), width=BANK,
                        ktiles=kt, x=x, meta=False, gate=gate)

        def split(hi, lo):
            return lambda kt, m: (hi[:, kt, :], lo[:, kt, :])

        cols = lambda kt, m: (xh[:, kt, META:TM], xl[:, kt, META:TM])
        plan = []
        for n, (w, kt, hi, lo) in enumerate((("w_a", 4, "pool_hi", "pool_lo"), ("w_b", 8, "attn_hi", "attn_lo"),
                                             ("w_c", 4, "conv_hi", "conv_lo"))):
            gate = part(io["w_in_2"], 0, KD, cols, n)
            gate["slab"] = lambda i, turn, n=n: weight_slab(io["w_in_2"][:, G0 + n * D - BANK:], i,
                                                            (turn + 1) * BANK)
            plan.append(gate)
            plan.append(part(io[w], 0, kt, split(life[hi], life[lo]), None))
        TURNS = D // BANK
        blocks = gemm.plan(plan, TURNS)
        block = s.block()

        @block.sync
        def _(sp):
            sp.dma_start(b_gate[:, :], io["b_gate"]).then_inc(landed, 16)
            with sp.Fori(0, TURNS) as turn:
                for b in blocks:
                    gemm.on_sync(sp, b, turn)

        @block.gpsimd
        def _(pool):
            ring.open_raw(pool)
            with pool.Fori(0, TURNS) as turn:
                for b in blocks:
                    gemm.on_gpsimd(pool, b, turn)

        @block.tensor
        def _(pe):
            ring.open_slots(pe)
            with pe.Fori(0, TURNS) as turn:
                for b in blocks:
                    gemm.on_tensor(pe, b, turn)

        @block.scalar
        def _(act):
            gemm.open_banks(act)
            act.wait_ge(landed, 16)

            def take(n, turn):
                b = blocks[n]
                if b["gate"] is not None:
                    act.wait_ge(y_used, turn * 12 + 4 * b["gate"] + 4)

                def use(j, m, got):
                    if b["gate"] is not None:
                        at = bass.ds(turn * 4 + b["gate"] * KD + m, 1)
                        return act.activation(sg[:, m, :], got, ACT.Sigmoid, bias=b_gate[:, at])
                    return act.activation(y[:, m, :], got, ACT.Copy)

                gemm.take(act, b, use, turn)
                if b["gate"] is None:
                    act.wait_ge(gemm.bank_free, NBANK + b["tile0"] + 4 + turn * b["per"][1])
                    act.sem_inc(y_ready, 4)

            with act.Fori(0, TURNS) as turn:
                gemm.on_scalar(act, blocks[0], turn)
                for n in range(len(blocks)):
                    if n + 1 < len(blocks):
                        gemm.on_scalar(act, blocks[n + 1], turn)
                    take(n, turn)

        @block.vector
        def _(dve):
            chain = Chain(dve, vec)
            dve.sem_inc(y_used, 4)
            with dve.Fori(0, TURNS) as turn:
                chain.loop(turn, 4)
                for n in range(3):
                    dve.wait_ge(y_ready, turn * 12 + 4 * n + 4)
                    if n == 0:
                        dve.tensor_tensor(m_sum[:, :, :], sg[:, :, :], y[:, :, :], ALU.mult).then_inc(y_used, 4)
                    else:
                        chain(dve.tensor_tensor(y[:, :, :], sg[:, :, :], y[:, :, :], ALU.mult))
                        dve.tensor_tensor(m_sum[:, :, :], m_sum[:, :, :], y[:, :, :], ALU.add).then_inc(y_used, 4)
                dve.wait_ge(y_used, turn * 12 + 16)
                at = bass.ds(turn * 4, 4)
                chain(dve.tensor_copy(mh[:, at, :], m_sum[:, :, :]))
                chain(dve.tensor_tensor(ml[:, at, :], m_sum[:, :, :], mh[:, at, :].bitcast(F32), ALU.subtract))
            chain.end_loop(TURNS)


def phase_out_2(nc, bank, io, life):
    with ExitStack() as ctx:
        s = Scope(nc, ctx, "o2")
        mh, ml, h, xh, xl = (life[n] for n in ("m_hi", "m_lo", "h", "fh", "fl"))
        gain = s.sb("gain", [P, KD])
        const = s.sb("const", [P, CONST_2_W])
        ring = WeightRing(s)
        gemm = Gemm(s, ring, bank)
        landed, h_done, vec = s.sem("landed"), s.sem("h_done"), s.sem("vector_steps")
        norm = NormColumns(s, h, None, gain, xh, xl, const[:, CONSTS["ident"][0]:CONSTS["ident"][1]], bank)

        def part(c0):
            return dict(kind="rows", slab=lambda i, _: weight_slab(io["w_o"], i, c0), width=BANK, ktiles=KD,
                        x=lambda kt, m: (mh[:, kt, m * P:(m + 1) * P], ml[:, kt, m * P:(m + 1) * P]),
                        meta=False, c0=c0)

        blocks = gemm.plan([part(0), part(BANK)])
        block = s.block()

        @block.sync
        def _(sp):
            sp.dma_start(const[:, :], io["const"][:, 0:CONST_2_W]).then_inc(landed, 16)
            sp.dma_start(gain[:, :], io["norm2_g"]).then_inc(landed, 16)
            sp.dma_start(h[:, :, :], io["x2"].rearrange("(t p) d -> p t d", p=P)).then_inc(landed, 16)
            for b in blocks:
                gemm.on_sync(sp, b)

        @block.gpsimd
        def _(pool):
            ring.open_raw(pool)
            for b in blocks:
                gemm.on_gpsimd(pool, b)

        @block.scalar
        def _(act):
            for b in blocks:
                gemm.on_scalar(act, b)
            act.wait_ge(landed, 48)
            norm.on_scalar(act, lambda e, t: e.wait_ge(h_done, 1))

        @block.tensor
        def _(pe):
            ring.open_slots(pe)
            for b in blocks:
                gemm.on_tensor(pe, b)
            pe.wait_ge(landed, 48)
            pe.wait_ge(gemm.bank_free, NBANK + gemm.tile0)
            norm.on_tensor(pe)

        @block.vector
        def _(dve):
            chain = Chain(dve, vec)
            gemm.open_banks(dve)
            dve.wait_ge(landed, 48)
            for b in blocks:
                gemm.take(dve, b, lambda j, m, got: dve.tensor_tensor(
                    h[:, m, b["c0"]:b["c0"] + BANK], got, h[:, m, b["c0"]:b["c0"] + BANK], ALU.add))
            dve.wait_ge(gemm.bank_free, NBANK + gemm.tile0)
            dve.sem_inc(h_done, 1)
            norm.on_vector(dve, chain)


def phase_feed_forward(nc, bank, io, life):
    with ExitStack() as ctx:
        s = Scope(nc, ctx, "ff")
        h, xh, xl = life["h"], life["fh"], life["fl"]
        ah, al = s.sb("ah", [P, KF, T], F32R), s.sb("al", [P, KF, T], F32R)
        sg, up = s.sb("sg", [P, 2, T]), s.sb("up", [P, 2, T])
        stats_row = s.sb("gain_row", [P, D])
        ring = WeightRing(s)
        gemm = Gemm(s, ring, bank)
        down = Gemm(s, ring, bank, "down_")
        landed, ready, used, vec = s.sem("landed"), s.sem("pair_ready"), s.sem("pair_used"), s.sem("vector_steps")
        h_done, out_done, stored = s.sem("h_done"), s.sem("out_done"), s.sem("stored")
        stats = RowStats(s, h, None, "s_")

        def part(b):
            return dict(kind="columns", width=BANK, ktiles=KD, meta=False, b=b,
                        slab=lambda i, turn: weight_slab(io["w_gate_up"], i, turn * 2 * BANK + b * BANK),
                        x=lambda kt, m: (xh[:, kt, :], xl[:, kt, :]))

        NB = KF // 2
        TURNS = NB // 2
        pair_blocks = gemm.plan([part(0), part(1)], TURNS)
        tail = gemm.plan([part(2 * TURNS)])[0]
        down.slab0 = gemm.slab0

        def down_part(c0):
            return dict(kind="rows", slab=lambda i, _: weight_slab(io["w_down"], i, c0), width=BANK, ktiles=KF,
                        x=lambda kt, m: (ah[:, kt, m * P:(m + 1) * P], al[:, kt, m * P:(m + 1) * P]),
                        meta=False, c0=c0)

        downs = down.plan([down_part(0), down_part(BANK)])
        block = s.block()

        @block.sync
        def _(sp):
            sp.dma_start(stats_row[:, :], io["final_g"].to_broadcast([P, D])).then_inc(landed, 16)
            with sp.Fori(0, TURNS) as turn:
                for b in pair_blocks:
                    gemm.on_sync(sp, b, turn)
            gemm.on_sync(sp, tail)
            for b in downs:
                down.on_sync(sp, b)
            for t in range(NT):
                sp.wait_ge(out_done, t + 1)
                sp.dma_start(io["out"][t * P:(t + 1) * P, :], h[:, t, :]).then_inc(stored, 16)
            sp.wait_ge(stored, 16 * NT)

        @block.gpsimd
        def _(pool):
            ring.open_raw(pool)
            with pool.Fori(0, TURNS) as turn:
                for b in pair_blocks:
                    gemm.on_gpsimd(pool, b, turn)
            gemm.on_gpsimd(pool, tail)
            for b in downs:
                down.on_gpsimd(pool, b)

        @block.tensor
        def _(pe):
            ring.open_slots(pe)
            with pe.Fori(0, TURNS) as turn:
                for b in pair_blocks:
                    gemm.on_tensor(pe, b, turn)
            gemm.on_tensor(pe, tail)
            pe.wait_ge(gemm.bank_free, NBANK + gemm.tile0)
            pe.wait_ge(used, 2 * NB + 2)
            for b in downs:
                down.on_tensor(pe, b)

        @block.scalar
        def _(act):
            gemm.open_banks(act)

            def take(b, turn=0):
                first = 2 * b["b"] if b is not tail else 4 * TURNS

                def use(j, m, got):
                    if m < 2:
                        act.wait_ge(used, first + m + 1 + turn * 4)
                        return act.activation(sg[:, m, :], got, ACT.Silu)
                    return act.activation(up[:, m - 2, :], got, ACT.Copy)

                gemm.take(act, b, use, turn)
                act.wait_ge(gemm.bank_free, NBANK + b["tile0"] + 4 + turn * b["per"][1])
                act.sem_inc(ready, 2)

            gemm.on_scalar(act, pair_blocks[0], 0, AHEAD)
            with act.Fori(0, TURNS) as turn:
                for n, b in enumerate(pair_blocks):
                    gemm.on_scalar(act, b, turn, REST)
                    gemm.on_scalar(act, pair_blocks[1 - n], turn + n, AHEAD)
                    take(b, turn)
            gemm.on_scalar(act, tail, 0, REST)
            down.on_scalar(act, downs[0], 0, AHEAD)
            take(tail)
            down.on_scalar(act, downs[0], 0, REST)
            down.on_scalar(act, downs[1])
            stats.on_scalar(act, lambda e, t: e.wait_ge(h_done, 1))

        @block.vector
        def _(dve):
            chain = Chain(dve, vec)
            dve.sem_inc(used, 2)
            down.open_banks(dve)

            def hidden(b, turn=0):
                first = 2 * b["b"] if b is not tail else 4 * TURNS
                dve.wait_ge(ready, first + 2 + turn * 4)
                at = bass.ds(turn * 4 + first, 2)
                chain(dve.tensor_tensor(up[:, :, :], up[:, :, :], sg[:, :, :], ALU.mult))
                chain(dve.tensor_copy(ah[:, at, :], up[:, :, :]))
                dve.tensor_tensor(al[:, at, :], up[:, :, :], ah[:, at, :].bitcast(F32), ALU.subtract)\
                    .then_inc(used, 2)

            with dve.Fori(0, TURNS) as turn:
                chain.loop(turn, 4)
                for b in pair_blocks:
                    hidden(b, turn)
            chain.end_loop(TURNS)
            hidden(tail)
            dve.wait_ge(landed, 16)
            for b in downs:
                down.take(dve, b, lambda j, m, got: dve.tensor_tensor(
                    h[:, m, b["c0"]:b["c0"] + BANK], got, h[:, m, b["c0"]:b["c0"] + BANK], ALU.add))
            dve.wait_ge(down.bank_free, NBANK + down.tile0)
            dve.sem_inc(h_done, 1)
            stats.on_vector(dve, chain, lambda t: dve.scalar_tensor_tensor(
                h[:, t, :], h[:, t, :], stats.rstd[:, t:t + 1], stats_row[:, :], ALU.mult, ALU.mult)
                .then_inc(out_done, 1))



def program(nc, io):
    SEMAPHORES.clear()
    with ExitStack() as whole:
        bank = whole.enter_context(nc.psum_tensor("bank", [P, NBANK, BANK], F32))
        block_1(nc, bank, io)
        clear_semaphores(nc)
        block_2(nc, bank, io)


def block_1(nc, bank, io):
    picks_end, mix_end, const_end, parts_end, rows_end = (ExitStack() for _ in range(5))
    s = Scope(nc, picks_end, "b1")
    life = {"pick_keys": s.sb("pick_keys", [P, 2, T], BF16, side="right"),
            "pick_gates": s.sb("pick_gates", [P, T, 3], BF16, side="right")}
    const = Scope(nc, const_end, "b1c").sb("const", [P, CONST_W])
    s = Scope(nc, parts_end, "b1p")
    for n in ("q", "k", "v", "gv", "gr"):
        life[n] = s.sb(n, [P, NT, BANK])
    for n in ("k_m", "v_m", "gv_m"):
        life[n] = s.sb(n, [META, BANK])
    life["gqk"], life["zT"] = s.sb("gqk", [P, 4, TM]), s.sb("zT", [P, 1, TM])
    phase_project_1(nc, bank, const, io, life)
    life["mix"] = Scope(nc, mix_end, "b1m").sb("mix", [P, NT, D], side="right")
    phase_diff_attention(nc, bank, const, io, life)
    phase_linear_attention(nc, bank, const, io, life)
    parts_end.close()
    s = Scope(nc, rows_end, "b1r")
    life["h"] = s.sb("h", [P, NT, D])
    phase_mix_out(nc, bank, const, io, life)
    mix_end.close()
    phase_peer_pick(nc, bank, const, io, life)
    rows_end.close()
    const_end.close()
    phase_peer_experts(nc, bank, io, life)
    picks_end.close()


def block_2(nc, bank, io):
    life = {}
    left, right = ExitStack(), ExitStack()
    s = Scope(nc, left, "b2")
    for n in ("xh", "xl"):
        life[n] = s.sb(n, [P, KD, TM], F32R)
    r = Scope(nc, right, "b2r")
    const = r.sb("const", [P, CONST_2_W], side="right")
    for n, shape in (("bias", [P, NT, TM]), ("c", [P, NT, LAT]), ("c_m", [META, LAT]), ("cT", [P, TM]),
                     ("u", [P, 4, TM]), ("cc", [P, 4, TM]), ("cu", [P, 4, TM]), ("xs", [P, NT + 1, D]),
                     ("h_rows", [P, NT, D])):
        life[n] = r.sb(n, shape, side="right")
    life["q2"] = life["xs"][:, 0:NT, :].rearrange("p t (two n) -> p (t two) n", two=2)
    life["cb"] = life["h_rows"][:, 0:NT // 2, :].rearrange("p t (two n) -> p (t two) n", two=2)
    phase_project_2(nc, bank, const, io, life)
    for n in ("attn_hi", "attn_lo"):
        life[n] = s.sb(n, [P, AH, T], F32R)
    phase_sparse_attention(nc, bank, const, io, life)
    for n in ("pool_hi", "pool_lo", "conv_hi", "conv_lo"):
        life[n] = s.sb(n, [P, POOL_GROUPS, T], F32R)
    phase_pool_and_conv(nc, bank, io, life)
    right.close()
    right = ExitStack()
    r = Scope(nc, right, "b2m")
    for n in ("m_hi", "m_lo"):
        life[n] = r.sb(n, [P, KD, T], F32R, side="right")
    phase_branches(nc, bank, io, life)
    left.close()
    left = ExitStack()
    s = Scope(nc, left, "b2f")
    life["h"] = s.sb("h", [P, NT, D])
    for n in ("fh", "fl"):
        life[n] = s.sb(n, [P, KD, T], F32R)
    phase_out_2(nc, bank, io, life)
    right.close()
    phase_feed_forward(nc, bank, io, life)
    left.close()



def layouts(i):
    def rows(a):
        return a[0]

    def per_partition(a):
        return a[0].reshape(-1, P).T

    w2 = i["w_in_2"][0]
    at = np.cumsum([0, POOL_D, AH * LAT, LAT, IDX_H * IDX_D, IDX_D, IDX_H])
    q_idx, k_idx, w_idx = (w2[:, at[n]:at[n + 1]] for n in (3, 4, 5))
    gate_up = i["w_gate_up_2"][0].reshape(D, 2, FF // (BANK // 2), BANK // 2)
    return {
        "const": const_table(),
        "x": i["x"][0], "meta_tokens": i["meta_tokens"], "ln1_w": per_partition(i["ln1_w"]),
        "w_in": rows(i["w_in"]),
        "da_lambda_q1": i["da_lambda_q1"], "da_lambda_k1": i["da_lambda_k1"],
        "da_lambda_q2": i["da_lambda_q2"], "da_lambda_k2": i["da_lambda_k2"], "da_subln_w": i["da_subln_w"],
        "gla_gate_w2_f": rows(i["gla_gate_w2_f"]), "gla_gate_b_f": i["gla_gate_b_f"],
        "gla_gate_w2_b": rows(i["gla_gate_w2_b"]), "gla_gate_b_b": i["gla_gate_b_b"],
        "gla_norm_w": i["gla_norm_w"], "w_out": rows(i["w_out"]), "ln2_w": per_partition(i["ln2_w"]),
        "peer_w_q": rows(i["peer_w_q"]),
        "peer_keys": i["peer_sub_keys"].reshape(HP, PEER_KEYS, -1).transpose(2, 0, 1),
        "peer_u": i["peer_u"].reshape(PEER_KEYS, PEER_KEYS, KD, P).transpose(0, 3, 2, 1).reshape(PEER_KEYS, P, D),
        "peer_v": i["peer_v"].reshape(PEER_KEYS, PEER_KEYS, D),
        "final_norm_w": i["final_norm_w"][None],
        "meta_2": i["meta_2"], "norm1_g": per_partition(i["norm1_g_2"]), "w_in_2": w2,
        "w_index": np.concatenate([q_idx] + [k_idx] * 4, 1),
        "w_latent": np.concatenate([w2[:, at[2]:at[3]], w_idx], 1),
        "b_gate": per_partition(i["b_gate_2"]),
        "pool_w": i["pool_w_2"][0].transpose(1, 0, 2), "pool_scale": per_partition(i["pool_scale_2"]),
        "w_a": rows(i["w_a_2"]), "kv_norm_g": i["kv_norm_g_2"], "w_b": rows(i["w_b_2"]),
        "conv_w": i["conv_w_2"][0].reshape(3, POOL_GROUPS, P).transpose(2, 0, 1),
        "w_c": rows(i["w_c_2"]), "w_o": rows(i["w_o_2"]), "norm2_g": per_partition(i["norm2_g_2"]),
        "w_gate_up": gate_up.transpose(0, 2, 1, 3).reshape(D, 2 * FF),
        "w_down": rows(i["w_down_2"]), "final_g": i["final_g_2"][None],
    }


SCRATCH = {"h1": (T, D), "experts": (T, D), "x2": (T, D), "hn_hi": (P, KD, T), "hn_lo": (P, KD, T)}


def kernel(**inputs):
    import concourse.bacc as bacc
    from concourse.bass_utils import run_bass_kernel_spmd

    nc = bacc.Bacc("TRN2", target_bir_lowering=False, num_devices=1)
    arrays, io = {}, {}
    for name, a in layouts({n: np.asarray(a) for n, a in inputs.items()}).items():
        a = np.ascontiguousarray(a)
        arrays[f"in_{name}"] = a
        io[name] = nc.dram_tensor(f"in_{name}", a.shape, mybir.dt.from_np(a.dtype), kind="ExternalInput").ap()
    for name, shape in SCRATCH.items():
        io[name] = nc.dram_tensor(f"scratch_{name}", shape, F32, kind="Internal").ap()
    io["out"] = nc.dram_tensor("out", (T, D), F32, kind="ExternalOutput").ap()
    program(nc, io)
    got = run_bass_kernel_spmd(nc, [arrays], core_ids=[0])
    return got.results[0]["out"].reshape(1, T, D)
```

```python
import math
from contextlib import ExitStack

import numpy as np

import concourse.bass as bass
from concourse import mybir

F32 = mybir.dt.float32
F32R = mybir.dt.float32r
BF16 = mybir.dt.bfloat16
U32 = mybir.dt.uint32
ALU = mybir.AluOpType
ACT = mybir.ActivationFunctionType
AX = mybir.AxisListType

P = 128
D = 1024
KD = D // P
T = 512
NT = T // P
META = 16
TM = META + T
HM = TM // 2
BANK = 512
NBANK = 8
SLAB = 2
SLOTS = 4
EPS = 1e-6
NEG = -3.0e38
FILL = -1.0e30

DA_HEADS, DA_DIM, DA_V = 4, 64, 128
ROPE = DA_DIM // 4
HALF = ROPE // 2
THETA = 500000.0
LAM_INIT = 0.8 - 0.6 * math.exp(-0.3 * 0)
GLA_HEADS, GLA_DK, GLA_DV, GLA_TAU, CHUNK, RANK = 4, 64, 128, 16.0, 64, 16
NCHUNK = T // CHUNK

CONSTS = {}


def _const_layout():
    at = 0
    for name, width in (("ident", P), ("causal", P), ("causal_fill", P), ("iota", P), ("sum_f", P + 2),
                        ("sum_b", P + 2), ("sum_m", META), ("keep_f", GLA_HEADS * P), ("keep_b", GLA_HEADS * P),
                        ("cos", (NT + 1) * 8 * HALF), ("sin", (NT + 1) * 8 * HALF)):
        CONSTS[name] = (at, at + width)
        at += width
    return at


CONST_W = _const_layout()
CONST_2_W = CONSTS["causal_fill"][1]


def const_table():
    table = np.zeros((P, CONST_W), np.float32)

    def put(name, value):
        a, b = CONSTS[name]
        table[:value.shape[0], a:b] = value.reshape(value.shape[0], b - a)

    j, i = np.arange(P)[:, None], np.arange(P)[None, :]
    same = (j // CHUNK) == (i // CHUNK)
    mid = CHUNK // 2
    upto = same & (j % CHUNK <= mid)
    frm = same & (j % CHUNK >= mid)
    put("ident", np.eye(P, dtype=np.float32))
    put("iota", np.tile(np.arange(P, dtype=np.float32), (P, 1)))
    half = np.arange(2)[None, :] * CHUNK
    for name, along, to_mid in (("sum_f", same & (j <= i), upto), ("sum_b", same & (j >= i), frm)):
        shifted = (along.astype(np.float32) - to_mid) / GLA_TAU
        mids = to_mid[:, [0, CHUNK]].astype(np.float32) / GLA_TAU
        put(name, np.concatenate([shifted, mids], 1))
    jm, im = np.arange(META)[:, None], np.arange(META)[None, :]
    put("sum_m", ((jm <= im).astype(np.float32) - 1.0) / GLA_TAU)
    put("keep_f", np.tile((same & (j <= i)).astype(np.float32), (1, GLA_HEADS)))
    put("keep_b", np.tile((same & (j >= i)).astype(np.float32), (1, GLA_HEADS)))
    put("causal", (i <= j).astype(np.float32))
    put("causal_fill", np.where(i <= j, 0.0, FILL).astype(np.float32))
    inv = np.power(np.float32(THETA), -np.arange(0, ROPE, 2, dtype=np.float32) / np.float32(ROPE)).astype(np.float32)
    for name, f in (("cos", np.cos), ("sin", np.sin)):
        v = np.zeros((P, NT + 1, 8, HALF), np.float32)
        for t in range(NT + 1):
            n = P if t < NT else META
            pos = (np.arange(n) + (META + t * P if t < NT else 0)).astype(np.float32)
            v[:n, t] = f((pos[:, None] * inv[None, :]).astype(np.float32)).astype(np.float32)[:, None, :]
        put(name, v)
    return table


class Chain:

    def __init__(self, eng, sem):
        self.eng, self.sem, self.n = eng, sem, 0
        self.turn, self.per_turn = None, 0

    def __call__(self, ins):
        ins.then_inc(self.sem, 1)
        self.n += 1
        now = self.n if self.turn is None else self.n + self.turn * self.per_turn
        self.eng.wait_ge(self.sem, now)

    def loop(self, turn, per_turn):
        self.turn, self.per_turn, self.start = turn, per_turn, self.n

    def end_loop(self, turns):
        assert self.n - self.start == self.per_turn, (self.n - self.start, self.per_turn)
        self.n = self.start + self.per_turn * turns
        self.turn = None


SEMAPHORES = []


def clear_semaphores(nc):
    with nc.Block() as block:

        @block.gpsimd
        def _(pool):
            nc.clear_and_free_semaphores(SEMAPHORES)
    SEMAPHORES.clear()


class Scope:

    def __init__(self, nc, ctx, name):
        self.nc, self.ctx, self.name = nc, ctx, name

    def sb(self, name, shape, dt=F32, side="left"):
        return self.ctx.enter_context(self.nc.sbuf_tensor(f"{self.name}_{name}", shape, dt, side=side))

    def sem(self, name):
        sem = self.nc.alloc_semaphore(f"{self.name}_{name}")
        SEMAPHORES.append(sem)
        return sem

    def block(self):
        return self.ctx.enter_context(self.nc.Block())


class WeightRing:

    def __init__(self, s, side="left"):
        self.raw = s.sb("w_raw", [P, SLOTS, SLAB, BANK], side=side)
        self.hi = s.sb("w_hi", [P, SLOTS, SLAB, BANK], F32R, side=side)
        self.lo = s.sb("w_lo", [P, SLOTS, SLAB, BANK], F32R, side=side)
        self.next = 0
        self.landed = [s.sem(f"w_landed{k}") for k in range(SLOTS)]
        self.raw_free = s.sem("w_raw_free")
        self.hi_ready = s.sem("w_hi_ready")
        self.lo_ready = s.sem("w_lo_ready")
        self.slot_free = s.sem("w_slot_free")

    def open_raw(self, pool):
        pool.sem_inc(self.raw_free, SLOTS)

    def open_slots(self, pe):
        pe.sem_inc(self.slot_free, SLOTS - 1)

    def load(self, sp, n, slot, src, parts=None):
        sp.wait_ge(self.raw_free, n + 1)
        width = src.shape[2]
        sp.dma_start(self.raw[:, slot, :src.shape[1], :width], src).then_inc(self.landed[slot], 16)

    def round_hi(self, act, n, slot, turn, width=BANK, rows=SLAB):
        act.wait_ge(self.landed[slot], (turn + 1) * 16)
        act.wait_ge(self.slot_free, n + 1)
        act.activation(self.hi[:, slot, :rows, :width], self.raw[:, slot, :rows, :width], ACT.Copy)\
            .then_inc(self.hi_ready, 1)

    def take_lo(self, pool, n, slot, width=BANK, rows=SLAB):
        pool.wait_ge(self.hi_ready, n + 1)
        pool.tensor_tensor(self.lo[:, slot, :rows, :width], self.raw[:, slot, :rows, :width],
                           self.hi[:, slot, :rows, :width].bitcast(F32), ALU.subtract)\
            .then_inc(self.lo_ready, 1)
        pool.wait_ge(self.lo_ready, n + 1)
        pool.sem_inc(self.raw_free, 1)


def split_products(pe, out, lhs, rhs, start, stop, skip=False, frees=None):
    first = pe.matmul(out, lhs[0], rhs[0], start=start, stop=False, skip_group_check=skip)
    if frees is not None:
        first.then_inc(frees, 1)
    pe.matmul(out, lhs[0], rhs[1], start=False, stop=False, skip_group_check=skip)
    return pe.matmul(out, lhs[1], rhs[0], start=False, stop=stop, skip_group_check=skip)


def weight_slab(w, s, c0, width=BANK, rows=SLAB):
    return w.rearrange("(k p) n -> p k n", p=P)[:, SLAB * s:SLAB * s + rows, bass.ds(c0, width)]


AHEAD, REST = slice(0, SLOTS - 1), slice(SLOTS - 1, None)


class Gemm:

    def __init__(self, s, ring, bank, name=""):
        self.ring, self.bank = ring, bank
        self.tile_done, self.bank_free = s.sem(name + "tile_done"), s.sem(name + "bank_free")
        self.slab0, self.tile0 = ring.next, 0

    def plan(self, blocks, turns=1):
        slab, tile = self.slab0, self.tile0
        for b in blocks:
            b["slab0"], b["slabs"] = slab, -(-b["ktiles"] // SLAB)
            slab += b["slabs"]
            if b["kind"] == "rows":
                b["ms"] = list(range(NT)) + [-1] * b["meta"]
            else:
                b["ms"] = [(m, half) for m in range(b["width"] // P) for half in range(1 + b["meta"])]
            b["tile0"] = tile
            tile += len(b["ms"])
        if turns > 1:
            assert (slab - self.slab0) % SLOTS == 0 and (tile - self.tile0) % NBANK == 0
        per = (slab - self.slab0, tile - self.tile0)
        for b in blocks:
            b["per"] = per
        self.slab0 += turns * per[0]
        self.tile0 += turns * per[1]
        self.ring.next = self.slab0
        return blocks

    def open_banks(self, taker):
        taker.sem_inc(self.bank_free, NBANK)

    def ahead(self, block):
        at = self.slab0, self.tile0
        found = self.plan([dict(block)])[0]
        self.slab0, self.tile0 = at
        self.ring.next = self.slab0
        return found

    def on_sync(self, sp, b, turn=0, part=slice(None)):
        for i in range(b["slabs"])[part]:
            n = b["slab0"] + i
            self.ring.load(sp, n + turn * b["per"][0], n % SLOTS, b["slab"](i, turn))

    def on_scalar(self, act, b, turn=0, part=slice(None)):
        for i in range(b["slabs"])[part]:
            n = b["slab0"] + i
            self.ring.round_hi(act, n + turn * b["per"][0], n % SLOTS,
                               n // SLOTS + turn * (b["per"][0] // SLOTS), b["width"])

    def on_gpsimd(self, pool, b, turn=0, part=slice(None)):
        for i in range(b["slabs"])[part]:
            n = b["slab0"] + i
            self.ring.take_lo(pool, n + turn * b["per"][0], n % SLOTS, b["width"])

    def on_tensor(self, pe, b, turn=0):
        ring = self.ring
        for i in range(b["slabs"]):
            n = b["slab0"] + i
            pe.wait_ge(ring.lo_ready, n + 1 + turn * b["per"][0])
            for kk in range(SLAB):
                kt = i * SLAB + kk
                first, final = kt == 0, kt == b["ktiles"] - 1
                for j, m in enumerate(b["ms"]):
                    n_tile = b["tile0"] + j
                    if first:
                        pe.wait_ge(self.bank_free, n_tile + 1 + turn * b["per"][1])
                    frees = ring.slot_free if kk == 0 and j == 0 else None
                    out = self.bank[:, n_tile % NBANK, :]
                    wh, wl = ring.hi[:, n % SLOTS, kk, :], ring.lo[:, n % SLOTS, kk, :]
                    if b["kind"] == "rows":
                        w = (wh[:, 0:b["width"]], wl[:, 0:b["width"]])
                        last = split_products(pe, out[:, 0:b["width"]], b["x"](kt, m), w, first, final, frees=frees)
                    else:
                        c = slice(m[0] * P, (m[0] + 1) * P)
                        x = b["x"](kt, m[1])
                        last = split_products(pe, out[:, 0:x[0].shape[-1]], (wh[:, c], wl[:, c]), x, first, final,
                                              frees=frees)
                    if final:
                        last.then_inc(self.tile_done, 1)

    def take(self, eng, b, use, turn=0):
        for j, m in enumerate(b["ms"]):
            n = b["tile0"] + j
            eng.wait_ge(self.tile_done, n + 1 + turn * b["per"][1])
            use(j, m, self.bank[:, n % NBANK, :]).then_inc(self.bank_free, 1)



class RowStats:

    def __init__(self, s, rows, meta, name="n_", junk=None):
        self.rows, self.meta, self.width = rows, meta, rows.shape[2]
        self.tiles = NT + (meta is not None)
        self.junk = s.sb(name + "junk", [P, self.width]) if junk is None else junk
        self.ss, self.root = s.sb(name + "ss", [P, NT + 1]), s.sb(name + "root", [P, NT + 1])
        self.rstd = s.sb(name + "rstd", [P, NT + 1])
        self.squared, self.meaned, self.rooted = s.sem(name + "squared"), s.sem(name + "mean"), s.sem(name + "root")

    def tile(self, t):
        return (self.rows[:, t, :], P) if t < NT else (self.meta[:, :], META)

    def on_scalar(self, act, ready):
        for t in range(self.tiles + 1):
            if t < self.tiles:
                ready(act, t)
                if t:
                    act.wait_ge(self.squared, t)
                src, n = self.tile(t)
                act.activation(self.junk[0:n, :], src, ACT.Square, accum_out=self.ss[0:n, t:t + 1])\
                    .then_inc(self.squared, 1)
            if t:
                n = self.tile(t - 1)[1]
                act.wait_ge(self.meaned, t)
                act.activation(self.root[0:n, t - 1:t], self.ss[0:n, t - 1:t], ACT.Sqrt).then_inc(self.rooted, 1)

    def on_vector(self, dve, chain, use):
        for t in range(self.tiles + 1):
            if t < self.tiles:
                n = self.tile(t)[1]
                dve.wait_ge(self.squared, t + 1)
                dve.tensor_scalar(self.ss[0:n, t:t + 1], self.ss[0:n, t:t + 1], 1.0 / self.width, EPS, ALU.mult,
                                  ALU.add).then_inc(self.meaned, 1)
            if t:
                n = self.tile(t - 1)[1]
                dve.wait_ge(self.rooted, t)
                chain(dve.reciprocal(self.rstd[0:n, t - 1:t], self.root[0:n, t - 1:t]))
                use(t - 1)


class NormColumns:

    def __init__(self, s, rows, meta, gain_col, hi, lo, ident, bank, xs=None, junk=None,
                 gain_landed=None):
        self.gain_landed = gain_landed
        self.stats = RowStats(s, rows, meta, junk=junk)
        self.meta, self.gain, self.hi, self.lo, self.ident, self.bank = meta, gain_col, hi, lo, ident, bank
        self.xs = s.sb("n_xs", [P, self.stats.tiles, D]) if xs is None else xs
        self.mtmp = s.sb("n_mtmp", [P, KD, META]) if meta is not None else None
        self.scaled, self.turned = s.sem("n_scaled"), s.sem("n_turned")
        self.hi_done, self.done = s.sem("n_hi"), s.sem("n_done")
        off = META if meta is not None else 0
        self.cols = slice(off, off + T)

    def on_scalar(self, act, ready, between=None):
        self.stats.on_scalar(act, ready)
        if between:
            between()
        if self.gain_landed is not None:
            act.wait_ge(self.gain_landed, 16)
        for k in range(KD):
            act.wait_ge(self.turned, k + 1)
            act.activation(self.hi[:, k, self.cols], self.bank[:, k, :], ACT.Copy,
                           scale=self.gain[:, k:k + 1]).then_inc(self.hi_done, 1)

    def on_vector(self, dve, chain):
        def scale(t):
            src, n = self.stats.tile(t)
            dve.tensor_scalar(self.xs[0:n, t, :], src, self.stats.rstd[0:n, t:t + 1], None, ALU.mult)\
                .then_inc(self.scaled, 1)

        self.stats.on_vector(dve, chain, scale)
        if self.gain_landed is not None:
            dve.wait_ge(self.gain_landed, 16)
        for k in range(KD):
            dve.wait_ge(self.hi_done, k + 1)
            dve.scalar_tensor_tensor(self.lo[:, k, self.cols], self.bank[:, k, :], self.gain[:, k:k + 1],
                                     self.hi[:, k, self.cols].bitcast(F32), ALU.mult, ALU.subtract)\
                .then_inc(self.done, 1)
        if self.meta is not None:
            dve.wait_ge(self.turned, KD + 1)
            src = self.bank[:, 0, 0:KD * META].rearrange("p (k m) -> p k m", k=KD)
            gain = self.gain[:, :].unsqueeze(2).to_broadcast([P, KD, META])
            chain(dve.tensor_tensor(self.mtmp[:, :, :], src, gain, ALU.mult))
            hi = self.hi[:, :, 0:META]
            chain(dve.tensor_copy(hi, self.mtmp[:, :, :]))
            dve.tensor_tensor(self.lo[:, :, 0:META], self.mtmp[:, :, :], hi.bitcast(F32), ALU.subtract)\
                .then_inc(self.done, 1)

    def total(self):
        return KD + (self.meta is not None)

    def on_tensor(self, pe):
        for t in range(NT):
            pe.wait_ge(self.scaled, t + 1)
            for k in range(KD):
                last = pe.transpose(self.bank[:, k, t * P:(t + 1) * P], self.xs[:, t, k * P:(k + 1) * P],
                                    self.ident)
                if t == NT - 1:
                    last.then_inc(self.turned, 1)
        if self.meta is not None:
            pe.wait_ge(self.scaled, NT + 1)
            pe.wait_ge(self.done, 1)
            for k in range(KD):
                last = pe.transpose(self.bank[:, 0, k * META:(k + 1) * META],
                                    self.xs[0:META, NT, k * P:(k + 1) * P], self.ident[0:META, 0:META])
            last.then_inc(self.turned, 1)



def phase_project_1(nc, bank, const, io, life):
    with ExitStack() as ctx:
        s = Scope(nc, ctx, "p1")
        h, hm = s.sb("h", [P, NT, D]), s.sb("h_meta", [META, D])
        xh, xl = s.sb("xh", [P, KD, TM], F32R), s.sb("xl", [P, KD, TM], F32R)
        gain = s.sb("gain", [P, KD])
        ring = WeightRing(s)
        gemm = Gemm(s, ring, bank)
        c_landed, g_landed = s.sem("const_landed"), s.sem("gain_landed")
        x_landed = [s.sem(f"x_landed{t}") for t in range(NT + 1)]
        vec = s.sem("vector_steps")
        ident = const[:, CONSTS["ident"][0]:CONSTS["ident"][1]]
        norm = NormColumns(s, h, hm, gain, xh, xl, ident, bank, gain_landed=g_landed)

        def rows(kt, m):
            c = slice(META + m * P, META + (m + 1) * P) if m >= 0 else slice(0, P)
            return xh[:, kt, c], xl[:, kt, c]

        def columns(kt, half):
            c = slice(half * HM, (half + 1) * HM)
            return xh[:, kt, c], xl[:, kt, c]

        def part(kind, c0, width, meta, dst, dst_meta):
            return dict(kind=kind, slab=lambda i, turn: weight_slab(io["w_in"], i, c0, width), width=width,
                        ktiles=KD, x=rows if kind == "rows" else columns, meta=meta, dst=dst, dst_meta=dst_meta)

        L = life
        blocks = gemm.plan([
            part("rows", 0, BANK, False, L["q"], None), part("rows", 512, BANK, True, L["k"], L["k_m"]),
            part("rows", 1024, BANK, True, L["v"], L["v_m"]), part("columns", 1536, BANK, True, L["gqk"], None),
            part("rows", 2048, BANK, True, L["gv"], L["gv_m"]), part("rows", 2560, BANK, False, L["gr"], None),
            part("columns", 2976, P, True, L["zT"], None)])
        block = s.block()

        @block.sync
        def _(sp):
            sp.dma_start(gain[:, :], io["ln1_w"]).then_inc(g_landed, 16)
            sp.dma_start(const[:, 0:P], io["const"][:, 0:P]).then_inc(c_landed, 16)
            for t in range(NT):
                sp.dma_start(h[:, t, :], io["x"][t * P:(t + 1) * P, :]).then_inc(x_landed[t], 16)
            sp.dma_start(hm[:, :], io["meta_tokens"]).then_inc(x_landed[NT], 16)
            for n, b in enumerate(blocks):
                gemm.on_sync(sp, b)
                if n == 0:
                    sp.dma_start(const[:, P:CONST_W], io["const"][:, P:CONST_W]).then_inc(c_landed, 16)
            sp.wait_ge(c_landed, 32)

        @block.gpsimd
        def _(pool):
            ring.open_raw(pool)
            for b in blocks:
                gemm.on_gpsimd(pool, b)

        @block.scalar
        def _(act):
            norm.on_scalar(act, lambda e, t: e.wait_ge(x_landed[t], 16),
                           lambda: gemm.on_scalar(act, blocks[0], 0, AHEAD))
            gemm.on_scalar(act, blocks[0], 0, REST)
            for b in blocks[1:]:
                gemm.on_scalar(act, b)

        @block.tensor
        def _(pe):
            ring.open_slots(pe)
            pe.wait_ge(c_landed, 16)
            norm.on_tensor(pe)
            pe.wait_ge(norm.done, norm.total())
            for b in blocks:
                gemm.on_tensor(pe, b)

        @block.vector
        def _(dve):
            chain = Chain(dve, vec)
            gemm.open_banks(dve)
            for landed in x_landed:
                dve.wait_ge(landed, 16)
            norm.on_vector(dve, chain)
            for b in blocks:
                def use(j, m, got):
                    if b["kind"] == "rows":
                        return (dve.tensor_copy(b["dst"][:, m, :], got) if m >= 0 else
                                dve.tensor_copy(b["dst_meta"][:, :], got[0:META, :]))
                    f, half = m
                    return dve.tensor_copy(b["dst"][:, f, half * HM:(half + 1) * HM], got[:, 0:HM])

                gemm.take(dve, b, use)



def phase_diff_attention(nc, bank, const, io, life):
    with ExitStack() as ctx:
        s = Scope(nc, ctx, "da")
        q, k, km, v, vm, mix = (life[n] for n in ("q", "k", "k_m", "v", "v_m", "mix"))
        qT = s.sb("qT", [P, DA_HEADS, T])
        kT = s.sb("kT", [P, DA_HEADS, TM])
        rot = s.sb("rot", [P, 4, NT * 8 * HALF])
        p = s.sb("p", [P, 2, 2, TM])
        a = s.sb("a", [P, 2, TM])
        aT = s.sb("aT", [P, 2, T])
        aTm = s.sb("aTm", [META, 2, P])
        nmax, total, inv = s.sb("nmax", [P, 4]), s.sb("total", [P, 4]), s.sb("inv", [P, 4])
        lam_in = s.sb("lam_in", [P, 4, DA_DIM])
        lam_prod = s.sb("lam_prod", [P, 2, DA_DIM])
        lam_sum, lam = s.sb("lam_sum", [P, 2]), s.sb("lam", [P, 2])
        in_landed = s.sem("in_landed")
        turned_q, turned_k, cols_ready = s.sem("rot_q"), s.sem("rot_k"), s.sem("cols_ready")
        tp, lam_exp, lam_done = s.sem("transposed"), s.sem("lam_exp"), s.sem("lam_done")
        scored, maxed, exped = s.sem("scored"), s.sem("maxed"), s.sem("exped")
        diffed, a_turned, aT_ready = s.sem("diffed"), s.sem("a_turned"), s.sem("aT_ready")
        o_done, o_taken = s.sem("o_done"), s.sem("o_taken")
        vec = s.sem("vector_steps")
        ident = const[:, CONSTS["ident"][0]:CONSTS["ident"][1]]

        def angles(name, t0, t1, n):
            c0 = CONSTS[name][0] + t0 * 8 * HALF
            return const[0:n, c0:c0 + (t1 - t0) * 8 * HALF].rearrange("p (t h c) -> p t h c", h=8, c=HALF)

        turns = [(hd, t) for hd in range(DA_HEADS) for t in range(NT)]

        def pair(r, c):
            return 2 * c

        def scores_of(r, c):
            return bank[:, pair(r, c):pair(r, c) + 2, :].rearrange("p b n -> p (b n)")[:, 0:TM]

        O_BANK, M_BANK, W_BANK = 4, 5, 6
        block = s.block()

        @block.sync
        def _(sp):
            for n, name in enumerate(("da_lambda_q1", "da_lambda_k1", "da_lambda_q2", "da_lambda_k2")):
                sp.dma_start(lam_in[:, n, :], io[name].to_broadcast([P, DA_DIM])).then_inc(in_landed, 16)

        @block.scalar
        def _(act):
            act.wait_ge(lam_done, 1)
            act.activation(lam[:, :], lam_sum[:, :], ACT.Exp).then_inc(lam_exp, 1)
            for r in range(len(turns) + 3):
                if r >= 3:
                    e = r - 3
                    act.wait_ge(a_turned, e + 1)
                    if e >= 2:
                        act.wait_ge(o_done, e - 1)
                    act.activation(aTm[:, e % 2, :], bank[0:META, M_BANK, 0:P], ACT.Copy)
                    act.activation(aT[:, e % 2, :], bank[:, W_BANK + e % 2, :], ACT.Copy).then_inc(aT_ready, 1)
                if r < len(turns):
                    for c in range(2):
                        u = 2 * r + c
                        act.wait_ge(maxed, u + 1)
                        if r >= 2:
                            act.wait_ge(diffed, r - 1)
                        act.activation(p[:, r % 2, c, :], scores_of(r, c), ACT.Exp,
                                       bias=nmax[:, u % 4:u % 4 + 1], accum_out=total[:, u % 4:u % 4 + 1])\
                            .then_inc(exped, 1)

        @block.tensor
        def _(pe):
            def columns(n, src, sem, count):
                pe.wait_ge(sem, count)
                if n >= 4:
                    pe.wait_ge(cols_ready, n - 3)
                for t in range(NT):
                    last = pe.transpose(bank[:, n % 4, t * P:(t + 1) * P], src(t), ident)
                last.then_inc(tp, 1)

            for hd in range(DA_HEADS):
                columns(hd, lambda t: q[:, t, hd * P:(hd + 1) * P], turned_q, 1)
            for hd in range(DA_HEADS):
                columns(DA_HEADS + hd, lambda t: k[:, t, hd * P:(hd + 1) * P], turned_k, 2)
            for hd in range(DA_HEADS):
                last = pe.transpose(bank[:, 4, hd * META:(hd + 1) * META], km[:, hd * P:(hd + 1) * P],
                                    ident[0:META, 0:META])
            last.then_inc(tp, 1)
            pe.wait_ge(cols_ready, 2 * DA_HEADS + 1)
            for r in range(len(turns) + 3):
                if r < len(turns):
                    hd, t = turns[r]
                    for c in range(2):
                        u = 2 * r + c
                        if r:
                            pe.wait_ge(exped, u - 1)
                        cc = slice(c * DA_DIM, (c + 1) * DA_DIM)
                        b = pair(r, c)
                        pe.matmul(bank[:, b, :], qT[cc, hd, t * P:(t + 1) * P], kT[cc, hd, 0:BANK],
                                  start=True, stop=True)
                        pe.matmul(bank[:, b + 1, 0:TM - BANK], qT[cc, hd, t * P:(t + 1) * P],
                                  kT[cc, hd, BANK:TM], start=True, stop=True).then_inc(scored, 1)
                if 2 <= r <= len(turns) + 1:
                    e = r - 2
                    pe.wait_ge(diffed, e + 1)
                    pe.wait_ge(aT_ready, e)
                    pe.transpose(bank[0:META, M_BANK, 0:P], a[:, e % 2, 0:META], ident)
                    for kt in range(NT):
                        last = pe.transpose(bank[:, W_BANK + e % 2, kt * P:(kt + 1) * P],
                                            a[:, e % 2, META + kt * P:META + (kt + 1) * P], ident)
                    last.then_inc(a_turned, 1)
                if r >= 3:
                    e = r - 3
                    hd = turns[e][0]
                    pe.wait_ge(aT_ready, e + 1)
                    if e:
                        pe.wait_ge(o_taken, e)
                    o = bank[:, O_BANK, 0:DA_V]
                    pe.matmul(o, aTm[:, e % 2, :], vm[:, hd * DA_V:(hd + 1) * DA_V], start=True, stop=False)
                    for kt in range(NT):
                        last = pe.matmul(o, aT[:, e % 2, kt * P:(kt + 1) * P],
                                         v[:, kt, hd * DA_V:(hd + 1) * DA_V], start=False, stop=kt == NT - 1)
                    last.then_inc(o_done, 1)

        @block.vector
        def _(dve):
            chain = Chain(dve, vec)

            def rotate(rows, t0, t1, n):
                x1, x2 = rows[:, :, :, 0:HALF], rows[:, :, :, HALF:ROPE]
                cos, sin = angles("cos", t0, t1, n), angles("sin", t0, t1, n)
                w = (t1 - t0) * 8 * HALF
                r = [rot[0:n, i, 0:w].rearrange("p (t h c) -> p t h c", h=8, c=HALF) for i in range(4)]
                dve.tensor_tensor(r[0], x1, cos, ALU.mult)
                dve.tensor_tensor(r[1], x2, sin, ALU.mult)
                dve.tensor_tensor(r[2], x2, cos, ALU.mult)
                chain(dve.tensor_tensor(r[3], x1, sin, ALU.mult))
                dve.tensor_tensor(x1, r[0], r[1], ALU.subtract)
                return dve.tensor_tensor(x2, r[2], r[3], ALU.add)

            def split(ap):
                return ap.rearrange("p t (h c) -> p t h c", h=8)

            ins = rotate(split(q[:, :, :]), 0, NT, P)
            ins.then_inc(turned_q, 1)
            dve.wait_ge(turned_q, 1)
            ins = rotate(split(k[:, :, :]), 0, NT, P)
            ins.then_inc(turned_k, 1)
            dve.wait_ge(turned_k, 1)
            ins = rotate(km[:, :].rearrange("p (t h c) -> p t h c", t=1, h=8), NT, NT + 1, META)
            ins.then_inc(turned_k, 1)
            dve.wait_ge(in_landed, 16 * 4)
            for n in range(2):
                chain(dve.tensor_tensor(lam_prod[:, n, :], lam_in[:, 2 * n, :], lam_in[:, 2 * n + 1, :], ALU.mult))
            dve.tensor_reduce(lam_sum[:, :], lam_prod[:, :, :], AX.X, ALU.add).then_inc(lam_done, 1)
            dve.wait_ge(lam_exp, 1)
            chain(dve.tensor_tensor(lam[:, 0:1], lam[:, 1:2], lam[:, 0:1], ALU.subtract))
            chain(dve.tensor_scalar(lam[:, 0:1], lam[:, 0:1], -LAM_INIT, None, ALU.add))

            for hd in range(DA_HEADS):
                dve.wait_ge(tp, hd + 1)
                dve.tensor_scalar(qT[:, hd, :], bank[:, hd % 4, :], DA_DIM ** -0.5, None, ALU.mult)\
                    .then_inc(cols_ready, 1)
            for hd in range(DA_HEADS):
                dve.wait_ge(tp, DA_HEADS + hd + 1)
                dve.tensor_copy(kT[:, hd, META:TM], bank[:, hd % 4, :]).then_inc(cols_ready, 1)
            dve.wait_ge(tp, 2 * DA_HEADS + 1)
            dve.tensor_copy(kT[:, :, 0:META],
                            bank[:, 4, 0:DA_HEADS * META].rearrange("p (h m) -> p h m", m=META))\
                .then_inc(cols_ready, 1)

            def take_output(e):
                hd, t = turns[e]
                dve.wait_ge(o_done, e + 1)
                dve.tensor_copy(mix[:, t, hd * DA_V:(hd + 1) * DA_V], bank[:, O_BANK, 0:DA_V])\
                    .then_inc(o_taken, 1)

            def maximum(r, c):
                u = 2 * r + c
                dve.wait_ge(scored, u + 1)
                if u >= 4:
                    dve.wait_ge(exped, u - 3)
                dve.tensor_reduce(nmax[:, u % 4:u % 4 + 1], scores_of(r, c), AX.X, ALU.max, negate=True)\
                    .then_inc(maxed, 1)

            for r in range(len(turns) + 4):
                if r >= 4:
                    take_output(r - 4)
                if r < len(turns):
                    maximum(r, 0)
                if 1 <= r <= len(turns):
                    e = r - 1
                    o = 2 * (e % 2)
                    dve.wait_ge(exped, 2 * e + 2)
                    if e >= 2:
                        dve.wait_ge(a_turned, e - 1)
                    chain(dve.reciprocal(inv[:, o:o + 2], total[:, o:o + 2]))
                    dve.tensor_scalar(a[:, e % 2, :], p[:, e % 2, 0, :], inv[:, o:o + 1], None, ALU.mult)
                    chain(dve.tensor_tensor(inv[:, o + 1:o + 2], inv[:, o + 1:o + 2], lam[:, 0:1], ALU.mult))
                    dve.scalar_tensor_tensor(a[:, e % 2, :], p[:, e % 2, 1, :], inv[:, o + 1:o + 2],
                                             a[:, e % 2, :], ALU.mult, ALU.add).then_inc(diffed, 1)
                if r < len(turns):
                    maximum(r, 1)



def phase_linear_attention(nc, bank, const, io, life):
    with ExitStack() as ctx:
        s = Scope(nc, ctx, "gla")
        qk, zT, gv, gvm, gr, mix = (life[n] for n in ("gqk", "zT", "gv", "gv_m", "gr", "mix"))
        FW, BW = 0, 1
        GK = GLA_HEADS * GLA_DK
        w2 = s.sb("w2", [P, 2 * GK])
        w2_bias = s.sb("w2_bias", [P, 2 * GK])
        y, e = s.sb("y", [P, NT + 1, 2 * GK]), s.sb("e", [P, NT + 1, 2 * GK])
        grow, shrink = life["q"], life["k"]
        qs, ks = s.sb("qs", [P, 4, T]), s.sb("ks", [P, 4, T])
        mid, decay = s.sb("mid", [P, 4, NCHUNK]), s.sb("decay", [P, 4, NCHUNK])
        decay_m = s.sb("decay_m", [P, 2])
        km, kmT = s.sb("km", [P, 2, META]), s.sb("kmT", [META, GK])
        ksT = s.sb("ksT", [P, 4, NT, P])
        at = s.sb("at", [P, 2, NT, GLA_HEADS * P])
        kv = s.sb("kv", [P, 4, NCHUNK, GLA_DV])
        st = s.sb("st", [P, 4, NCHUNK, GLA_DV])
        gate = gr
        names = ("w2_landed", "zeroed", "z_done", "y_done", "e_done", "ln_done", "lg_done", "b_done", "grown",
                 "qk_done", "mid_taken", "decay_sum", "decayed", "km_done", "k_turned", "k_taken", "a_done",
                 "a_taken", "kv_done", "kv_taken", "states", "o_done", "o_taken",
                 "gated", "da_squared", "da_mean", "da_rooted", "vector_steps")
        da_sq = s.sb("da_sq", [P, NT * DA_HEADS, DA_V])
        da_ss, da_root = s.sb("da_ss", [P, NT * DA_HEADS]), s.sb("da_root", [P, NT * DA_HEADS])
        sub_w = s.sb("sub_w", [P, DA_V])
        S = {n: s.sem(n) for n in names}
        ident = const[:, CONSTS["ident"][0]:CONSTS["ident"][1]]

        def c(name, n=P):
            return const[0:n, CONSTS[name][0]:CONSTS[name][1]]

        sums = [c("sum_f"), c("sum_b")]
        rows96 = slice(96, 96 + 2 * RANK)
        tiles = [(t, P) for t in range(NT)] + [(NT, META)]
        block = s.block()

        @block.sync
        def _(sp):
            sp.wait_ge(S["zeroed"], 1)
            sp.dma_start(w2[96:96 + RANK, 0:GK], io["gla_gate_w2_f"]).then_inc(S["w2_landed"], 16)
            sp.dma_start(w2[96 + RANK:P, GK:2 * GK], io["gla_gate_w2_b"]).then_inc(S["w2_landed"], 16)
            sp.dma_start(w2_bias[:, 0:GK], io["gla_gate_b_f"].to_broadcast([P, GK])).then_inc(S["w2_landed"], 16)
            sp.dma_start(w2_bias[:, GK:2 * GK], io["gla_gate_b_b"].to_broadcast([P, GK]))\
                .then_inc(S["w2_landed"], 16)
            sp.dma_start(sub_w[:, :], io["da_subln_w"].to_broadcast([P, DA_V])).then_inc(S["w2_landed"], 16)

        @block.tensor
        def _(pe):
            pe.wait_ge(S["w2_landed"], 16 * 5)
            for t, n in tiles:
                cols = slice(META + t * P, META + (t + 1) * P) if t < NT else slice(0, META)
                pe.matmul(bank[0:n, t, :], zT[rows96, 0, cols], w2[rows96, :], start=True, stop=True)\
                    .then_inc(S["z_done"], 1)
            pe.wait_ge(S["lg_done"], 2)
            for g in range(4):
                for t in range(NT):
                    lg = y[:, t, g * P:(g + 1) * P]
                    last = pe.matmul(bank[:, g, t * P:(t + 1) * P], lg, sums[g // 2][:, 0:P], start=True, stop=True)
                last.then_inc(S["b_done"], 1)
            for g in range(4):
                for t in range(NT):
                    lg = y[:, t, g * P:(g + 1) * P]
                    pe.matmul(bank[:, 5, 2 * (g * NT + t):2 * (g * NT + t) + 2], lg, sums[g // 2][:, P:P + 2],
                              start=True, stop=True)
            for m in range(2):
                last = pe.matmul(bank[:, 5, 64 + m * META:64 + (m + 1) * META], y[0:META, NT, m * P:(m + 1) * P],
                                 c("sum_m", META), start=True, stop=True)
            last.then_inc(S["b_done"], 1)
            for g in range(4):
                pe.wait_ge(S["qk_done"], g + 1)
                if g >= 2:
                    pe.wait_ge(S["k_taken"], g - 1)
                for t in range(NT):
                    last = pe.transpose(bank[:, 6 + g % 2, t * P:(t + 1) * P], ks[:, g, t * P:(t + 1) * P], ident)
                last.then_inc(S["k_turned"], 1)
            pe.wait_ge(S["km_done"], 1)
            pe.wait_ge(S["k_taken"], 4)
            for m in range(2):
                last = pe.transpose(bank[0:META, 6, m * P:(m + 1) * P], km[:, m, :], ident)
            last.then_inc(S["k_turned"], 1)
            for t in range(NT):
                if t == 0:
                    pe.wait_ge(S["grown"], 5)
                    pe.wait_ge(S["mid_taken"], 2)
                else:
                    pe.wait_ge(S["a_taken"], t)
                for d in range(2):
                    for hd in range(GLA_HEADS):
                        g, hp = 2 * d + hd // 2, hd % 2
                        r = slice(hp * GLA_DK, (hp + 1) * GLA_DK)
                        last = pe.matmul(bank[:, 2 * d + hp, (hd // 2) * P:(hd // 2 + 1) * P],
                                         ks[r, g, t * P:(t + 1) * P], qs[r, g, t * P:(t + 1) * P],
                                         start=True, stop=True)
                last.then_inc(S["a_done"], 1)
            pe.wait_ge(S["k_taken"], 5)
            for hd in range(GLA_HEADS):
                out = bank[(hd % 2) * GLA_DK:(hd % 2 + 1) * GLA_DK, 7, (hd // 2) * GLA_DV:(hd // 2 + 1) * GLA_DV]
                last = pe.matmul(out, kmT[:, hd * GLA_DK:(hd + 1) * GLA_DK],
                                 gvm[:, hd * GLA_DV:(hd + 1) * GLA_DV], start=True, stop=True)
            last.then_inc(S["kv_done"], 1)
            pe.wait_ge(S["a_taken"], NT)
            for d in range(2):
                for cp in range(2):
                    for half in range(2):
                        n = (d * 2 + cp) * 2 + half
                        b = n % 4
                        if n >= 4:
                            pe.wait_ge(S["kv_taken"], 1 + n - 3)
                        for i in range(2):
                            t = 2 * half + i
                            r = slice(cp * CHUNK, (cp + 1) * CHUNK)
                            for hd in range(GLA_HEADS):
                                m, hp = hd // 2, hd % 2
                                out = bank[hp * GLA_DK:(hp + 1) * GLA_DK, b,
                                           (i * 2 + m) * GLA_DV:(i * 2 + m + 1) * GLA_DV]
                                last = pe.matmul(out, ksT[r, 2 * d + m, t, hp * GLA_DK:(hp + 1) * GLA_DK],
                                                 gv[r, t, hd * GLA_DV:(hd + 1) * GLA_DV], start=True, stop=True)
                        last.then_inc(S["kv_done"], 1)
            pe.wait_ge(S["kv_taken"], 9)
            pe.wait_ge(S["states"], 2)
            for t in range(NT):
                for hp in range(2):
                    b = (2 * t + hp) % NBANK
                    for m in range(2):
                        hd = 2 * m + hp
                        r = slice(hp * GLA_DK, (hp + 1) * GLA_DK)
                        cols = slice(m * GLA_DV, (m + 1) * GLA_DV)
                        pe.matmul(bank[:, b, cols], at[:, 0, t, (hp * 2 + m) * P:(hp * 2 + m + 1) * P],
                                  gv[:, t, hd * GLA_DV:(hd + 1) * GLA_DV], start=True, stop=False,
                                  skip_group_check=True)
                        for cp in range(2):
                            ch = 2 * t + cp
                            out = bank[cp * CHUNK:(cp + 1) * CHUNK, b, cols]
                            toks = slice(ch * CHUNK, (ch + 1) * CHUNK)
                            for d in range(2):
                                if d == BW and ch == NCHUNK - 1:
                                    continue
                                last = pe.matmul(out, qs[r, 2 * d + m, toks], st[r, 2 * d + m, ch, :],
                                                 start=False, stop=True, skip_group_check=True)
                    last.then_inc(S["o_done"], 1)

        @block.scalar
        def _(act):
            act.activation(da_sq[:, :, :].rearrange("p (t h) v -> p t h v", t=NT),
                           mix[:, :, 0:DA_HEADS * DA_V].rearrange("p t (h v) -> p t h v", h=DA_HEADS),
                           ACT.Square).then_inc(S["da_squared"], 1)
            act.wait_ge(S["da_mean"], 1)
            act.activation(da_root[:, :], da_ss[:, :], ACT.Sqrt).then_inc(S["da_rooted"], 1)
            act.activation(gate[:, :, :], gr[:, :, :], ACT.Silu).then_inc(S["gated"], 1)
            for i, (n, ts) in enumerate(((P, slice(0, NT)), (META, slice(NT, NT + 1)))):
                act.wait_ge(S["y_done"], i + 1)
                act.activation(e[0:n, ts, :], e[0:n, ts, :], ACT.Exp, scale=-1.0).then_inc(S["e_done"], 1)
            for i, (n, ts) in enumerate(((P, slice(0, NT)), (META, slice(NT, NT + 1)))):
                act.wait_ge(S["e_done"], i + 1)
                act.activation(e[0:n, ts, :], e[0:n, ts, :], ACT.Ln, bias=1.0).then_inc(S["ln_done"], 1)
            for g in range(4):
                act.wait_ge(S["b_done"], g + 1)
                act.activation(grow[:, g, :], bank[:, g, :], ACT.Exp)
                act.activation(shrink[:, g, :], bank[:, g, :], ACT.Exp, scale=-1.0).then_inc(S["grown"], 1)
            act.wait_ge(S["b_done"], 5)
            act.activation(km[:, :, :], bank[:, 5, 64:64 + 2 * META].rearrange("p (m c) -> p m c", m=2), ACT.Exp,
                           scale=-1.0).then_inc(S["grown"], 1)
            act.wait_ge(S["decay_sum"], 1)
            act.activation(decay[:, :, :], decay[:, :, :], ACT.Exp)
            act.activation(decay_m[:, :], decay_m[:, :], ACT.Exp).then_inc(S["decayed"], 1)
            for g in range(4):
                act.wait_ge(S["k_turned"], g + 1)
                act.activation(ksT[:, g, :, :].rearrange("p t c -> p (t c)"), bank[:, 6 + g % 2, :], ACT.Copy)\
                    .then_inc(S["k_taken"], 1)
            act.wait_ge(S["k_turned"], 5)
            act.activation(kmT[:, :], bank[0:META, 6, 0:GK], ACT.Copy).then_inc(S["k_taken"], 1)
            act.wait_ge(S["decayed"], 1)
            act.wait_ge(S["kv_done"], 1)
            for m in range(2):
                last = act.activation(st[:, m, 0, :], bank[:, 7, m * GLA_DV:(m + 1) * GLA_DV], ACT.Copy,
                                      scale=decay_m[:, m:m + 1])
            last.then_inc(S["kv_taken"], 1)
            for d in range(2):
                for cp in range(2):
                    for half in range(2):
                        n = (d * 2 + cp) * 2 + half
                        act.wait_ge(S["kv_done"], n + 2)
                        for i in range(2):
                            for m in range(2):
                                g, ch = 2 * d + m, 2 * (2 * half + i) + cp
                                last = act.activation(kv[:, g, ch, :],
                                                      bank[:, n % 4, (i * 2 + m) * GLA_DV:(i * 2 + m + 1) * GLA_DV],
                                                      ACT.Copy, scale=decay[:, g, ch:ch + 1])
                        last.then_inc(S["kv_taken"], 1)

        @block.vector
        def _(dve):
            chain = Chain(dve, S["vector_steps"])
            dve.memset(w2[96:P, :], 0.0).then_inc(S["zeroed"], 1)
            dve.wait_ge(S["da_squared"], 1)
            chain(dve.tensor_reduce(da_ss[:, :], da_sq[:, :, :], AX.X, ALU.add))
            dve.tensor_scalar(da_ss[:, :], da_ss[:, :], 1.0 / DA_V, EPS, ALU.mult, ALU.add).then_inc(S["da_mean"], 1)
            dve.wait_ge(S["w2_landed"], 16 * 5)
            chain(dve.tensor_scalar(sub_w[:, :], sub_w[:, :], 1.0 - LAM_INIT, None, ALU.mult))
            dve.wait_ge(S["da_rooted"], 1)
            chain(dve.reciprocal(da_root[:, :], da_root[:, :]))
            for t in range(NT):
                for hd in range(DA_HEADS):
                    o = mix[:, t, hd * DA_V:(hd + 1) * DA_V]
                    n = t * DA_HEADS + hd
                    dve.scalar_tensor_tensor(o, o, da_root[:, n:n + 1], sub_w[:, :], ALU.mult, ALU.mult)
            for t, n in tiles:
                dve.wait_ge(S["z_done"], t + 1)
                last = dve.tensor_tensor(y[0:n, t, :], bank[0:n, t, :], w2_bias[0:n, :], ALU.add)
            chain(last)
            groups = ((P, slice(0, NT)), (META, slice(NT, NT + 1)))
            for n, ts in groups:
                dve.scalar_tensor_tensor(e[0:n, ts, :], y[0:n, ts, :], -1.0, y[0:n, ts, :], ALU.mult, ALU.max)\
                    .then_inc(S["y_done"], 1)
            for i, (n, ts) in enumerate(groups):
                dve.wait_ge(S["ln_done"], i + 1)
                dve.scalar_tensor_tensor(y[0:n, ts, :], y[0:n, ts, :], 0.0, e[0:n, ts, :], ALU.min, ALU.subtract)\
                    .then_inc(S["lg_done"], 1)
            for g in range(4):
                m = g % 2
                dve.wait_ge(S["grown"], g + 1)
                dve.scalar_tensor_tensor(qs[:, g, :], qk[:, m, META:TM], GLA_DK ** -0.5, grow[:, g, :],
                                         ALU.mult, ALU.mult)
                dve.tensor_tensor(ks[:, g, :], qk[:, 2 + m, META:TM], shrink[:, g, :], ALU.mult)\
                    .then_inc(S["qk_done"], 1)
            dve.wait_ge(S["grown"], 5)
            dve.tensor_tensor(km[:, :, :], km[:, :, :], qk[:, 2:4, 0:META], ALU.mult).then_inc(S["km_done"], 1)
            dve.wait_ge(S["b_done"], 5)
            dve.tensor_copy(mid[:, :, :], bank[:, 5, 0:4 * NCHUNK].rearrange("p (g c) -> p g c", g=4))\
                .then_inc(S["mid_taken"], 1)
            dve.wait_ge(S["mid_taken"], 1)
            dve.tensor_copy(decay_m[:, :], mid[:, 0:2, 0])
            ends = [bank[:, g, :].rearrange("p (c i) -> p c i", i=CHUNK)[:, :, CHUNK - 1 if g < 2 else 0]
                    for g in range(4)]
            for g in range(4):
                if g < 2:
                    dve.tensor_tensor(decay[:, g, 0:NCHUNK - 1], ends[g][:, 0:NCHUNK - 1], mid[:, g, 1:NCHUNK], ALU.add)
                    last = dve.tensor_copy(decay[:, g, NCHUNK - 1:NCHUNK], ends[g][:, NCHUNK - 1:NCHUNK])
                else:
                    dve.tensor_tensor(decay[:, g, 1:NCHUNK], ends[g][:, 1:NCHUNK], mid[:, g, 0:NCHUNK - 1], ALU.add)
                    last = dve.tensor_copy(decay[:, g, 0:1], ends[g][:, 0:1])
            last.then_inc(S["mid_taken"], 1)
            dve.wait_ge(S["mid_taken"], 2)
            dve.sem_inc(S["decay_sum"], 1)
            for t in range(NT):
                dve.wait_ge(S["a_done"], t + 1)
                for d, keep in ((FW, c("keep_f")), (BW, c("keep_b"))):
                    last = dve.tensor_tensor(
                        at[:, d, t, :].rearrange("p (b n) -> p b n", b=2), bank[:, 2 * d:2 * d + 2, 0:2 * P],
                        keep.rearrange("p (b n) -> p b n", b=2), ALU.mult)
                last.then_inc(S["a_taken"], 1)
                dve.wait_ge(S["a_taken"], t + 1)
                last = dve.tensor_tensor(at[:, 0, t, :], at[:, 0, t, :], at[:, 1, t, :], ALU.add)
            chain(last)
            dve.wait_ge(S["kv_taken"], 1)
            dve.wait_ge(S["decayed"], 1)
            for i in range(NCHUNK - 1):
                f, b = i, NCHUNK - 1 - i
                if i == 0:
                    dve.wait_ge(S["kv_taken"], 9)
                for m in range(2):
                    last = dve.scalar_tensor_tensor(st[:, m, f + 1, :], st[:, m, f, :], decay[:, m, f:f + 1],
                                                    kv[:, m, f, :], ALU.mult, ALU.add)
                for m in range(2, 4):
                    if i == 0:
                        last = dve.tensor_copy(st[:, m, b - 1, :], kv[:, m, b, :])
                    else:
                        last = dve.scalar_tensor_tensor(st[:, m, b - 1, :], st[:, m, b, :], decay[:, m, b:b + 1],
                                                        kv[:, m, b, :], ALU.mult, ALU.add)
                chain(last)
            dve.sem_inc(S["states"], 2)
            for t in range(NT):
                for hp in range(2):
                    dve.wait_ge(S["o_done"], 2 * t + hp + 1)
                    out = mix[:, t, 512:1024].rearrange("p (m hp v) -> p m hp v", m=2, hp=2)[:, :, hp, :]
                    dve.tensor_copy(out, bank[:, 2 * t + hp, 0:2 * GLA_DV].rearrange("p (m v) -> p m v", m=2))\
                        .then_inc(S["o_taken"], 1)


class TurnColumns:

    def __init__(self, s, rows, hi, lo, ident, bank, name="t_"):
        self.rows, self.hi, self.lo, self.ident, self.bank = rows, hi, lo, ident, bank
        self.tiles = rows.shape[2] // P
        self.turned, self.hi_done, self.done = s.sem(name + "turned"), s.sem(name + "hi"), s.sem(name + "done")

    def on_tensor(self, pe, ks):
        for k in ks:
            for t in range(NT):
                last = pe.transpose(self.bank[:, k, t * P:(t + 1) * P], self.rows[:, t, k * P:(k + 1) * P],
                                    self.ident)
            last.then_inc(self.turned, 1)

    def on_scalar(self, act, ks):
        for k in ks:
            act.wait_ge(self.turned, k + 1)
            act.activation(self.hi[:, k, :], self.bank[:, k, :], ACT.Copy).then_inc(self.hi_done, 1)

    def on_vector(self, dve, ks):
        for k in ks:
            dve.wait_ge(self.hi_done, k + 1)
            dve.tensor_tensor(self.lo[:, k, :], self.bank[:, k, :], self.hi[:, k, :].bitcast(F32), ALU.subtract)\
                .then_inc(self.done, 1)


PEER_H, PEER_KEYS, PEER_K = 8, 128, 16
HP = 2 * PEER_H



def phase_mix_out(nc, bank, const, io, life):
    with ExitStack() as ctx:
        s = Scope(nc, ctx, "mo")
        mix, h = life["mix"], life["h"]
        xh, xl = s.sb("xh", [P, KD, T], F32R), s.sb("xl", [P, KD, T], F32R)
        x_in = s.sb("x_in", [P, NT, D])
        ring = WeightRing(s)
        gemm = Gemm(s, ring, bank)
        x_landed, done = s.sem("x_landed"), s.sem("h_done")
        stored = life["h1_stored"] = s.sem("h1_stored")
        gate = life["gr"]
        norm_w = s.sb("norm_w", [P, GLA_DV])
        sq = s.sb("sq", [P, NT * GLA_HEADS, GLA_DV])
        ss, root = s.sb("ss", [P, NT * GLA_HEADS]), s.sb("root", [P, NT * GLA_HEADS])
        w_landed, squared, mean, rooted, gated, vec = (
            s.sem("norm_w_landed"), s.sem("squared"), s.sem("mean"), s.sem("rooted"), s.sem("gated"),
            s.sem("vector_steps"))
        ident = const[:, CONSTS["ident"][0]:CONSTS["ident"][1]]
        first, second = range(KD // 2), range(KD // 2, KD)
        turn = TurnColumns(s, mix, xh, xl, ident, bank)

        def part(c0):
            return dict(kind="rows", slab=lambda i, _: weight_slab(io["w_out"], i, c0), width=BANK, ktiles=KD,
                        x=lambda kt, m: (xh[:, kt, m * P:(m + 1) * P], xl[:, kt, m * P:(m + 1) * P]),
                        meta=False, c0=c0)

        blocks = gemm.plan([part(0), part(BANK)])
        block = s.block()

        @block.sync
        def _(sp):
            sp.dma_start(norm_w[:, :], io["gla_norm_w"].to_broadcast([P, GLA_DV])).then_inc(w_landed, 16)
            for n, b in enumerate(blocks):
                gemm.on_sync(sp, b)
                if n == 0:
                    sp.dma_start(x_in[:, :, :], io["x"].rearrange("(t p) d -> p t d", p=P)).then_inc(x_landed, 16)
            sp.wait_ge(done, 1)
            sp.dma_start(io["h1"].rearrange("(t p) d -> p t d", p=P), h[:, :, :]).then_inc(stored, 16)

        @block.gpsimd
        def _(pool):
            ring.open_raw(pool)
            for b in blocks:
                gemm.on_gpsimd(pool, b)

        @block.scalar
        def _(act):
            act.activation(sq[:, :, :].rearrange("p (t h) v -> p t h v", t=NT),
                           mix[:, :, D // 2:D].rearrange("p t (h v) -> p t h v", h=GLA_HEADS), ACT.Square)\
                .then_inc(squared, 1)
            turn.on_scalar(act, first)
            act.wait_ge(mean, 1)
            act.activation(root[:, :], ss[:, :], ACT.Sqrt).then_inc(rooted, 1)
            gemm.on_scalar(act, blocks[0], 0, AHEAD)
            turn.on_scalar(act, second)
            gemm.on_scalar(act, blocks[0], 0, REST)
            gemm.on_scalar(act, blocks[1])

        @block.tensor
        def _(pe):
            ring.open_slots(pe)
            turn.on_tensor(pe, first)
            pe.wait_ge(gated, 1)
            turn.on_tensor(pe, second)
            pe.wait_ge(turn.done, KD)
            for b in blocks:
                gemm.on_tensor(pe, b)

        @block.vector
        def _(dve):
            chain = Chain(dve, vec)
            gemm.open_banks(dve)
            dve.wait_ge(squared, 1)
            chain(dve.tensor_reduce(ss[:, :], sq[:, :, :], AX.X, ALU.add))
            dve.tensor_scalar(ss[:, :], ss[:, :], 1.0 / GLA_DV, EPS, ALU.mult, ALU.add).then_inc(mean, 1)
            dve.wait_ge(w_landed, 16)
            dve.wait_ge(rooted, 1)
            chain(dve.reciprocal(root[:, :], root[:, :]))
            for t in range(NT):
                for hd in range(GLA_HEADS):
                    o = mix[:, t, D // 2 + hd * GLA_DV:D // 2 + (hd + 1) * GLA_DV]
                    n = t * GLA_HEADS + hd
                    last = dve.scalar_tensor_tensor(o, o, root[:, n:n + 1], norm_w[:, :], ALU.mult, ALU.mult)
            chain(last)
            dve.tensor_tensor(mix[:, :, D // 2:D], mix[:, :, D // 2:D], gate[:, :, :], ALU.mult).then_inc(gated, 1)
            turn.on_vector(dve, first)
            turn.on_vector(dve, second)
            dve.wait_ge(x_landed, 16)
            for b in blocks:
                gemm.take(dve, b, lambda j, m, got: dve.tensor_tensor(
                    h[:, m, b["c0"]:b["c0"] + BANK], got, x_in[:, m, b["c0"]:b["c0"] + BANK], ALU.add))
            dve.wait_ge(gemm.bank_free, NBANK + gemm.tile0)
            dve.sem_inc(done, 1)



def phase_peer_pick(nc, bank, const, io, life):
    with ExitStack() as ctx:
        s = Scope(nc, ctx, "pp")
        h = life["h"]
        K, B = PEER_K, HP // 4
        G = NT * 2
        xh, xl = s.sb("xh", [P, KD, T], F32R), s.sb("xl", [P, KD, T], F32R)
        gain = s.sb("gain", [P, KD])
        keys = s.sb("keys", [P, HP, PEER_KEYS])
        qT = s.sb("qT", [P, 4, T])
        sc = s.sb("sc", [P, 2, NT * 4, PEER_KEYS])
        ts, ti = s.sb("ts", [P, NT * 4, K]), s.sb("ti", [P, NT * 4, K], U32)
        tif = s.sb("tif", [P, 2, NT * 4, K])
        cand = s.sb("cand", [P, G, K, K])
        bs, bp = s.sb("bs", [P, 2, G, K]), s.sb("bp", [P, G, K], U32)
        place = s.sb("place", [P, 2, G, K], U32)
        placef = s.sb("placef", [P, 2, G, K])
        hot = s.sb("hot", [P, 2, G, K, K])
        tsum = s.sb("tsum", [P, G])
        pick = s.sb("pick", [P, NT, 3, P])
        ring = WeightRing(s)
        gemm = Gemm(s, ring, bank)
        names = ("stored", "scored", "score_taken", "vector_steps", "sc_used", "shifted", "exped", "hot_done",
                 "hot_used", "picked", "turned", "gpsimd_steps")
        S = {n: s.sem(n) for n in names}
        gain_landed, keys_landed = s.sem("gain_landed"), s.sem("keys_landed")
        ident = const[:, CONSTS["ident"][0]:CONSTS["ident"][1]]
        iota = const[:, CONSTS["iota"][0]:CONSTS["iota"][0] + K]
        norm = NormColumns(s, h, None, gain, xh, xl, ident, bank, gain_landed=gain_landed)

        def part(b):
            return dict(kind="columns", width=BANK, ktiles=KD, meta=False,
                        slab=lambda i, _: weight_slab(io["peer_w_q"], i, b * BANK),
                        x=lambda kt, half: (xh[:, kt, :], xl[:, kt, :]))

        blocks = gemm.plan([part(b) for b in range(B)])

        def picks(b, j):
            return pick[:, :, j, 2 * b * K:2 * (b + 1) * K]

        def key_of(b, j):
            return tif[:, b % 2, :, :].rearrange("p (g two) k -> p g two k", two=2)[:, :, j, :]

        block = s.block()

        @block.sync
        def _(sp):
            sp.dma_start(gain[:, :], io["ln2_w"]).then_inc(gain_landed, 16)
            for n, b in enumerate(blocks):
                gemm.on_sync(sp, b)
                if n == 0:
                    sp.dma_start(keys[:, :, :], io["peer_keys"]).then_inc(keys_landed, 16)
                    sp.wait_ge(norm.done, norm.total())
                    sp.dma_start(io["hn_hi"], xh[:, :, :].bitcast(F32)).then_inc(S["stored"], 16)
                    sp.dma_start(io["hn_lo"], xl[:, :, :].bitcast(F32)).then_inc(S["stored"], 16)
            sp.wait_ge(S["stored"], 32)
            sp.wait_ge(life["h1_stored"], 16)

        @block.gpsimd
        def _(pool):
            ring.open_raw(pool)

            chain = Chain(pool, S["gpsimd_steps"])

            def key_rows(b):
                pool.wait_ge(S["hot_done"], b + 1)
                for j in range(2):
                    last = pool.tensor_tensor(hot[:, j, :, :, :], hot[:, j, :, :, :],
                                              key_of(b, j).unsqueeze(2).to_broadcast([P, G, K, K]), ALU.mult)
                chain(last)
                for w in (8, 4, 2):
                    chain(pool.tensor_tensor(hot[:, :, :, :, 0:w], hot[:, :, :, :, 0:w], hot[:, :, :, :, w:2 * w],
                                             ALU.add))
                for j in range(2):
                    rows = hot[:, j, :, :, :].rearrange("p (t h) r k -> p t h r k", h=2)
                    last = pool.tensor_tensor(picks(b, j).rearrange("p t (h r) -> p t h r", h=2),
                                              rows[:, :, :, :, 0], rows[:, :, :, :, 1], ALU.add)
                last.then_inc(S["hot_used"], 1)

            gemm.on_gpsimd(pool, blocks[0])
            for n in range(1, B):
                gemm.on_gpsimd(pool, blocks[n])
                if n >= 2:
                    key_rows(n - 2)
            key_rows(B - 2)

        @block.scalar
        def _(act):
            gemm.open_banks(act)
            norm.on_scalar(act, lambda e, t: None, lambda: gemm.on_scalar(act, blocks[0], 0, AHEAD))

            def exp(b):
                act.wait_ge(S["shifted"], b + 1)
                act.activation(bs[:, b % 2, :, :], bs[:, b % 2, :, :], ACT.Exp).then_inc(S["exped"], 1)

            for n, b in enumerate(blocks):
                gemm.on_scalar(act, b, 0, REST)
                if n + 1 < B:
                    gemm.on_scalar(act, blocks[n + 1], 0, AHEAD)
                if n:
                    act.wait_ge(S["scored"], NT * n)
                gemm.take(act, b, lambda j, m, got: act.activation(qT[:, m[0], :], got, ACT.Copy))
                if n >= 2:
                    act.wait_ge(S["sc_used"], n - 1)
                for t in range(NT):
                    act.wait_ge(S["scored"], NT * n + t + 1)
                    act.activation(sc[:, n % 2, 4 * t:4 * t + 4, :].rearrange("p a k -> p (a k)"),
                                   bank[:, 4 * (n % 2) + t, :], ACT.Copy).then_inc(S["score_taken"], 1)
                if n:
                    exp(n - 1)
            exp(B - 1)

        @block.tensor
        def _(pe):
            ring.open_slots(pe)
            norm.on_tensor(pe)
            pe.wait_ge(norm.done, norm.total())
            for n, b in enumerate(blocks):
                if n >= 2:
                    pe.wait_ge(S["score_taken"], NT * (n - 1))
                gemm.on_tensor(pe, b)
                if n == 0:
                    pe.wait_ge(keys_landed, 16)
                pe.wait_ge(gemm.bank_free, NBANK + 4 * (n + 1))
                for t in range(NT):
                    for i in range(4):
                        last = pe.matmul(bank[:, 4 * (n % 2) + t, i * P:(i + 1) * P], qT[:, i, t * P:(t + 1) * P],
                                         keys[:, 4 * n + i, :], start=True, stop=True)
                    last.then_inc(S["scored"], 1)
            pe.wait_ge(S["score_taken"], NT * B)
            pe.wait_ge(S["picked"], B)
            pe.wait_ge(S["hot_used"], B - 1)
            for t in range(NT):
                for j in range(3):
                    last = pe.transpose(bank[:, j, t * P:(t + 1) * P], pick[:, t, j, :], ident)
            last.then_inc(S["turned"], 1)

        @block.vector
        def _(dve):
            chain = Chain(dve, S["vector_steps"])
            norm.on_vector(dve, chain)

            def best_16(groups, values, scores, index):
                for half in (slice(0, 8), slice(8, K)):
                    for g in range(groups):
                        last = dve.max(scores(g)[:, half], values(g))
                    chain(last)
                    for g in range(groups):
                        last = dve.max_index(index(g)[:, half], scores(g)[:, half], values(g))
                    chain(last)
                    if half.start == 0:
                        for g in range(groups):
                            last = dve.match_replace(values(g), scores(g)[:, half], values(g), NEG)
                        chain(last)

            def finish(b):
                gates = bs[:, b % 2, :, :]
                dve.wait_ge(S["exped"], b + 1)
                chain(dve.tensor_reduce(tsum[:, :], gates, AX.X, ALU.add))
                chain(dve.reciprocal(tsum[:, :], tsum[:, :]))
                dve.tensor_tensor(picks(b, 2).rearrange("p t (h r) -> p t h r", h=2),
                                  gates.rearrange("p (t h) r -> p t h r", h=2),
                                  tsum[:, :].rearrange("p (t h) -> p t h", h=2).unsqueeze(3)
                                  .to_broadcast([P, NT, 2, K]), ALU.mult).then_inc(S["picked"], 1)
                dve.wait_ge(S["picked"], b + 1)

            for b in range(B):
                values, best = sc[:, b % 2, :, :], bs[:, b % 2, :, :]
                dve.wait_ge(S["score_taken"], NT * (b + 1))
                best_16(NT * 4, lambda g: values[:, g, :], lambda g: ts[:, g, :], lambda g: ti[:, g, :])
                dve.sem_inc(S["sc_used"], 1)
                chain(dve.tensor_copy(tif[:, b % 2, :, :], ti[:, :, :]))
                if b:
                    finish(b - 1)
                pair = ts[:, :, :].rearrange("p (g two) k -> p g two k", two=2)
                chain(dve.tensor_tensor(cand[:, :, :, :], pair[:, :, 0, :].unsqueeze(3).to_broadcast([P, G, K, K]),
                                        pair[:, :, 1, :].unsqueeze(2).to_broadcast([P, G, K, K]), ALU.add))
                best_16(G, lambda g: cand[:, g, :, :].rearrange("p a b -> p (a b)"), lambda g: best[:, g, :],
                        lambda g: bp[:, g, :])
                chain(dve.tensor_copy(tsum[:, :], best[:, :, 0]))
                dve.tensor_tensor(best, best, tsum[:, :].unsqueeze(2).to_broadcast([P, G, K]), ALU.subtract)\
                    .then_inc(S["shifted"], 1)
                dve.tensor_single_scalar(place[:, 0, :, :], bp[:, :, :], 4, ALU.logical_shift_right)
                chain(dve.tensor_single_scalar(place[:, 1, :, :], bp[:, :, :], K - 1, ALU.bitwise_and))
                chain(dve.tensor_copy(placef[:, :, :, :], place[:, :, :, :]))
                if b:
                    dve.wait_ge(S["hot_used"], b)
                for j in range(2):
                    last = dve.tensor_tensor(
                        hot[:, j, :, :, :].rearrange("p h r k -> p (h r) k"),
                        iota.unsqueeze(1).to_broadcast([P, G * K, K]),
                        placef[:, j, :, :].rearrange("p h r -> p (h r)").unsqueeze(2).to_broadcast([P, G * K, K]),
                        ALU.is_equal)
                last.then_inc(S["hot_done"], 1)
            dve.wait_ge(S["hot_done"], B)
            for j in range(2):
                last = dve.tensor_tensor(hot[:, j, :, :, :], hot[:, j, :, :, :],
                                         key_of(B - 1, j).unsqueeze(2).to_broadcast([P, G, K, K]), ALU.mult)
            chain(last)
            for j in range(2):
                dve.tensor_reduce(picks(B - 1, j).rearrange("p t (h r) -> p t h r", h=2),
                                  hot[:, j, :, :, :].rearrange("p (t h) r k -> p t h r k", h=2), AX.X, ALU.add)
            finish(B - 1)
            dve.wait_ge(S["turned"], 1)
            dve.tensor_copy(life["pick_keys"][:, :, :], bank[:, 0:2, :])
            left, parts = cand[:, :, :, :].rearrange("p h r k -> p (h r k)")[:, 0:T], life["pick_gates"]
            chain(dve.tensor_copy(left, bank[:, 2, :]))
            for n in range(3):
                chain(dve.tensor_copy(parts[:, :, n], left))
                if n < 2:
                    chain(dve.tensor_tensor(left, left, parts[:, :, n], ALU.subtract))



SWEEPS = 2
ST = T // SWEEPS
ROUND = 32
ROUNDS = PEER_KEYS // ROUND
GROUP = ST // ROUND
HALF_GROUP = GROUP // 2
FIRST = ROUND // 4
RAW = 4
PARTS = 3


def phase_peer_experts(nc, bank, io, life):
    with ExitStack() as ctx:
        s = Scope(nc, ctx, "pe")
        keys, parts = life["pick_keys"], life["pick_gates"]
        iota = s.sb("iota", [P, P])
        counting = s.sb("counting", [P, P], BF16)
        zero = s.sb("zero", [P, P], F32R)
        gates = [s.sb(f"gates{k}", [P, ROUND, ST]) for k in range(2)]
        xh, xl = s.sb("xh", [P, KD, T], F32R), s.sb("xl", [P, KD, T], F32R)
        u_raw, v_raw = s.sb("u_raw", [P, RAW, KD, P]), s.sb("v_raw", [P, RAW, D])
        uh, ul = s.sb("uh", [P, 2, KD, P], F32R), s.sb("ul", [P, 2, KD, P], F32R)
        vh, vl = s.sb("vh", [P, 2, D], F32R), s.sb("vl", [P, 2, D], F32R)
        hid = s.sb("hid", [P, 2, ST])
        hh, hl = s.sb("hh", [P, 2, ST], F32R), s.sb("hl", [P, 2, ST], F32R)
        eq1 = s.sb("eq1", [P, 2, GROUP, ROUND], BF16)
        hot1 = s.sb("hot1", [P, 2, GROUP, PARTS, ROUND], BF16)
        hot2 = s.sb("hot2", [P, 2, GROUP, P], BF16)
        out = s.sb("out", [P, 4, BANK])
        names = ("iota_landed", "x_landed", "u_hi", "u_lo", "v_hi", "v_lo", "a_done", "a_taken", "hid_ready",
                 "h_hi", "h_lo", "v_done", "eq1_ready", "hot1_ready", "hot2_ready", "hot_read", "first_taken",
                 "spread", "gates_taken", "zeroed", "out_done", "out_taken", "out_stored", "vector_steps")
        S = {n: s.sem(n) for n in names}
        u_landed = [s.sem(f"u_landed{k}") for k in range(RAW)]
        v_landed = [s.sem(f"v_landed{k}") for k in range(RAW)]
        A_BANK, G_BANK = 4, 6
        N = SWEEPS * PEER_KEYS
        block = s.block()


        def rounds(eng, body, at_round=None, at_sweep=None):
            for r in range(SWEEPS * ROUNDS):
                if at_round:
                    at_round(r)
                peel = r % ROUNDS == ROUNDS - 1
                turns = ROUND // RAW - peel
                with eng.Fori(0, turns) as i:
                    for c in range(RAW):
                        body(r, r * ROUND + c, i, c)
                if peel:
                    for c in range(RAW):
                        body(r, r * ROUND + turns * RAW + c, None, c)
                    if at_sweep:
                        at_sweep(r // ROUNDS)

        def at(n, i):
            return n if i is None else i * RAW + n

        def spread_here(r):
            return r < SWEEPS * ROUNDS - 1

        @block.sync
        def _(sp):
            sp.dma_start(iota[:, :], io["const"][:, CONSTS["iota"][0]:CONSTS["iota"][1]])\
                .then_inc(S["iota_landed"], 16)
            sp.dma_start(xh[:, :, :].bitcast(F32), io["hn_hi"]).then_inc(S["x_landed"], 16)
            sp.dma_start(xl[:, :, :].bitcast(F32), io["hn_lo"]).then_inc(S["x_landed"], 16)
            for sweep in range(SWEEPS):
                with sp.Fori(0, PEER_KEYS // RAW) as i:
                    for c in range(RAW):
                        q = at(sweep * PEER_KEYS + c, i)
                        sp.wait_ge(S["u_lo"], q + 1)
                        sp.dma_start(u_raw[:, c, :, :].rearrange("p k j -> p (k j)"),
                                     io["peer_u"][bass.ds(RAW * i + c, 1), :, :].rearrange("a p n -> p (a n)"))\
                            .then_inc(u_landed[c], 16)
                        sp.wait_ge(S["v_lo"], q + 1)
                        sp.dma_start(v_raw[:, c, :],
                                     io["peer_v"][bass.ds(RAW * i + c, 1), :, :].rearrange("a p n -> p (a n)"))\
                            .then_inc(v_landed[c], 16)

        @block.scalar
        def _(act):
            def split_u(n, i):
                turn = n // RAW if i is None else i + n // RAW
                act.wait_ge(u_landed[n % RAW], 16 * turn + 16)
                act.wait_ge(S["a_done"], at(n, i) + 1)
                act.activation(uh[:, n % 2, :, :], u_raw[:, n % RAW, :, :], ACT.Copy).then_inc(S["u_hi"], 1)

            def split_v(n, i):
                turn = n // RAW if i is None else i + n // RAW
                act.wait_ge(v_landed[n % RAW], 16 * turn + 16)
                act.wait_ge(S["v_done"], at(n, i) + 1)
                act.activation(vh[:, n % 2, :], v_raw[:, n % RAW, :], ACT.Copy).then_inc(S["v_hi"], 1)

            def take_gates(g, k):
                act.wait_ge(S["hot_read"], g + 3)
                act.activation(gates[0][:, :, bass.ds(g * GROUP, GROUP)].rearrange("p i n -> p n i"),
                               bank[:, G_BANK + k, 0:GROUP * ROUND].rearrange("p (n i) -> p n i", n=GROUP),
                               ACT.Copy).then_inc(S["first_taken"], 1)

            act.sem_inc(S["a_taken"], 2)
            act.sem_inc(S["first_taken"], 2)
            with act.Fori(0, FIRST) as i:
                for k in range(2):
                    take_gates(2 * i + k, k)
            split_u(0, None)
            split_u(1, None)
            split_v(0, None)
            with act.Fori(FIRST, ROUND // 2) as i:
                for k in range(2):
                    take_gates(2 * i + k, k)

            def body(r, n, i, c):
                q, k = at(n, i), c % 2
                act.wait_ge(S["a_done"], q + 3)
                act.wait_ge(S["h_lo"], q + 1)
                act.activation(hid[:, k, :], bank[:, A_BANK + k, 0:ST], ACT.Gelu).then_inc(S["a_taken"], 1)
                if i is not None or n + 2 < N:
                    split_u(n + 2, i)
                act.wait_ge(S["hid_ready"], q + 1)
                act.wait_ge(S["v_done"], q + 1)
                act.activation(hh[:, k, :], hid[:, k, :], ACT.Copy).then_inc(S["h_hi"], 1)
                if i is not None or n + 1 < N:
                    split_v(n + 1, i)

            rounds(act, body)

        @block.gpsimd
        def _(pool):
            pool.sem_inc(S["v_lo"], RAW)
            pool.sem_inc(S["hot1_ready"], 2)

            def split_v(n, i):
                pool.wait_ge(S["v_hi"], at(n, i) + 1)
                pool.tensor_tensor(vl[:, n % 2, :], v_raw[:, n % RAW, :], vh[:, n % 2, :].bitcast(F32),
                                   ALU.subtract).then_inc(S["v_lo"], 1)

            def times_gates(g, n0, k):
                pool.wait_ge(S["eq1_ready"], g + 1)
                pool.tensor_tensor(hot1[:, k, :, :, :],
                                   eq1[:, k, :, :].unsqueeze(2).to_broadcast([P, GROUP, PARTS, ROUND]),
                                   parts[:, bass.ds(n0, GROUP), :].unsqueeze(3)
                                   .to_broadcast([P, GROUP, PARTS, ROUND]), ALU.mult).then_inc(S["hot1_ready"], 1)

            with pool.Fori(0, FIRST) as i:
                for k in range(2):
                    times_gates(2 * i + k, (2 * i + k) * GROUP, k)
            split_v(0, None)
            with pool.Fori(FIRST, ROUND // 2) as i:
                for k in range(2):
                    times_gates(2 * i + k, (2 * i + k) * GROUP, k)

            def body(r, n, i, c):
                q = at(n, i)
                if spread_here(r):
                    times_gates(q + ROUND, (q - r * ROUND) * GROUP + (r + 1) // ROUNDS * ST, c % 2)
                if i is not None or n + 1 < N:
                    split_v(n + 1, i)

            def at_sweep(sweep):
                for m in range(2):
                    pool.wait_ge(S["out_taken"], 2 * sweep + m + 1)
                    pool.dma_start(io["experts"][(2 * sweep + m) * P:(2 * sweep + m + 1) * P, :]
                                   .rearrange("p (c n) -> p c n", c=2), out[:, 2 * m:2 * m + 2, :])\
                        .then_inc(S["out_stored"], 16)

            rounds(pool, body, None, at_sweep)
            pool.wait_ge(S["out_stored"], 16 * 2 * SWEEPS)

        @block.vector
        def _(dve):
            dve.sem_inc(S["u_lo"], RAW)
            dve.sem_inc(S["h_lo"], 2)
            dve.memset(zero[:, :].bitcast(F32), 0.0).then_inc(S["zeroed"], 1)
            dve.wait_ge(S["iota_landed"], 16)
            dve.tensor_copy(counting[:, :], iota[:, :]).then_inc(S["vector_steps"], 1)
            dve.wait_ge(S["vector_steps"], 1)

            def one_hots(r, g, n0, k):
                n = bass.ds(n0, GROUP)
                first = (r % ROUNDS) * ROUND
                dve.wait_ge(S["hot_read"], g + 1)
                dve.wait_ge(S["hot1_ready"], g + 1)
                dve.tensor_tensor(eq1[:, k, :, :], counting[:, first:first + ROUND].unsqueeze(1)
                                  .to_broadcast([P, GROUP, ROUND]),
                                  keys[:, 0, n].unsqueeze(2).to_broadcast([P, GROUP, ROUND]), ALU.is_equal)\
                    .then_inc(S["eq1_ready"], 1)
                dve.tensor_tensor(hot2[:, k, :, :], counting[:, :].unsqueeze(1).to_broadcast([P, GROUP, P]),
                                  keys[:, 1, n].unsqueeze(2).to_broadcast([P, GROUP, P]), ALU.is_equal)\
                    .then_inc(S["hot2_ready"], 1)

            def take_gates(r, q):
                for half in range(2):
                    dve.wait_ge(S["spread"], 2 * q + half + 1)
                    n = bass.ds((q - (r - 1) * ROUND) * GROUP + half * HALF_GROUP, HALF_GROUP)
                    dve.tensor_reduce(gates[r % 2][:, :, n].rearrange("p i n -> p n i"),
                                      bank[:, G_BANK + half, 0:HALF_GROUP * PARTS * ROUND]
                                      .rearrange("p (n w i) -> p n i w", n=HALF_GROUP, w=PARTS), AX.X, ALU.add)\
                        .then_inc(S["gates_taken"], 1)

            def split_u(n, i):
                dve.wait_ge(S["u_hi"], at(n, i) + 1)
                dve.tensor_tensor(ul[:, n % 2, :, :], u_raw[:, n % RAW, :, :], uh[:, n % 2, :, :].bitcast(F32),
                                  ALU.subtract).then_inc(S["u_lo"], 1)

            dve.sem_inc(S["gates_taken"], 2)
            with dve.Fori(0, FIRST) as i:
                for k in range(2):
                    one_hots(0, 2 * i + k, (2 * i + k) * GROUP, k)
            split_u(0, None)
            split_u(1, None)
            with dve.Fori(FIRST, ROUND // 2) as i:
                for k in range(2):
                    one_hots(0, 2 * i + k, (2 * i + k) * GROUP, k)

            def at_round(r):
                if r:
                    dve.wait_ge(S["gates_taken"], 2 * r * ROUND + 2)
                    dve.wait_ge(S["hid_ready"], r * ROUND)
                else:
                    dve.wait_ge(S["first_taken"], ROUND + 2)

            def body(r, n, i, c):
                q, k = at(n, i), c % 2
                dve.wait_ge(S["a_taken"], q + 3)
                g = gates[r % 2][:, bass.ds(q - r * ROUND, 1), :].rearrange("p a n -> p (a n)")
                dve.tensor_tensor(hid[:, k, :], hid[:, k, :], g, ALU.mult).then_inc(S["hid_ready"], 1)
                if spread_here(r):
                    one_hots(r + 1, q + ROUND, (q - r * ROUND) * GROUP + (r + 1) // ROUNDS * ST, k)
                dve.wait_ge(S["h_hi"], q + 1)
                dve.tensor_tensor(hl[:, k, :], hid[:, k, :], hh[:, k, :].bitcast(F32), ALU.subtract)\
                    .then_inc(S["h_lo"], 1)
                if i is not None or n + 2 < N:
                    split_u(n + 2, i)
                if spread_here(r):
                    take_gates(r + 1, q)

            def at_sweep(sweep):
                dve.wait_ge(S["out_done"], sweep + 1)
                for m in range(2):
                    if sweep:
                        dve.wait_ge(S["out_stored"], 16 * 2 * sweep)
                    dve.tensor_copy(out[:, 2 * m:2 * m + 2, :], bank[:, 2 * m:2 * m + 2, :])\
                        .then_inc(S["out_taken"], 1)

            rounds(dve, body, at_round, at_sweep)

        @block.tensor
        def _(pe):
            pe.sem_inc(S["a_done"], 2)
            pe.sem_inc(S["v_done"], 2)
            pe.sem_inc(S["hot_read"], 2)

            def add_gates(g, k):
                pe.wait_ge(S["hot1_ready"], g + 3)
                pe.wait_ge(S["hot2_ready"], g + 1)
                pe.wait_ge(S["first_taken"], g + 1)
                for j in range(GROUP):
                    for p in range(PARTS):
                        last = pe.matmul(bank[:, G_BANK + k, j * ROUND:(j + 1) * ROUND], hot2[:, k, j, :],
                                         hot1[:, k, j, p, :], start=p == 0, stop=p == PARTS - 1)
                last.then_inc(S["hot_read"], 1)

            def spread_gates(q, k):
                pe.wait_ge(S["hot1_ready"], q + ROUND + 3)
                pe.wait_ge(S["hot2_ready"], q + ROUND + 1)
                for half in range(2):
                    pe.wait_ge(S["gates_taken"], 2 * q + half + 1)
                    for j in range(HALF_GROUP):
                        n = half * HALF_GROUP + j
                        last = pe.matmul(bank[:, G_BANK + half, j * PARTS * ROUND:(j + 1) * PARTS * ROUND],
                                         hot2[:, k, n, :], hot1[:, k, n, :, :].rearrange("p w i -> p (w i)"),
                                         start=True, stop=True)
                    last.then_inc(S["spread"], 1)

            def scores(q, k, sweep):
                pe.wait_ge(S["u_lo"], q + RAW + 1)
                pe.wait_ge(S["a_taken"], q + 1)
                t = slice(sweep * ST, (sweep + 1) * ST)
                for kt in range(KD):
                    last = split_products(pe, bank[:, A_BANK + k, 0:ST], (uh[:, k, kt, :], ul[:, k, kt, :]),
                                          (xh[:, kt, t], xl[:, kt, t]), kt == 0, kt == KD - 1)
                last.then_inc(S["a_done"], 1)

            def values(q, k, frees):
                pe.wait_ge(S["h_lo"], q + 3)
                pe.wait_ge(S["v_lo"], q + RAW + 1)
                for m in range(2):
                    for c in range(2):
                        t, d = slice(m * P, (m + 1) * P), slice(c * BANK, (c + 1) * BANK)
                        last = split_products(pe, bank[:, 2 * m + c, :], (hh[:, k, t], hl[:, k, t]),
                                              (vh[:, k, d], vl[:, k, d]), False, False, True,
                                              frees if m == c == 0 else None)
                last.then_inc(S["v_done"], 1)

            def zero_products(start):
                for b in range(4):
                    for c in range(BANK // P):
                        last = pe.matmul(bank[:, b, c * P:(c + 1) * P], zero[:, :], zero[:, :],
                                         start=start and c == 0, stop=not start, skip_group_check=True)
                return last

            pe.wait_ge(S["zeroed"], 1)
            zero_products(True)
            with pe.Fori(0, FIRST) as i:
                for k in range(2):
                    add_gates(2 * i + k, k)
            pe.wait_ge(S["x_landed"], 32)
            scores(0, 0, 0)
            with pe.Fori(FIRST, ROUND // 2) as i:
                for k in range(2):
                    add_gates(2 * i + k, k)
            pe.wait_ge(S["first_taken"], ROUND + 2)

            def body(r, n, i, c):
                q, k = at(n, i), c % 2
                if i is not None or n + 1 < N:
                    last_of_sweep = i is None and (n + 1) % PEER_KEYS == 0
                    scores(q + 1, 1 - k, r // ROUNDS + last_of_sweep)
                if spread_here(r):
                    spread_gates(q, k)
                values(q, k, S["hot_read"] if spread_here(r) else None)

            def at_sweep(sweep):
                zero_products(False).then_inc(S["out_done"], 1)
                if sweep + 1 < SWEEPS:
                    pe.wait_ge(S["out_taken"], 2 * (sweep + 1))
                    zero_products(True)

            rounds(pe, body, None, at_sweep)



POOL_GROUPS, POOL_D = 4, 512
AH, LAT = 8, 128
IDX_H, IDX_D = 8, 32
INDEX_SCALE = (IDX_H ** -0.5) * (IDX_D ** -0.5)
ATTN_SCALE = LAT ** -0.5
TOP = min(256, T // 4)
FF = 2816
KF = FF // P


def seen(t):
    return META + (t + 1) * P


def phase_project_2(nc, bank, const, io, life):
    with ExitStack() as ctx:
        s = Scope(nc, ctx, "p2")
        xh, xl = life["xh"], life["xl"]
        bias = life["bias"]
        h = life["h_rows"]
        hm = s.sb("h_meta", [META, D])
        gain, gain_row = s.sb("gain", [P, KD]), s.sb("gain_row", [P, D])
        add = life["xs"]
        kv_g = s.sb("kv_g", [P, LAT])
        qi = s.sb("qi", [P, 2, TM])
        ki = s.sb("ki", [P, TM])
        wi = s.sb("wi", [P, NT, IDX_H])
        rel = s.sb("rel", [P, 2, TM])
        score = s.sb("score", [P, NT, TM])
        best = s.sb("best", [P, 8])
        c, cm, cT = life["c"], life["c_m"], life["cT"]
        ring = WeightRing(s)
        early = Gemm(s, ring, bank, "early_")
        late = Gemm(s, ring, bank, "late_")
        g_landed, stored = s.sem("gains_landed"), s.sem("stored")
        h_landed = [s.sem(f"h_landed{t}") for t in range(NT)]
        added, y_done, vec = s.sem("added"), s.sem("y_done"), s.sem("vector_steps")
        scored, relued, summed = s.sem("scored"), s.sem("relued"), s.sem("summed")
        c_done, c_turned, c_taken = s.sem("c_done"), s.sem("c_turned"), s.sem("c_taken")
        ident = const[:, CONSTS["ident"][0]:CONSTS["ident"][1]]
        causal = const[:, CONSTS["causal"][0]:CONSTS["causal"][1]]
        causal_fill = const[:, CONSTS["causal_fill"][0]:CONSTS["causal_fill"][1]]
        out_stats = RowStats(s, h, None, "o_")
        norm = NormColumns(s, h, hm, gain, xh, xl, ident, bank, life["xs"], out_stats.junk)
        c_stats = RowStats(s, c, cm, "c_")

        def rows(kt, m):
            cc = slice(META + m * P, META + (m + 1) * P) if m >= 0 else slice(0, P)
            return xh[:, kt, cc], xl[:, kt, cc]

        def all_columns(kt, half):
            cc = slice(half * HM, (half + 1) * HM)
            return xh[:, kt, cc], xl[:, kt, cc]

        def columns(kt, half):
            return xh[:, kt, META:TM], xl[:, kt, META:TM]

        def part(kind, w, c0, width, meta, dst=None, first=0):
            return dict(kind=kind, slab=lambda i, turn: weight_slab(w, i, c0, width), width=width, ktiles=KD,
                        x=rows if kind == "rows" else all_columns if meta else columns, meta=meta, dst=dst,
                        first=first)

        b_index, b_lat = early.plan([part("columns", io["w_index"], 0, 3 * P, True),
                                     part("rows", io["w_latent"], 0, LAT + IDX_H, True)])
        late.slab0 = early.slab0
        w = io["w_in_2"]
        c_conv = 1960
        blocks = late.plan([
            part("columns", w, 0, BANK, True, life["u"]), part("columns", w, 512, BANK, False, life["q2"], 0),
            part("columns", w, 1024, BANK, False, life["q2"], 4), part("columns", w, c_conv, BANK, False, life["cb"]),
            part("columns", w, c_conv + 512, BANK, True, life["cc"]),
            part("columns", w, c_conv + 1024, BANK, True, life["cu"])])
        units = [(t, hd) for t in range(NT) for hd in range(IDX_H)]
        block = s.block()

        @block.sync
        def _(sp):
            for t in range(NT):
                rows_t = slice(t * P, (t + 1) * P)
                sp.dma_start(h[:, t, :], io["h1"][rows_t, :]).then_inc(h_landed[t], 16)
                sp.dma_start(add[:, t, :], io["experts"][rows_t, :]).then_inc(h_landed[t], 16)
                if t == 0:
                    sp.dma_start(gain_row[:, :], io["final_norm_w"].to_broadcast([P, D])).then_inc(g_landed, 16)
            sp.dma_start(const[:, :], io["const"][:, 0:CONST_2_W]).then_inc(g_landed, 16)
            sp.dma_start(gain[:, :], io["norm1_g"]).then_inc(g_landed, 16)
            sp.dma_start(kv_g[:, :], io["kv_norm_g"].to_broadcast([P, LAT])).then_inc(g_landed, 16)
            sp.dma_start(hm[:, :], io["meta_2"]).then_inc(g_landed, 16)
            for b in (b_index, b_lat):
                early.on_sync(sp, b)
            sp.wait_ge(y_done, NT)
            sp.dma_start(io["x2"].rearrange("(t p) d -> p t d", p=P), h[:, :, :]).then_inc(stored, 16)
            for b in blocks:
                late.on_sync(sp, b)
            sp.wait_ge(stored, 16)

        @block.gpsimd
        def _(pool):
            ring.open_raw(pool)
            for b in (b_index, b_lat):
                early.on_gpsimd(pool, b)
            for b in blocks:
                late.on_gpsimd(pool, b)

        @block.scalar
        def _(act):
            late.open_banks(act)
            out_stats.on_scalar(act, lambda e, t: e.wait_ge(added, t + 1))
            act.wait_ge(g_landed, 16 * 5)
            norm.on_scalar(act, lambda e, t: e.wait_ge(y_done, min(t + 1, NT)),
                           lambda: early.on_scalar(act, b_index, 0, AHEAD))
            early.on_scalar(act, b_index, 0, REST)
            early.on_scalar(act, b_lat)
            c_stats.on_scalar(act, lambda e, t: e.wait_ge(early.bank_free, NBANK + early.tile0))
            late.on_scalar(act, blocks[0], 0, AHEAD)
            for n, (t, hd) in enumerate(units):
                act.wait_ge(scored, n + 1)
                if n >= 2:
                    act.wait_ge(summed, n - 1)
                pair = bank[:, 2 * (n % 4):2 * (n % 4) + 2, :].rearrange("p b n -> p (b n)")
                act.activation(rel[:, n % 2, 0:seen(t)], pair[:, 0:seen(t)], ACT.Relu).then_inc(relued, 1)
            act.wait_ge(c_turned, 1)
            act.activation(cT[:, META:TM], bank[:, 0, :], ACT.Copy)
            act.activation(cT[:, 0:META], bank[:, 1, 0:META], ACT.Copy).then_inc(c_taken, 1)

            def use(b):
                def one(j, m, got):
                    f, half = m
                    n = HM if b["meta"] else T
                    return act.activation(b["dst"][:, b["first"] + f, half * n:(half + 1) * n], got[:, 0:n],
                                          ACT.Copy)
                return one

            late.on_scalar(act, blocks[0], 0, REST)
            for n, b in enumerate(blocks):
                if n + 1 < len(blocks):
                    late.on_scalar(act, blocks[n + 1], 0, AHEAD)
                if b["dst"] is life["cb"]:
                    act.wait_ge(stored, 16)
                late.take(act, b, use(b))
                if n + 1 < len(blocks):
                    late.on_scalar(act, blocks[n + 1], 0, REST)

        @block.tensor
        def _(pe):
            ring.open_slots(pe)
            pe.wait_ge(g_landed, 16 * 5)
            norm.on_tensor(pe)
            pe.wait_ge(norm.done, norm.total())
            for b in (b_index, b_lat):
                early.on_tensor(pe, b)
            pe.wait_ge(early.bank_free, NBANK + early.tile0)
            for n, (t, hd) in enumerate(units):
                if n >= 4:
                    pe.wait_ge(relued, n - 3)
                r = slice((hd % 4) * IDX_D, (hd % 4 + 1) * IDX_D)
                lhs = qi[r, hd // 4, META + t * P:META + (t + 1) * P]
                b0, w0 = 2 * (n % 4), min(seen(t), BANK)
                last = pe.matmul(bank[:, b0, 0:w0], lhs, ki[r, 0:w0], start=True, stop=True)
                if seen(t) > BANK:
                    last = pe.matmul(bank[:, b0 + 1, 0:seen(t) - BANK], lhs, ki[r, BANK:seen(t)],
                                     start=True, stop=True)
                last.then_inc(scored, 1)
            pe.wait_ge(relued, len(units))
            pe.wait_ge(c_done, NT + 1)
            for t in range(NT):
                pe.transpose(bank[:, 0, t * P:(t + 1) * P], c[:, t, :], ident)
            pe.transpose(bank[:, 1, 0:META], cm[:, :], ident[0:META, 0:META]).then_inc(c_turned, 1)
            pe.wait_ge(c_taken, 1)
            for b in blocks:
                late.on_tensor(pe, b)

        @block.vector
        def _(dve):
            chain = Chain(dve, vec)
            early.open_banks(dve)
            for t in range(NT):
                dve.wait_ge(h_landed[t], 32)
                dve.tensor_tensor(h[:, t, :], h[:, t, :], add[:, t, :], ALU.add).then_inc(added, 1)
            dve.wait_ge(g_landed, 16 * 5)
            out_stats.on_vector(dve, chain, lambda t: dve.scalar_tensor_tensor(
                h[:, t, :], h[:, t, :], out_stats.rstd[:, t:t + 1], gain_row[:, :], ALU.mult, ALU.mult)
                .then_inc(y_done, 1))
            dve.wait_ge(y_done, NT)
            norm.on_vector(dve, chain)

            def use_index(j, m, got):
                f, half = m
                c = slice(half * HM, (half + 1) * HM)
                return dve.tensor_copy(qi[:, f, c] if f < 2 else ki[:, c], got[:, 0:HM])

            def use_latent(j, m, got):
                if m < 0:
                    return dve.tensor_copy(cm[:, :], got[0:META, 0:LAT])
                dve.tensor_scalar(wi[:, m, :], got[:, LAT:LAT + IDX_H], INDEX_SCALE, None, ALU.mult)
                return dve.tensor_copy(c[:, m, :], got[:, 0:LAT])

            early.take(dve, b_index, use_index)
            early.take(dve, b_lat, use_latent)
            dve.wait_ge(early.bank_free, NBANK + early.tile0)

            def normed(t):
                rows_t, n = c_stats.tile(t)
                dve.scalar_tensor_tensor(rows_t, rows_t, c_stats.rstd[0:n, t:t + 1], kv_g[0:n, :], ALU.mult,
                                         ALU.mult).then_inc(c_done, 1)

            c_stats.on_vector(dve, chain, normed)
            for n, (t, hd) in enumerate(units):
                dve.wait_ge(relued, n + 1)
                got, acc = rel[:, n % 2, 0:seen(t)], score[:, t, 0:seen(t)]
                if hd == 0:
                    last = dve.tensor_scalar(acc, got, wi[:, t, 0:1], None, ALU.mult)
                else:
                    dve.wait_ge(summed, n)
                    last = dve.scalar_tensor_tensor(acc, got, wi[:, t, hd:hd + 1], acc, ALU.mult, ALU.add)
                last.then_inc(summed, 1)
            dve.wait_ge(summed, len(units))
            for t in range(NT):
                own = score[:, t, META + t * P:seen(t)]
                chain(dve.tensor_tensor(own, own, causal, ALU.mult))
                last = dve.tensor_tensor(own, own, causal_fill, ALU.add)
            chain(last)
            for t in range(NT):
                work = score[:, t, 0:seen(t)]
                for _ in range(TOP // 8):
                    chain(dve.max(best[:, :], work))
                    chain(dve.match_replace(work, best[:, :], work, NEG))
                b = bias[:, t, 0:seen(t)]
                chain(dve.tensor_scalar(b, work, 2 * NEG / 3, 1.0, ALU.is_lt, ALU.subtract))
                chain(dve.tensor_scalar(b, b, -FILL, None, ALU.mult))
                own = bias[:, t, META + t * P:seen(t)]
                last = dve.tensor_tensor(own, own, causal_fill, ALU.add)
            chain(last)


def phase_sparse_attention(nc, bank, const, io, life):
    with ExitStack() as ctx:
        s = Scope(nc, ctx, "sa")
        q, c, cm, cT, bias = (life[n] for n in ("q2", "c", "c_m", "cT", "bias"))
        oh, ol = life["attn_hi"], life["attn_lo"]
        masked = s.sb("masked", [P, 2, TM])
        p = s.sb("p", [P, 3, TM])
        pT, pTm = s.sb("pT", [P, 2, T]), s.sb("pTm", [META, 2, P])
        mx, total = s.sb("mx", [P, 2]), s.sb("total", [P, 3])
        u, cb, cc, cu = (life[n] for n in ("u", "cb", "cc", "cu"))
        ph, pl, vh, vl = (life[n] for n in ("pool_hi", "pool_lo", "conv_hi", "conv_lo"))
        sums = s.sb("sums", [P, 2, TM])
        pooled = s.sb("pooled", [P, POOL_GROUPS, T])
        conv = cu[:, :, 0:T]
        pool_w = s.sb("pool_w", [P, POOL_GROUPS, P])
        scale, conv_w = s.sb("scale", [P, POOL_GROUPS]), s.sb("conv_w", [P, 3, POOL_GROUPS])
        part = s.sb("part", [P, POOL_GROUPS])
        names = ("scored", "masked_done", "maxed", "exped", "scaled", "turned", "taken", "o_done", "o_hi", "o_lo",
                 "vector_steps", "landed", "pooled", "conv_done", "mixed", "mixed_hi", "conv_hi", "gpsimd_steps")
        S = {n: s.sem(n) for n in names}
        ident = const[:, CONSTS["ident"][0]:CONSTS["ident"][1]]
        units = [(t, hd) for t in range(NT) for hd in range(AH)]
        N = len(units)
        block = s.block()

        @block.sync
        def _(sp):
            sp.dma_start(pool_w[:, :, :], io["pool_w"]).then_inc(S["landed"], 16)
            sp.dma_start(scale[:, :], io["pool_scale"]).then_inc(S["landed"], 16)
            sp.dma_start(conv_w[:, :, :], io["conv_w"]).then_inc(S["landed"], 16)

        @block.gpsimd
        def _(pool):
            chain = Chain(pool, S["gpsimd_steps"])
            for g in range(POOL_GROUPS):
                last = pool.memset(part[:, g:g + 1], 1.0 / (2 << g))
            chain(last)
            for g in range(POOL_GROUPS):
                src, lo = u[:, g, :], 0
                for j in range(g + 1):
                    dst, step = sums[:, j % 2, :], 1 << j
                    lo += step
                    chain(pool.tensor_tensor(dst[:, lo:TM], src[:, lo:TM], src[:, lo - step:TM - step], ALU.add))
                    src = dst
                chain(pool.tensor_tensor(pooled[:, g, :], src[:, META:TM], part[:, g:g + 1].to_broadcast([P, T]),
                                         ALU.mult))
            pool.tensor_tensor(pooled[:, :, :], pooled[:, :, :], u[:, :, META:TM], ALU.subtract)\
                .then_inc(S["pooled"], 1)
            pool.wait_ge(S["landed"], 48)
            chain(pool.tensor_tensor(cc[:, :, :], cc[:, :, :], cu[:, :, :], ALU.mult))
            pool.wait_ge(S["pooled"], 1)
            tap, shape = u[:, :, 0:T], [P, POOL_GROUPS, T]
            for k in range(3):
                to = tap if k else conv
                chain(pool.tensor_tensor(to, cc[:, :, META - 2 + k:TM - 2 + k],
                                         conv_w[:, k, :].unsqueeze(2).to_broadcast(shape), ALU.mult))
                if k:
                    chain(pool.tensor_tensor(conv, conv, tap, ALU.add))
            pool.tensor_tensor(conv, conv, cb[:, :, :], ALU.mult).then_inc(S["conv_done"], 1)

        @block.tensor
        def _(pe):
            for n in range(N + 3):
                if n < N:
                    t, hd = units[n]
                    if n >= 2:
                        pe.wait_ge(S["masked_done"], n - 1)
                    b0, w0 = 2 * (n % 2), min(seen(t), BANK)
                    lhs = q[:, hd, t * P:(t + 1) * P]
                    last = pe.matmul(bank[:, b0, 0:w0], lhs, cT[:, 0:w0], start=True, stop=True)
                    if seen(t) > BANK:
                        last = pe.matmul(bank[:, b0 + 1, 0:seen(t) - BANK], lhs, cT[:, BANK:seen(t)],
                                         start=True, stop=True)
                    last.then_inc(S["scored"], 1)
                if 2 <= n <= N + 1:
                    e = n - 2
                    t = units[e][0]
                    pe.wait_ge(S["scaled"], e + 1)
                    if e >= 1:
                        pe.wait_ge(S["taken"], e)
                    pe.transpose(bank[0:META, 6, 0:P], p[:, e % 3, 0:META], ident)
                    for kt in range(t + 1):
                        last = pe.transpose(bank[:, 4 + e % 2, kt * P:(kt + 1) * P],
                                            p[:, e % 3, META + kt * P:META + (kt + 1) * P], ident)
                    last.then_inc(S["turned"], 1)
                if n >= 3:
                    e = n - 3
                    t = units[e][0]
                    pe.wait_ge(S["taken"], e + 1)
                    if e >= 1:
                        pe.wait_ge(S["o_lo"], e)
                    o = bank[:, 7, 0:P]
                    pe.matmul(o, cm[:, :], pTm[:, e % 2, :], start=True, stop=False)
                    for kt in range(t + 1):
                        last = pe.matmul(o, c[:, kt, :], pT[:, e % 2, kt * P:(kt + 1) * P], start=False,
                                         stop=kt == t)
                    last.then_inc(S["o_done"], 1)
            pe.wait_ge(S["landed"], 48)
            pe.wait_ge(S["pooled"], 1)
            pe.wait_ge(S["masked_done"], N)
            for g in range(POOL_GROUPS):
                pe.matmul(bank[:, g, :], pool_w[:, g, :], pooled[:, g, :], start=True, stop=True)\
                    .then_inc(S["mixed"], 1)

        @block.scalar
        def _(act):
            for n in range(N + 4):
                if n >= 4:
                    e = n - 4
                    t, hd = units[e]
                    act.wait_ge(S["o_done"], e + 1)
                    act.activation(oh[:, hd, t * P:(t + 1) * P], bank[:, 7, 0:P], ACT.Copy).then_inc(S["o_hi"], 1)
                if 3 <= n <= N + 2:
                    e = n - 3
                    t = units[e][0]
                    act.wait_ge(S["turned"], e + 1)
                    if e >= 2:
                        act.wait_ge(S["o_done"], e - 1)
                    act.activation(pTm[:, e % 2, :], bank[0:META, 6, 0:P], ACT.Copy)
                    act.activation(pT[:, e % 2, 0:(t + 1) * P], bank[:, 4 + e % 2, 0:(t + 1) * P], ACT.Copy)\
                        .then_inc(S["taken"], 1)
                if n < N:
                    t = units[n][0]
                    act.wait_ge(S["maxed"], n + 1)
                    if n >= 3:
                        act.wait_ge(S["turned"], n - 2)
                    act.activation(p[:, n % 3, 0:seen(t)], masked[:, n % 2, 0:seen(t)], ACT.Exp,
                                   bias=mx[:, n % 2:n % 2 + 1], scale=ATTN_SCALE,
                                   accum_out=total[:, n % 3:n % 3 + 1]).then_inc(S["exped"], 1)
            act.wait_ge(S["landed"], 48)
            act.wait_ge(S["conv_done"], 1)
            act.activation(vh[:, :, :], conv, ACT.Copy).then_inc(S["conv_hi"], 1)
            for g in range(POOL_GROUPS):
                act.wait_ge(S["mixed"], g + 1)
                act.activation(ph[:, g, :], bank[:, g, :], ACT.Copy, scale=scale[:, g:g + 1])\
                    .then_inc(S["mixed_hi"], 1)

        @block.vector
        def _(dve):
            chain = Chain(dve, S["vector_steps"])
            for n in range(N + 4):
                if n >= 4:
                    e = n - 4
                    t, hd = units[e]
                    cols = slice(t * P, (t + 1) * P)
                    dve.wait_ge(S["o_hi"], e + 1)
                    dve.tensor_tensor(ol[:, hd, cols], bank[:, 7, 0:P], oh[:, hd, cols].bitcast(F32), ALU.subtract)\
                        .then_inc(S["o_lo"], 1)
                if n < N:
                    t = units[n][0]
                    dve.wait_ge(S["scored"], n + 1)
                    if n >= 2:
                        dve.wait_ge(S["exped"], n - 1)
                    pair = bank[:, 2 * (n % 2):2 * (n % 2) + 2, :].rearrange("p b n -> p (b n)")
                    dve.tensor_tensor_reduce(masked[:, n % 2, 0:seen(t)], pair[:, 0:seen(t)], bias[:, t, 0:seen(t)],
                                             1.0, NEG, ALU.add, ALU.max, mx[:, n % 2:n % 2 + 1])\
                        .then_inc(S["masked_done"], 1)
                    dve.wait_ge(S["masked_done"], n + 1)
                    dve.tensor_scalar(mx[:, n % 2:n % 2 + 1], mx[:, n % 2:n % 2 + 1], -ATTN_SCALE, None,
                                      ALU.mult).then_inc(S["maxed"], 1)
                if n >= 1 and n - 1 < N:
                    e = n - 1
                    t = units[e][0]
                    dve.wait_ge(S["exped"], e + 1)
                    chain(dve.reciprocal(total[:, e % 3:e % 3 + 1], total[:, e % 3:e % 3 + 1]))
                    dve.tensor_scalar(p[:, e % 3, 0:seen(t)], p[:, e % 3, 0:seen(t)], total[:, e % 3:e % 3 + 1],
                                      None, ALU.mult).then_inc(S["scaled"], 1)
            dve.wait_ge(S["landed"], 48)
            dve.wait_ge(S["conv_hi"], 1)
            dve.tensor_tensor(vl[:, :, :], conv, vh[:, :, :].bitcast(F32), ALU.subtract)
            for g in range(POOL_GROUPS):
                dve.wait_ge(S["mixed_hi"], g + 1)
                dve.scalar_tensor_tensor(pl[:, g, :], bank[:, g, :], scale[:, g:g + 1],
                                         ph[:, g, :].bitcast(F32), ALU.mult, ALU.subtract)


def out_2_block(io, life, c0):
    mh, ml = life["m_hi"], life["m_lo"]
    return dict(kind="rows", slab=lambda i, _: weight_slab(io["w_o"], i, c0), width=BANK, ktiles=KD,
                x=lambda kt, m: (mh[:, kt, m * P:(m + 1) * P], ml[:, kt, m * P:(m + 1) * P]), meta=False, c0=c0)


def feed_forward_block(io, life, b):
    return dict(kind="columns", width=BANK, ktiles=KD, meta=False, b=b,
                slab=lambda i, turn: weight_slab(io["w_gate_up"], i, turn * 2 * BANK + b * BANK),
                x=lambda kt, half: (life["fh"][:, kt, :], life["fl"][:, kt, :]))


def phase_branches(nc, bank, io, life):
    with ExitStack() as ctx:
        s = Scope(nc, ctx, "br")
        xh, xl, mh, ml = (life[n] for n in ("xh", "xl", "m_hi", "m_lo"))
        sg, y = s.sb("sg", [P, 4, T]), s.sb("y", [P, 4, T])
        m_sum = s.sb("m_sum", [P, 4, T])
        b_gate = s.sb("b_gate", [P, 3 * KD])
        ring = life["ring"]
        gemm = Gemm(s, ring, bank)
        landed, y_ready, y_used, vec = s.sem("landed"), s.sem("y_ready"), s.sem("y_used"), s.sem("vector_steps")
        G0 = 3496

        def part(w, c0, kt, x, gate):
            return dict(kind="columns", slab=lambda i, turn: weight_slab(w, i, c0 + turn * BANK), width=BANK,
                        ktiles=kt, x=x, meta=False, gate=gate)

        def split(hi, lo):
            return lambda kt, half: (hi[:, kt, :], lo[:, kt, :])

        cols = lambda kt, half: (xh[:, kt, META:TM], xl[:, kt, META:TM])
        plan = []
        for n, (w, kt, hi, lo) in enumerate((("w_a", 4, "pool_hi", "pool_lo"), ("w_b", 8, "attn_hi", "attn_lo"),
                                             ("w_c", 4, "conv_hi", "conv_lo"))):
            gate = part(io["w_in_2"], 0, KD, cols, n)
            gate["slab"] = lambda i, turn, n=n: weight_slab(io["w_in_2"][:, G0 + n * D - BANK:], i,
                                                            (turn + 1) * BANK)
            plan.append(gate)
            plan.append(part(io[w], 0, kt, split(life[hi], life[lo]), None))
        TURNS = D // BANK
        blocks = gemm.plan(plan, TURNS)
        following = gemm.ahead(out_2_block(io, life, 0))
        block = s.block()

        @block.sync
        def _(sp):
            sp.dma_start(b_gate[:, :], io["b_gate"]).then_inc(landed, 16)
            with sp.Fori(0, TURNS) as turn:
                for b in blocks:
                    gemm.on_sync(sp, b, turn)
            gemm.on_sync(sp, following, 0, AHEAD)

        @block.gpsimd
        def _(pool):
            ring.open_raw(pool)
            with pool.Fori(0, TURNS) as turn:
                for b in blocks:
                    gemm.on_gpsimd(pool, b, turn)
            gemm.on_gpsimd(pool, following, 0, AHEAD)

        @block.tensor
        def _(pe):
            ring.open_slots(pe)
            with pe.Fori(0, TURNS) as turn:
                for b in blocks:
                    gemm.on_tensor(pe, b, turn)

        @block.scalar
        def _(act):
            gemm.open_banks(act)
            act.wait_ge(landed, 16)

            def take(n, turn):
                b = blocks[n]
                if b["gate"] is not None:
                    act.wait_ge(y_used, turn * 12 + 4 * b["gate"] + 4)

                def use(j, m, got):
                    f = m[0]
                    if b["gate"] is not None:
                        at = bass.ds(turn * 4 + b["gate"] * KD + f, 1)
                        return act.activation(sg[:, f, :], got, ACT.Sigmoid, bias=b_gate[:, at])
                    return act.activation(y[:, f, :], got, ACT.Copy)

                gemm.take(act, b, use, turn)
                if b["gate"] is None:
                    act.wait_ge(gemm.bank_free, NBANK + b["tile0"] + 4 + turn * b["per"][1])
                    act.sem_inc(y_ready, 4)

            gemm.on_scalar(act, blocks[0], 0, AHEAD)
            with act.Fori(0, TURNS) as turn:
                gemm.on_scalar(act, blocks[0], turn, REST)
                for n in range(len(blocks)):
                    if n + 1 < len(blocks):
                        gemm.on_scalar(act, blocks[n + 1], turn)
                    else:
                        gemm.on_scalar(act, blocks[0], turn + 1, AHEAD)
                    take(n, turn)

        @block.vector
        def _(dve):
            chain = Chain(dve, vec)
            dve.sem_inc(y_used, 4)
            with dve.Fori(0, TURNS) as turn:
                chain.loop(turn, 4)
                for n in range(3):
                    dve.wait_ge(y_ready, turn * 12 + 4 * n + 4)
                    if n == 0:
                        dve.tensor_tensor(m_sum[:, :, :], sg[:, :, :], y[:, :, :], ALU.mult).then_inc(y_used, 4)
                    else:
                        chain(dve.tensor_tensor(y[:, :, :], sg[:, :, :], y[:, :, :], ALU.mult))
                        dve.tensor_tensor(m_sum[:, :, :], m_sum[:, :, :], y[:, :, :], ALU.add).then_inc(y_used, 4)
                dve.wait_ge(y_used, turn * 12 + 16)
                at = bass.ds(turn * 4, 4)
                chain(dve.tensor_copy(mh[:, at, :], m_sum[:, :, :]))
                chain(dve.tensor_tensor(ml[:, at, :], m_sum[:, :, :], mh[:, at, :].bitcast(F32), ALU.subtract))
            chain.end_loop(TURNS)


def phase_out_2(nc, bank, io, life):
    with ExitStack() as ctx:
        s = Scope(nc, ctx, "o2")
        h, xh, xl = (life[n] for n in ("h", "fh", "fl"))
        gain = s.sb("gain", [P, KD])
        const = s.sb("const", [P, CONST_2_W])
        ring = life["ring"]
        gemm = Gemm(s, ring, bank)
        landed, h_done, vec = s.sem("landed"), s.sem("h_done"), s.sem("vector_steps")
        norm = NormColumns(s, h, None, gain, xh, xl, const[:, CONSTS["ident"][0]:CONSTS["ident"][1]], bank)

        blocks = gemm.plan([out_2_block(io, life, 0), out_2_block(io, life, BANK)])
        following = gemm.ahead(feed_forward_block(io, life, 0))
        block = s.block()

        @block.sync
        def _(sp):
            for n, b in enumerate(blocks):
                gemm.on_sync(sp, b, 0, REST if n == 0 else slice(None))
                if n == 0:
                    sp.dma_start(h[:, :, :], io["x2"].rearrange("(t p) d -> p t d", p=P)).then_inc(landed, 16)
                    sp.dma_start(const[:, :], io["const"][:, 0:CONST_2_W]).then_inc(landed, 16)
                    sp.dma_start(gain[:, :], io["norm2_g"]).then_inc(landed, 16)
            gemm.on_sync(sp, following, 0, AHEAD)

        @block.gpsimd
        def _(pool):
            gemm.on_gpsimd(pool, blocks[0], 0, REST)
            gemm.on_gpsimd(pool, blocks[1])
            gemm.on_gpsimd(pool, following, 0, AHEAD)

        @block.scalar
        def _(act):
            gemm.on_scalar(act, blocks[0], 0, REST)
            gemm.on_scalar(act, blocks[1])
            gemm.on_scalar(act, following, 0, AHEAD)
            act.wait_ge(landed, 48)
            norm.on_scalar(act, lambda e, t: e.wait_ge(h_done, 1))

        @block.tensor
        def _(pe):
            for b in blocks:
                gemm.on_tensor(pe, b)
            pe.wait_ge(landed, 48)
            pe.wait_ge(gemm.bank_free, NBANK + gemm.tile0)
            norm.on_tensor(pe)

        @block.vector
        def _(dve):
            chain = Chain(dve, vec)
            gemm.open_banks(dve)
            dve.wait_ge(landed, 48)
            for b in blocks:
                gemm.take(dve, b, lambda j, m, got: dve.tensor_tensor(
                    h[:, m, b["c0"]:b["c0"] + BANK], got, h[:, m, b["c0"]:b["c0"] + BANK], ALU.add))
            dve.wait_ge(gemm.bank_free, NBANK + gemm.tile0)
            dve.sem_inc(h_done, 1)
            norm.on_vector(dve, chain)


def phase_feed_forward(nc, bank, io, life):
    with ExitStack() as ctx:
        s = Scope(nc, ctx, "ff")
        h = life["h"]
        ah, al = s.sb("ah", [P, KF, T], F32R), s.sb("al", [P, KF, T], F32R)
        sg, up = s.sb("sg", [P, 2, T]), s.sb("up", [P, 2, T])
        stats_row = s.sb("gain_row", [P, D])
        ring = life["ring"]
        gemm = Gemm(s, ring, bank)
        down = Gemm(s, ring, bank, "down_")
        landed, ready, used, vec = s.sem("landed"), s.sem("pair_ready"), s.sem("pair_used"), s.sem("vector_steps")
        h_done, out_done, stored = s.sem("h_done"), s.sem("out_done"), s.sem("stored")
        stats = RowStats(s, h, None, "s_")

        NB = KF // 2
        TURNS = NB // 2
        pair_blocks = gemm.plan([feed_forward_block(io, life, b) for b in range(2)], TURNS)
        tail = gemm.plan([feed_forward_block(io, life, 2 * TURNS)])[0]
        down.slab0 = gemm.slab0

        def down_part(c0):
            return dict(kind="rows", slab=lambda i, _: weight_slab(io["w_down"], i, c0), width=BANK, ktiles=KF,
                        x=lambda kt, m: (ah[:, kt, m * P:(m + 1) * P], al[:, kt, m * P:(m + 1) * P]),
                        meta=False, c0=c0)

        downs = down.plan([down_part(0), down_part(BANK)])
        block = s.block()

        @block.sync
        def _(sp):
            with sp.Fori(0, TURNS) as turn:
                gemm.on_sync(sp, pair_blocks[0], turn, REST)
                gemm.on_sync(sp, pair_blocks[1], turn)
                gemm.on_sync(sp, pair_blocks[0], turn + 1, AHEAD)
            gemm.on_sync(sp, tail, 0, REST)
            sp.dma_start(stats_row[:, :], io["final_g"].to_broadcast([P, D])).then_inc(landed, 16)
            for b in downs:
                down.on_sync(sp, b)
            for t in range(NT):
                sp.wait_ge(out_done, t + 1)
                sp.dma_start(io["out"][t * P:(t + 1) * P, :], h[:, t, :]).then_inc(stored, 16)
            sp.wait_ge(stored, 16 * NT)

        @block.gpsimd
        def _(pool):
            with pool.Fori(0, TURNS) as turn:
                gemm.on_gpsimd(pool, pair_blocks[0], turn, REST)
                gemm.on_gpsimd(pool, pair_blocks[1], turn)
                gemm.on_gpsimd(pool, pair_blocks[0], turn + 1, AHEAD)
            gemm.on_gpsimd(pool, tail, 0, REST)
            for b in downs:
                down.on_gpsimd(pool, b)

        @block.tensor
        def _(pe):
            with pe.Fori(0, TURNS) as turn:
                for b in pair_blocks:
                    gemm.on_tensor(pe, b, turn)
            gemm.on_tensor(pe, tail)
            pe.wait_ge(gemm.bank_free, NBANK + gemm.tile0)
            pe.wait_ge(used, 2 * NB + 2)
            for b in downs:
                down.on_tensor(pe, b)

        @block.scalar
        def _(act):
            gemm.open_banks(act)

            def take(b, turn=0):
                first = 2 * b["b"] if b is not tail else 4 * TURNS

                def use(j, m, got):
                    f = m[0]
                    if f < 2:
                        act.wait_ge(used, first + f + 1 + turn * 4)
                        return act.activation(sg[:, f, :], got, ACT.Silu)
                    return act.activation(up[:, f - 2, :], got, ACT.Copy)

                gemm.take(act, b, use, turn)
                act.wait_ge(gemm.bank_free, NBANK + b["tile0"] + 4 + turn * b["per"][1])
                act.sem_inc(ready, 2)

            with act.Fori(0, TURNS) as turn:
                for n, b in enumerate(pair_blocks):
                    gemm.on_scalar(act, b, turn, REST)
                    gemm.on_scalar(act, pair_blocks[1 - n], turn + n, AHEAD)
                    take(b, turn)
            gemm.on_scalar(act, tail, 0, REST)
            down.on_scalar(act, downs[0], 0, AHEAD)
            take(tail)
            down.on_scalar(act, downs[0], 0, REST)
            down.on_scalar(act, downs[1])
            stats.on_scalar(act, lambda e, t: e.wait_ge(h_done, 1))

        @block.vector
        def _(dve):
            chain = Chain(dve, vec)
            dve.sem_inc(used, 2)
            down.open_banks(dve)

            def hidden(b, turn=0):
                first = 2 * b["b"] if b is not tail else 4 * TURNS
                dve.wait_ge(ready, first + 2 + turn * 4)
                at = bass.ds(turn * 4 + first, 2)
                chain(dve.tensor_tensor(up[:, :, :], up[:, :, :], sg[:, :, :], ALU.mult))
                chain(dve.tensor_copy(ah[:, at, :], up[:, :, :]))
                dve.tensor_tensor(al[:, at, :], up[:, :, :], ah[:, at, :].bitcast(F32), ALU.subtract)\
                    .then_inc(used, 2)

            with dve.Fori(0, TURNS) as turn:
                chain.loop(turn, 4)
                for b in pair_blocks:
                    hidden(b, turn)
            chain.end_loop(TURNS)
            hidden(tail)
            dve.wait_ge(landed, 16)
            for b in downs:
                down.take(dve, b, lambda j, m, got: dve.tensor_tensor(
                    h[:, m, b["c0"]:b["c0"] + BANK], got, h[:, m, b["c0"]:b["c0"] + BANK], ALU.add))
            dve.wait_ge(down.bank_free, NBANK + down.tile0)
            dve.sem_inc(h_done, 1)
            stats.on_vector(dve, chain, lambda t: dve.scalar_tensor_tensor(
                h[:, t, :], h[:, t, :], stats.rstd[:, t:t + 1], stats_row[:, :], ALU.mult, ALU.mult)
                .then_inc(out_done, 1))



def program(nc, io):
    SEMAPHORES.clear()
    with ExitStack() as whole:
        bank = whole.enter_context(nc.psum_tensor("bank", [P, NBANK, BANK], F32))
        block_1(nc, bank, io)
        clear_semaphores(nc)
        block_2(nc, bank, io)


def block_1(nc, bank, io):
    picks_end, gate_end, mix_end, const_end, parts_end, rows_end = (ExitStack() for _ in range(6))
    s = Scope(nc, picks_end, "b1")
    life = {"pick_keys": s.sb("pick_keys", [P, 2, T], BF16, side="right"),
            "pick_gates": s.sb("pick_gates", [P, T, 3], BF16, side="right")}
    const = Scope(nc, const_end, "b1c").sb("const", [P, CONST_W])
    s = Scope(nc, parts_end, "b1p")
    for n in ("q", "k", "v", "gv"):
        life[n] = s.sb(n, [P, NT, BANK])
    life["gr"] = Scope(nc, gate_end, "b1g").sb("gr", [P, NT, BANK], side="right")
    for n in ("k_m", "v_m", "gv_m"):
        life[n] = s.sb(n, [META, BANK])
    life["gqk"], life["zT"] = s.sb("gqk", [P, 4, TM]), s.sb("zT", [P, 1, TM])
    phase_project_1(nc, bank, const, io, life)
    life["mix"] = Scope(nc, mix_end, "b1m").sb("mix", [P, NT, D], side="right")
    phase_diff_attention(nc, bank, const, io, life)
    phase_linear_attention(nc, bank, const, io, life)
    parts_end.close()
    s = Scope(nc, rows_end, "b1r")
    life["h"] = s.sb("h", [P, NT, D])
    phase_mix_out(nc, bank, const, io, life)
    mix_end.close()
    gate_end.close()
    phase_peer_pick(nc, bank, const, io, life)
    rows_end.close()
    const_end.close()
    phase_peer_experts(nc, bank, io, life)
    picks_end.close()


def block_2(nc, bank, io):
    life = {}
    left, right = ExitStack(), ExitStack()
    s = Scope(nc, left, "b2")
    for n in ("xh", "xl"):
        life[n] = s.sb(n, [P, KD, TM], F32R)
    r = Scope(nc, right, "b2r")
    const = r.sb("const", [P, CONST_2_W], side="right")
    for n, shape in (("bias", [P, NT, TM]), ("c", [P, NT, LAT]), ("c_m", [META, LAT]), ("cT", [P, TM]),
                     ("u", [P, 4, TM]), ("cc", [P, 4, TM]), ("cu", [P, 4, TM]), ("xs", [P, NT + 1, D]),
                     ("h_rows", [P, NT, D])):
        life[n] = r.sb(n, shape, side="right")
    life["q2"] = life["xs"][:, 0:NT, :].rearrange("p t (two n) -> p (t two) n", two=2)
    life["cb"] = life["h_rows"][:, 0:NT // 2, :].rearrange("p t (two n) -> p (t two) n", two=2)
    phase_project_2(nc, bank, const, io, life)
    for n in ("attn_hi", "attn_lo"):
        life[n] = s.sb(n, [P, AH, T], F32R)
    for n in ("pool_hi", "pool_lo", "conv_hi", "conv_lo"):
        life[n] = s.sb(n, [P, POOL_GROUPS, T], F32R)
    phase_sparse_attention(nc, bank, const, io, life)
    right.close()
    right, ring_end = ExitStack(), ExitStack()
    life["ring"] = WeightRing(Scope(nc, ring_end, "b2w"), side="right")
    r = Scope(nc, right, "b2m")
    for n in ("m_hi", "m_lo"):
        life[n] = r.sb(n, [P, KD, T], F32R, side="right")
    phase_branches(nc, bank, io, life)
    left.close()
    left = ExitStack()
    s = Scope(nc, left, "b2f")
    life["h"] = s.sb("h", [P, NT, D])
    for n in ("fh", "fl"):
        life[n] = s.sb(n, [P, KD, T], F32R)
    phase_out_2(nc, bank, io, life)
    right.close()
    phase_feed_forward(nc, bank, io, life)
    left.close()
    ring_end.close()



def layouts(i):
    def rows(a):
        return a[0]

    def per_partition(a):
        return a[0].reshape(-1, P).T

    w2 = i["w_in_2"][0]
    at = np.cumsum([0, POOL_D, AH * LAT, LAT, IDX_H * IDX_D, IDX_D, IDX_H])
    q_idx, k_idx, w_idx = (w2[:, at[n]:at[n + 1]] for n in (3, 4, 5))
    gate_up = i["w_gate_up_2"][0].reshape(D, 2, FF // (BANK // 2), BANK // 2)
    return {
        "const": const_table(),
        "x": i["x"][0], "meta_tokens": i["meta_tokens"], "ln1_w": per_partition(i["ln1_w"]),
        "w_in": rows(i["w_in"]),
        "da_lambda_q1": i["da_lambda_q1"], "da_lambda_k1": i["da_lambda_k1"],
        "da_lambda_q2": i["da_lambda_q2"], "da_lambda_k2": i["da_lambda_k2"], "da_subln_w": i["da_subln_w"],
        "gla_gate_w2_f": rows(i["gla_gate_w2_f"]), "gla_gate_b_f": i["gla_gate_b_f"],
        "gla_gate_w2_b": rows(i["gla_gate_w2_b"]), "gla_gate_b_b": i["gla_gate_b_b"],
        "gla_norm_w": i["gla_norm_w"], "w_out": rows(i["w_out"]), "ln2_w": per_partition(i["ln2_w"]),
        "peer_w_q": rows(i["peer_w_q"]),
        "peer_keys": i["peer_sub_keys"].reshape(HP, PEER_KEYS, -1).transpose(2, 0, 1),
        "peer_u": i["peer_u"].reshape(PEER_KEYS, PEER_KEYS, KD, P).transpose(0, 3, 2, 1).reshape(PEER_KEYS, P, D),
        "peer_v": i["peer_v"].reshape(PEER_KEYS, PEER_KEYS, D),
        "final_norm_w": i["final_norm_w"][None],
        "meta_2": i["meta_2"], "norm1_g": per_partition(i["norm1_g_2"]), "w_in_2": w2,
        "w_index": np.concatenate([q_idx] + [k_idx] * 4, 1),
        "w_latent": np.concatenate([w2[:, at[2]:at[3]], w_idx], 1),
        "b_gate": per_partition(i["b_gate_2"]),
        "pool_w": i["pool_w_2"][0].transpose(1, 0, 2), "pool_scale": per_partition(i["pool_scale_2"]),
        "w_a": rows(i["w_a_2"]), "kv_norm_g": i["kv_norm_g_2"], "w_b": rows(i["w_b_2"]),
        "conv_w": i["conv_w_2"][0].reshape(3, POOL_GROUPS, P).transpose(2, 0, 1),
        "w_c": rows(i["w_c_2"]), "w_o": rows(i["w_o_2"]), "norm2_g": per_partition(i["norm2_g_2"]),
        "w_gate_up": gate_up.transpose(0, 2, 1, 3).reshape(D, 2 * FF),
        "w_down": rows(i["w_down_2"]), "final_g": i["final_g_2"][None],
    }


SCRATCH = {"h1": (T, D), "experts": (T, D), "x2": (T, D), "hn_hi": (P, KD, T), "hn_lo": (P, KD, T)}


def kernel(**inputs):
    import concourse.bacc as bacc
    from concourse.bass_utils import run_bass_kernel_spmd

    nc = bacc.Bacc("TRN2", target_bir_lowering=False, num_devices=1)
    arrays, io = {}, {}
    for name, a in layouts({n: np.asarray(a) for n, a in inputs.items()}).items():
        a = np.ascontiguousarray(a)
        arrays[f"in_{name}"] = a
        io[name] = nc.dram_tensor(f"in_{name}", a.shape, mybir.dt.from_np(a.dtype), kind="ExternalInput").ap()
    for name, shape in SCRATCH.items():
        io[name] = nc.dram_tensor(f"scratch_{name}", shape, F32, kind="Internal").ap()
    io["out"] = nc.dram_tensor("out", (T, D), F32, kind="ExternalOutput").ap()
    program(nc, io)
    got = run_bass_kernel_spmd(nc, [arrays], core_ids=[0])
    return got.results[0]["out"].reshape(1, T, D)
```
